# Optimizing a Trainium2 kernel written in Bass

```python
import math
import jax
import jax.numpy as jnp
from jax import lax
import numpy as np

D_MODEL = 1024
BATCH = 1
SEQ = 512
DEPTH = 1

CHUNK = 64
ROPE_THETA = 10000.0
NORM_EPS = 1e-6
HEAD_DIM = 64
DA_HEADS = 4
DA_V_DIM = 2 * HEAD_DIM
Q_BLOCK = 128
SW_Q_HEADS = 8
SW_KV_HEADS = 2
WINDOW = 128
WINDOW_CHUNKS = WINDOW // CHUNK
DA_Q = DA_HEADS * 2 * HEAD_DIM
DA_K = DA_HEADS * 2 * HEAD_DIM
DA_V = DA_HEADS * DA_V_DIM
SW_Q = SW_Q_HEADS * HEAD_DIM
SW_K = SW_KV_HEADS * HEAD_DIM
SW_V = SW_KV_HEADS * HEAD_DIM
IN_WIDTH = DA_Q + DA_K + DA_V + SW_Q + SW_K + SW_V
DA_WIDTH = DA_V
SW_WIDTH = SW_Q
N_BRANCHES = 2
N_EXPERTS = 64
TOP_K = 8
N_GROUPS = 8
TOPK_GROUPS = 4
EXPERT_FF = 256
SHARED_FF = 256
ROUTED_SCALE = 2.5
MOE_BLOCK = 128
ADA_PARTS = 6

kernel_name = "hybrid_diffattn_swa_sink_moe_adaln"

def rms_norm(x, g):
    xf = x.astype(jnp.float32)
    y = xf * lax.rsqrt(jnp.mean(xf * xf, axis=-1, keepdims=True) + NORM_EPS)
    return (y * g.astype(jnp.float32)).astype(x.dtype)

def modulate(h, shift, scale):
    return h * (1 + scale[:, None, :]) + shift[:, None, :]

def rope_tables(positions):
    inv_freq = 1.0 / (ROPE_THETA ** (jnp.arange(0, HEAD_DIM, 2, dtype=jnp.float32) / HEAD_DIM))
    ang = positions.astype(jnp.float32)[..., None] * inv_freq
    return jnp.cos(ang), jnp.sin(ang)

def apply_rope(t, cos, sin):
    c = cos[:, :, None, :].astype(t.dtype)
    s = sin[:, :, None, :].astype(t.dtype)
    t1, t2 = jnp.split(t, 2, axis=-1)
    return jnp.concatenate([t1 * c - t2 * s, t2 * c + t1 * s], axis=-1)

def diff_attention(q, k, v, lam, norm_g, lambda_init):
    B, S, H, _, d = q.shape
    nb = S // Q_BLOCK
    scale = d ** -0.5
    lam_f = lam.astype(jnp.float32)
    lmbda = jnp.exp(jnp.sum(lam_f[0] * lam_f[1])) - jnp.exp(jnp.sum(lam_f[2] * lam_f[3])) + lambda_init
    key_chunk = jnp.arange(S) // CHUNK
    qb = q.reshape(B, nb, Q_BLOCK, H, 2, d).transpose(1, 0, 2, 3, 4, 5)

    def block(args):
        qi, i = args
        s = jnp.einsum('bqhmd,bkhmd->bhmqk', qi, k).astype(jnp.float32) * scale
        q_chunk = (i * Q_BLOCK + jnp.arange(Q_BLOCK)) // CHUNK
        mask = key_chunk[None, :] <= q_chunk[:, None]
        p = jax.nn.softmax(jnp.where(mask, s, -jnp.inf), axis=-1)
        p = p[:, :, 0] - lmbda * p[:, :, 1]
        return jnp.einsum('bhqk,bkhe->bqhe', p.astype(v.dtype), v)

    o = lax.map(block, (qb, jnp.arange(nb)))
    o = o.transpose(1, 0, 2, 3, 4).reshape(B, S, H, 2 * d)
    o = rms_norm(o, norm_g) * (1 - lambda_init)
    return o.reshape(B, S, H * 2 * d)

def sliding_window_attention(q, k, v, sinks):
    B, S, Hq, d = q.shape
    Hkv = k.shape[2]
    R = Hq // Hkv
    nc = S // CHUNK
    qc = q.reshape(B, nc, CHUNK, Hkv, R, d)

    def band(t):
        tc = t.reshape(B, nc, CHUNK, Hkv, d)
        padded = jnp.pad(tc, ((0, 0), (WINDOW_CHUNKS - 1, 0), (0, 0), (0, 0), (0, 0)))
        return jnp.concatenate([padded[:, j:j + nc] for j in range(WINDOW_CHUNKS)], axis=2)

    kb, vb = band(k), band(v)
    s = jnp.einsum('bcqgrd,bckgd->bcgrqk', qc, kb).astype(jnp.float32) * d ** -0.5
    key_chunk = jnp.arange(nc)[:, None] - (WINDOW_CHUNKS - 1) + jnp.arange(WINDOW)[None, :] // CHUNK
    valid = key_chunk >= 0
    s = jnp.where(valid[None, :, None, None, None, :], s, -jnp.inf)
    sink = sinks.astype(jnp.float32).reshape(Hkv, R)[None, None, :, :, None, None]
    m = jnp.maximum(jnp.max(s, axis=-1, keepdims=True), sink)
    e = jnp.exp(s - m)
    p = e / (jnp.sum(e, axis=-1, keepdims=True) + jnp.exp(sink - m))
    o = jnp.einsum('bcgrqk,bckgd->bcqgrd', p.astype(v.dtype), vb)
    return o.reshape(B, S, Hq * d)

def token_mixer(h, cos, sin, w_in, b_in, da_lambda, da_norm_g, lambda_init, sw_sinks,
                w_branch_a, w_branch_b, w_gate, b_gate, w_out):
    B, S, _ = h.shape
    proj = h @ w_in + b_in
    o1 = DA_Q
    o2 = o1 + DA_K
    o3 = o2 + DA_V
    o4 = o3 + SW_Q
    o5 = o4 + SW_K
    qa = apply_rope(proj[..., :o1].reshape(B, S, 2 * DA_HEADS, HEAD_DIM), cos, sin)
    ka = apply_rope(proj[..., o1:o2].reshape(B, S, 2 * DA_HEADS, HEAD_DIM), cos, sin)
    va = proj[..., o2:o3].reshape(B, S, DA_HEADS, DA_V_DIM)
    qs = apply_rope(proj[..., o3:o4].reshape(B, S, SW_Q_HEADS, HEAD_DIM), cos, sin)
    ks = apply_rope(proj[..., o4:o5].reshape(B, S, SW_KV_HEADS, HEAD_DIM), cos, sin)
    vs = proj[..., o5:].reshape(B, S, SW_KV_HEADS, HEAD_DIM)

    ya = diff_attention(qa.reshape(B, S, DA_HEADS, 2, HEAD_DIM), ka.reshape(B, S, DA_HEADS, 2, HEAD_DIM),
                        va, da_lambda, da_norm_g, lambda_init)
    yb = sliding_window_attention(qs, ks, vs, sw_sinks)

    gates = jax.nn.sigmoid(h @ w_gate + b_gate).reshape(B, S, N_BRANCHES, D_MODEL)
    merged = gates[:, :, 0] * (ya @ w_branch_a) + gates[:, :, 1] * (yb @ w_branch_b)
    return merged @ w_out

def route(h, w_router, router_bias):
    N = h.shape[0]
    scores = jax.nn.sigmoid((h @ w_router).astype(jnp.float32))
    choice = scores + router_bias.astype(jnp.float32)
    grp = choice.reshape(N, N_GROUPS, N_EXPERTS // N_GROUPS)
    grp_score = jnp.sum(lax.top_k(grp, 2)[0], axis=-1)
    _, gidx = lax.top_k(grp_score, TOPK_GROUPS)
    gmask = jnp.sum(jax.nn.one_hot(gidx, N_GROUPS, dtype=jnp.float32), axis=1) > 0
    emask = jnp.repeat(gmask, N_EXPERTS // N_GROUPS, axis=1)
    _, idx = lax.top_k(jnp.where(emask, choice, -jnp.inf), TOP_K)
    w = jnp.take_along_axis(scores, idx, axis=1)
    w = w / jnp.sum(w, axis=-1, keepdims=True) * ROUTED_SCALE
    return idx, w

def routed_experts(h, idx, wts, w_exp_gate, w_exp_up, w_exp_down):
    N, D = h.shape
    A = N * TOP_K
    flat_e = idx.reshape(A)
    flat_tok = jnp.repeat(jnp.arange(N, dtype=jnp.int32), TOP_K)
    flat_w = wts.reshape(A)
    order = jnp.argsort(flat_e)
    sorted_e = flat_e[order]
    counts = jnp.bincount(flat_e, length=N_EXPERTS)
    padded = (counts + MOE_BLOCK - 1) // MOE_BLOCK * MOE_BLOCK
    start = jnp.cumsum(counts) - counts
    pend = jnp.cumsum(padded)
    pstart = pend - padded
    row = pstart[sorted_e] + (jnp.arange(A) - start[sorted_e])
    n_blocks = -(-A // MOE_BLOCK) + N_EXPERTS
    P = n_blocks * MOE_BLOCK
    row_tok = jnp.zeros((P,), jnp.int32).at[row].set(flat_tok[order])
    row_w = jnp.zeros((P,), h.dtype).at[row].set(flat_w[order].astype(h.dtype))
    block_e = jnp.minimum(jnp.searchsorted(pend, jnp.arange(n_blocks) * MOE_BLOCK, side='right'),
                          N_EXPERTS - 1)

    def block(args):
        tok, e = args
        xb = h[tok]
        return (jax.nn.silu(xb @ w_exp_gate[e]) * (xb @ w_exp_up[e])) @ w_exp_down[e]

    out = lax.map(block, (row_tok.reshape(n_blocks, MOE_BLOCK), block_e))
    out = out.reshape(P, D) * row_w[:, None]
    return jax.ops.segment_sum(out, row_tok, num_segments=N)

def channel_mixer(h, w_router, router_bias, w_exp_gate, w_exp_up, w_exp_down,
                  w_sh_gate, w_sh_up, w_sh_down):
    B, S, D = h.shape
    hf = h.reshape(B * S, D)
    idx, wts = route(hf, w_router, router_bias)
    routed = routed_experts(hf, idx, wts, w_exp_gate, w_exp_up, w_exp_down)
    shared = (jax.nn.silu(hf @ w_sh_gate) * (hf @ w_sh_up)) @ w_sh_down
    return (routed + shared).reshape(B, S, D)

def setup_inputs(seed: int = 0) -> dict:
    key = jax.random.key(seed)
    ks = jax.random.split(key, 32)
    f32 = jnp.float32

    def nrm(k, shape, scale):
        return jax.random.normal(k, shape, f32) * scale

    L, D = DEPTH, D_MODEL
    offsets = jax.random.randint(ks[2], (BATCH, 1), 0, 8192, dtype=jnp.int32)
    return {
        'x': nrm(ks[0], (BATCH, SEQ, D), 1.0),
        'c': nrm(ks[1], (BATCH, D), 1.0),
        'positions': offsets + jnp.arange(SEQ, dtype=jnp.int32)[None, :],
        'norm1_g': 1.0 + nrm(ks[3], (L, D), 0.1),
        'norm2_g': 1.0 + nrm(ks[4], (L, D), 0.1),
        'w_ada': nrm(ks[5], (L, D, ADA_PARTS * D), 0.5 * D ** -0.5),
        'b_ada': nrm(ks[6], (L, ADA_PARTS * D), 0.02),
        'w_in': nrm(ks[7], (L, D, IN_WIDTH), D ** -0.5),
        'b_in': nrm(ks[8], (L, IN_WIDTH), 0.02),
        'da_lambda': nrm(ks[9], (L, 4, HEAD_DIM), 0.1),
        'da_norm_g': 1.0 + nrm(ks[10], (L, DA_V_DIM), 0.1),
        'sw_sinks': nrm(ks[11], (L, SW_Q_HEADS), 1.0),
        'w_branch_a': nrm(ks[12], (L, DA_WIDTH, D), DA_WIDTH ** -0.5),
        'w_branch_b': nrm(ks[13], (L, SW_WIDTH, D), SW_WIDTH ** -0.5),
        'w_gate': nrm(ks[14], (L, D, N_BRANCHES * D), D ** -0.5),
        'b_gate': nrm(ks[15], (L, N_BRANCHES * D), 0.02),
        'w_out': nrm(ks[16], (L, D, D), D ** -0.5),
        'w_router': nrm(ks[17], (L, D, N_EXPERTS), D ** -0.5),
        'router_bias': nrm(ks[18], (L, N_EXPERTS), 0.01),
        'w_exp_gate': nrm(ks[19], (L, N_EXPERTS, D, EXPERT_FF), D ** -0.5),
        'w_exp_up': nrm(ks[20], (L, N_EXPERTS, D, EXPERT_FF), D ** -0.5),
        'w_exp_down': nrm(ks[21], (L, N_EXPERTS, EXPERT_FF, D), EXPERT_FF ** -0.5),
        'w_sh_gate': nrm(ks[22], (L, D, SHARED_FF), D ** -0.5),
        'w_sh_up': nrm(ks[23], (L, D, SHARED_FF), D ** -0.5),
        'w_sh_down': nrm(ks[24], (L, SHARED_FF, D), SHARED_FF ** -0.5),
        'final_norm_g': 1.0 + nrm(ks[25], (D,), 0.1),
    }

def reference(x, c, positions, norm1_g, norm2_g, w_ada, b_ada, w_in, b_in, da_lambda, da_norm_g,
              sw_sinks, w_branch_a, w_branch_b, w_gate, b_gate, w_out, w_router, router_bias,
              w_exp_gate, w_exp_up, w_exp_down, w_sh_gate, w_sh_up, w_sh_down, final_norm_g):
    cos, sin = rope_tables(positions)
    c_act = jax.nn.silu(c)
    for layer in range(DEPTH):
        lambda_init = 0.8 - 0.6 * math.exp(-0.3 * layer)
        mod = c_act @ w_ada[layer] + b_ada[layer]
        sh1, sc1, g1, sh2, sc2, g2 = jnp.split(mod, ADA_PARTS, axis=-1)

        h = modulate(rms_norm(x, norm1_g[layer]), sh1, sc1)
        mix = token_mixer(h, cos, sin, w_in[layer], b_in[layer], da_lambda[layer], da_norm_g[layer],
                          lambda_init, sw_sinks[layer], w_branch_a[layer], w_branch_b[layer],
                          w_gate[layer], b_gate[layer], w_out[layer])
        x = x + g1[:, None, :] * mix

        h = modulate(rms_norm(x, norm2_g[layer]), sh2, sc2)
        ffn = channel_mixer(h, w_router[layer], router_bias[layer], w_exp_gate[layer], w_exp_up[layer],
                            w_exp_down[layer], w_sh_gate[layer], w_sh_up[layer], w_sh_down[layer])
        x = x + g2[:, None, :] * ffn
    return rms_norm(x, final_norm_g)


_drawn_inputs = setup_inputs


def setup_inputs(seed=0):
    import zlib

    import numpy as np

    out = dict(_drawn_inputs(seed))
    spreads = {}
    factors = {'b_in': 2.745, 'da_lambda': 5.59, 'sw_sinks': 8.0, 'b_gate': 23.271}
    for name, (base, spread) in spreads.items():
        noise = np.random.default_rng([zlib.crc32(name.encode()), seed]).standard_normal(out[name].shape)
        drawn = base * np.exp(spread * noise) if base else spread * noise
        out[name] = jnp.asarray(drawn.astype(out[name].dtype))
    for name, factor in factors.items():
        out[name] = (out[name] * factor).astype(out[name].dtype)
    return out
```

```python
import math
from contextlib import ExitStack

import concourse.bass as bass
from concourse import mybir

ALU = mybir.AluOpType
ACT = mybir.ActivationFunctionType
F32 = mybir.dt.float32
I32 = mybir.dt.int32
AX_X = mybir.AxisListType.X

P = 128
D = 1024
S = 512
KD = D // P
TT = S // P
HD = 64
CHUNK = 64
DA_HEADS = 4
SW_HEADS = 8
SW_KV = 2
N_EXP = 64
N_GRP = 8
TOP_K = 8
TOP_G = 4
FF = 256
KF = FF // P
SLOTS = 128
MAX_OVER = 31
ROUTED_SCALE = 2.5
EPS = 1e-6
LAMBDA_INIT = 0.8 - 0.6 * math.exp(-0.3 * 0)
SCALE = HD ** -0.5
MASKED = -1e30
SKIP = 1e6

TWO_PI_A = 6.28125
TWO_PI_B = round((2 * math.pi - TWO_PI_A) * 2 ** 20) / 2 ** 20
TWO_PI_C = 2 * math.pi - TWO_PI_A - TWO_PI_B
ROUND = 1.5 * 2 ** 23
PI_IN = 3.1415925

ROW_C, ROW_ADA, ROW_N1, ROW_N2, ROW_BIN, ROW_BG, ROW_DAG, ROWS = 0, 8, 56, 64, 72, 90, 106, 107

RING = 6
UNIT = 2048
UNROLL = 4


def weight_units():
    units = [("ada", u) for u in range(8)] + [("in", u) for u in range(9)]
    for j in range(8):
        units += [("gate", j), ("ada", 8 + 2 * j), ("ada", 9 + 2 * j)]
    units += [("branch_a", 0), ("branch_b", 0), ("branch_a", 1), ("branch_b", 1)]
    units += [("out", u) for u in range(4)]
    units += [("sh_gate", 0), ("sh_up", 0), ("sh_down", 0)]
    return units


def attention_units():
    return ([("da", h, i) for h in range(DA_HEADS) for i in range(TT)]
            + [("sw", g, i) for g in range(SW_KV) for i in range(TT)])


def fillers():
    out = []
    for j in range(8):
        out += [("gate", 2 * j), ("gate", 2 * j + 1), ("ada", 8 + 2 * j), ("ada", 9 + 2 * j)]
    return out


def psum_tiles():
    tiles = [("ada", u, "D") for u in range(8)]
    tiles += [("qk", j, "A") for j in range(8)]
    tiles += [("v", j, "D") for j in range(4)]
    tiles += [("qk", j, "A") for j in range(8, 13)]
    tiles += [("v", 4, "D")]
    tiles += [(k, u, "A" if k == "gate" else "D") for k, u in fillers()]
    tiles += [("branch", j, "D") for j in range(16)]
    tiles += [("out", j, "D") for j in range(2 * TT)]
    tiles += [("router", 0, "A"), ("sh_gate", 0, "A"), ("sh_up", 0, "D"), ("rank", 0, "D"),
              ("sh_gate", 1, "A"), ("sh_up", 1, "D")]
    tiles += [("sh_down", j, "A") for j in range(2 * TT)]
    return tiles


def build(nc, x_d, c_d, pos_d, n1_d, n2_d, w_ada_d, b_ada_d, w_in_d, b_in_d, lam_d, dag_d, sinks_d,
          w_ba_d, w_bb_d, w_gate_d, b_gate_d, w_out_d, w_router_d, r_bias_d, w_eg_d, w_eu_d, w_ed_d,
          w_sg_d, w_su_d, w_sd_d, fng_d, inv_freq_d, out_d):
    units = weight_units()
    unit_no = {u: n for n, u in enumerate(units)}
    tiles = psum_tiles()
    tile_no = {(k, i): n for n, (k, i, _) in enumerate(tiles)}
    att = attention_units()
    fill = fillers()
    NU = len(att)

    def fill_of(u):
        return fill[len(fill) * u // NU:len(fill) * (u + 1) // NU]

    t_steps = []
    n_steps = 0
    for kind, _, _ in att:
        t_steps.append(n_steps)
        n_steps += 1 if kind == "da" else 2

    xn2_d = nc.dram_tensor("xn2_scratch", (S, D), F32, kind="Internal").ap()
    y_d = nc.dram_tensor("expert_rows", (S * TOP_K, D), F32, kind="Internal").ap()
    g_d = nc.dram_tensor("gate_rows", (2, D), F32, kind="Internal").ap()

    with ExitStack() as ctx:
        def sb(name, cols, dt=F32):
            return ctx.enter_context(nc.sbuf_tensor(name, [P, cols], dt))

        def sem(name):
            return ctx.enter_context(nc.semaphore(name))

        wring = sb("wring", 12 * UNIT)
        x_sb = sb("x_sb", TT * D)[:, :].rearrange("p (t d) -> p t d", t=TT)
        hT = sb("hT", KD * S)[:, :].rearrange("p (k s) -> p k s", k=KD)
        G = sb("G", 16 * S)
        O = sb("O", 8 * S)
        xg = sb("xg", 2 * D)[:, :].rearrange("p (b d) -> p b d", b=2)
        gate_b = sb("gate_b", D)
        fng = sb("fng", D)
        bias_v = sb("bias_v", 640)
        wr = sb("wr", KD * N_EXP)[:, :].rearrange("p (k e) -> p k e", k=KD)
        hact = sb("hact", 2 * KF * SLOTS)[:, :].rearrange("p (b k s) -> p b k s", b=2, k=KF)
        ident = sb("ident", P)
        rows = sb("rows", P)
        cols = sb("cols", ROWS)
        mod = sb("mod", 48)
        small = sb("small", 160)

        def slot(s):
            return wring[:, s * UNIT:(s + 1) * UNIT]

        late = wring[:, RING * UNIT:12 * UNIT]
        qk = late[:, 0:13 * S].rearrange("p (j s) -> p j s", j=13)
        yT = late[:, 0:8 * S].rearrange("p (j s) -> p j s", j=8)
        v_sb = late[:, 13 * S:13 * S + TT * 640].rearrange("p (t c) -> p t c", t=TT)
        probs = late[:, 18 * S:22 * S].rearrange("p (b c) -> p b c", b=2)
        pT = late[:, 22 * S:24 * S].rearrange("p (b c) -> p b c", b=2)

        gates = G[:, :].rearrange("p (j s) -> p j s", j=16)
        cos_t, sin_t = gates[:, 12, :], gates[:, 13, :]
        swapped = gates[:, 14:16, :]
        ang, rnd = gates[:, 8, :], gates[:, 9, :]
        pos_i, ang_abs = gates[:, 10, :].bitcast(I32), gates[:, 11, :]
        square = G[:, 0:D]
        shared = G[:, 0:TT * D].rearrange("p (t d) -> p t d", t=TT)
        xgT = G[:, TT * D:TT * D + 2 * D].rearrange("p (b k s) -> p b k s", b=2, k=KD)
        y_sb = G[:, TT * D + 2 * D:TT * D + 4 * D].rearrange("p (b d) -> p b d", b=2)
        which = G[:, TT * D + 2 * D:TT * D + 4 * D].rearrange("p (i e) -> p i e", i=32)
        hsT = xgT[:, 1, :, :].rearrange("p k s -> p (k s)").rearrange("p (k s) -> p k s", k=KF)
        sg = xg[:, 0, 0:S]

        kdup = xg[:, 0, 0:S]
        o_da = O[:, 0:4 * S].rearrange("p (i h v) -> p i h v", i=TT, h=DA_HEADS)
        o_sw = O[:, 4 * S:8 * S].rearrange("p (i h v) -> p i h v", i=TT, h=SW_HEADS)
        mixed = O[:, 0:2 * S].rearrange("p (b s) -> p b s", b=2)
        junk2 = O[:, 2 * S:4 * S]
        TE = TT * N_EXP

        def rt(n, width=TE):
            return O[:, 4 * S + n * TE:4 * S + n * TE + width]

        def te(a):
            return a.rearrange("p (t e) -> p t e", t=TT)

        scores, choice, masked, replaced = rt(0), rt(1), rt(2), rt(3)
        chosen, cum, rank_m = rt(4), rt(5), rt(6)
        top8 = O[:, 0:TE]
        Z = O[:, TE:4 * TE].rearrange("p (t e c) -> p t e c", t=TT, c=3)
        onehot = sb("onehot", 2 * TT * SLOTS)[:, :].rearrange("p (b t s) -> p b t s", b=2, t=TT)
        iota_s = sb("iota_s", SLOTS)
        upper = sb("upper", P)
        ones = sb("ones", P)
        tri8 = sb("tri8", 64)
        rbias = sb("rbias", N_EXP)
        idx_i = ctx.enter_context(nc.sbuf_tensor("idx_i", [P, 2 * UNROLL], I32))
        idx_w = sb("idx_w", UNROLL)
        idx_f = sb("idx_f", 2 * 3)
        over_i = ctx.enter_context(nc.sbuf_tensor("over_i", [P, 40], I32))
        over_f = sb("over_f", 3 * 32)
        att_s = sb("att_s", 2 * 24)
        lam = gates[:, 7, 0:256]

        at = [0]

        def col(n):
            at[0] += n
            return small[:, at[0] - n:at[0]]

        cact, a1, a2 = col(8), col(8), col(8)
        eps, half_pi, sign, invf = col(1), col(1), col(1), col(1)
        ss1, rs1, ss2, rs2, ss3, rs3 = col(4), col(4), col(4), col(4), col(4), col(4)
        ssq, rsq = col(16), col(16)
        lam_s, lam_e, neglam = col(2), col(2), col(1)
        sinks = col(8)
        tok1, dest1 = col(4), col(4)
        denom, rden = col(4), col(4)
        dag = col(1)
        gh = col(8)

        psum = ctx.enter_context(nc.psum_tensor("psum", [P, 8 * 512], F32))

        def bank(b, n=1):
            return psum[:, b * 512:(b + n) * 512]

        T_BANK, O_BANK, IDX_BANK = 6, 7, 6

        kdup_ready = sem("kdup_ready")
        x_in = [sem(f"x_in{t}") for t in range(TT)]
        rows_in, misc_in, late_in = sem("rows_in"), sem("misc_in"), sem("late_in")
        landed = [sem(f"landed{s}") for s in range(12)]
        w_used = sem("w_used")
        consts = sem("consts")
        pool_step, dve_step, act_step = sem("pool_step"), sem("dve_step"), sem("act_step")
        rows_T, cols_ready, cact_ready = sem("rows_T"), sem("cols_ready"), sem("cact_ready")
        ss_ready, std_ready = sem("ss_ready"), sem("std_ready")
        xn_ready, xT_done, xT_free = sem("xn_ready"), sem("xT_done"), sem("xT_free")
        h_ready = sem("h_ready")
        ang_ready, rope_ready = sem("ang_ready"), sem("rope_ready")
        tile_done, free_a, free_d = sem("tile_done"), sem("free_a"), sem("free_d")
        roped, v_ready, lam_ready, lam_exp = sem("roped"), sem("v_ready"), sem("lam_ready"), sem("lam_exp")
        s_done, max_ready, exp_done, p_ready = sem("s_done"), sem("max_ready"), sem("exp_done"), sem("p_ready")
        pT_done, pT_ready, pv_done, o_ready = sem("pT_done"), sem("pT_ready"), sem("pv_done"), sem("o_ready")
        sq_done, da_std, da_scaled = sem("sq_done"), sem("da_std"), sem("da_scaled")
        yT_done, yT_ready = sem("yT_done"), sem("yT_ready")
        gate_row, gate_stored, g_in = sem("gate_row"), sem("gate_stored"), sem("g_in")
        merged_b, merged = sem("merged_b"), sem("merged")
        x2_ready = sem("x2_ready")
        xn2_stored = [sem(f"xn2_stored{t}") for t in range(2)]
        chosen_ready, routed = sem("chosen_ready"), sem("routed")
        sg_ready, hs_ready = sem("sg_ready"), sem("hs_ready")
        oh_ready, idx_done, idx_ready = sem("oh_ready"), sem("idx_done"), sem("idx_ready")
        gathered = [sem(f"gathered{b}") for b in range(2)]
        xgT_done, xgT_dve, xgT_act = sem("xgT_done"), sem("xgT_dve"), sem("xgT_act")
        gu_done, dn_done = sem("gu_done"), sem("dn_done")
        silu_ready, hact_ready = sem("silu_ready"), sem("hact_ready")
        y_ready = sem("y_ready")
        scattered = [sem(f"scattered{b}") for b in range(2)]
        over_list, over_done = sem("over_list"), sem("over_done")
        ov_landed = [sem(f"ov_landed{s}") for s in range(3)]
        ov = {n: sem(f"ov_{n}") for n in (
            "oh", "idxT", "idx", "gathered", "xgT", "xgT_dve", "xgT_act", "gu", "silu", "hact", "dn",
            "y", "scattered", "left")}
        y_in = [sem(f"y_in{b}") for b in range(2)]
        x3_ready, rs3_ready, sum_step = sem("x3_ready"), sem("rs3_ready"), sem("sum_step")
        summed, ss3_ready, std3_ready, fin_ready = sem("summed"), sem("ss3_ready"), sem("std3_ready"), sem("fin_ready")
        out_done = [sem(f"out_done{t}") for t in range(TT)]

        block = ctx.enter_context(nc.Block())

        def freed(eng, n):
            if n >= 2:
                owner = tiles[n - 2][2]
                count = sum(1 for t in tiles[:n - 1] if t[2] == owner)
                eng.wait_ge(free_a if owner == "A" else free_d, count)

        def past(eng, semaphore, n):
            if not isinstance(n, int) or n > 0:
                eng.wait_ge(semaphore, n)

        def expert_unit(src, e, cols_major):
            if cols_major:
                return src[bass.ds(e, 1)].rearrange("a (k p) f -> p (a k) f", p=P)
            return src[bass.ds(e, 1)].rearrange("a (k p) d -> p (a k) d", p=P)

        def as_k(s, k):
            return slot(s).rearrange("p (k f) -> p k f", k=k)

        @block.sync
        def _(sp):
            for t in range(TT):
                sp.dma_start(x_sb[:, t, :], x_d[t * P:(t + 1) * P, :]).then_inc(x_in[t], 16)
            src = {
                "ada": (w_ada_d, 256), "in": (w_in_d, 256), "gate": (w_gate_d, 256),
                "branch_a": (w_ba_d, 512), "branch_b": (w_bb_d, 512),
                "sh_gate": (w_sg_d, 256), "sh_up": (w_su_d, 256), "sh_down": (w_sd_d, D),
            }
            for n, (kind, u) in enumerate(units):
                if n >= RING:
                    sp.wait_ge(w_used, n - RING + 1)
                if kind == "out":
                    dram = w_out_d[u * 2 * P:(u + 1) * 2 * P, :].rearrange("(k p) n -> p k n", p=P)
                else:
                    w, width = src[kind]
                    dram = w[:, u * width:(u + 1) * width].rearrange("(k p) n -> p k n", p=P)
                sp.dma_start(as_k(n % RING, dram.shape[1]), dram).then_inc(landed[n % RING], 16)

            def load_expert(e, j):
                sp.dma_start(as_k(3 * j, KD), expert_unit(w_eg_d, e, True)).then_inc(landed[3 * j], 16)
                sp.dma_start(as_k(3 * j + 1, KD), expert_unit(w_eu_d, e, True)).then_inc(landed[3 * j + 1], 16)

            def load_down(e, j):
                sp.dma_start(as_k(3 * j + 2, KF), expert_unit(w_ed_d, e, False)).then_inc(landed[3 * j + 2], 16)

            sp.wait_ge(tile_done, tile_no["branch", 15] + 1)
            for j in (2, 3):
                load_expert(j, j)
                load_down(j, j)
            sp.wait_ge(w_used, len(units))
            for j in (0, 1):
                load_expert(j, j)
                load_down(j, j)
            with sp.Fori(1, N_EXP // UNROLL) as i:
                for j in range(UNROLL):
                    sp.wait_ge(gu_done, UNROLL * i + j - 3)
                    load_expert(UNROLL * i + j, j)
                    sp.wait_ge(dn_done, UNROLL * i + j - 3)
                    load_down(UNROLL * i + j, j)
            sp.wait_ge(dn_done, N_EXP)
            sp.wait_ge(over_list, 1)
            n_over = sp.value_load(over_i[0:1, 32:33], min_val=0, max_val=MAX_OVER)
            with sp.Fori(0, MAX_OVER) as i:
                with sp.If(i < n_over):
                    e = sp.value_load(over_i[0:1, bass.ds(i, 1)], min_val=0, max_val=N_EXP - 1)
                    sp.wait_ge(ov["dn"], i + 1)
                    for s, (w, k) in enumerate(((w_eg_d, True), (w_eu_d, True), (w_ed_d, False))):
                        sp.dma_start(as_k(s, KD if k else KF), expert_unit(w, e, k)).then_inc(ov_landed[s], 16)
            sp.wait_ge(scattered[0], 16 * (N_EXP // 2))
            sp.wait_ge(scattered[1], 16 * (N_EXP // 2))
            sp.wait_ge(over_done, 1)
            for t in range(TT):
                if t >= 2:
                    sp.wait_ge(summed, t - 1)
                sp.dma_start(wring[:, (t % 2) * 8 * D:(t % 2 + 1) * 8 * D],
                             y_d[t * P * TOP_K:(t + 1) * P * TOP_K, :].rearrange("(p k) d -> p (k d)", k=TOP_K)
                             ).then_inc(y_in[t % 2], 16)
            for t in range(TT):
                sp.wait_ge(fin_ready, t + 1)
                sp.dma_start(out_d[t * P:(t + 1) * P, :], x_sb[:, t, :]).then_inc(out_done[t], 16)
            for t in range(TT):
                sp.wait_ge(out_done[t], 16)

        @block.gpsimd
        def _(pool):
            steps = 0

            def step(ins):
                nonlocal steps
                steps += 1
                ins.then_inc(pool_step, 1)
                pool.wait_ge(pool_step, steps)

            pool.dma_start(pos_i, pos_d[0, :].partition_broadcast(P)).then_inc(misc_in, 16)
            pool.dma_start(invf, inv_freq_d).then_inc(misc_in, 16)
            pool.dma_start(lam[:, :], lam_d.rearrange("a d -> (a d)").partition_broadcast(P)).then_inc(misc_in, 16)
            pool.dma_start(sinks, sinks_d.partition_broadcast(P)).then_inc(misc_in, 16)
            pool.dma_start(bias_v[:, 0:512], b_in_d[1024:1536].partition_broadcast(P)).then_inc(misc_in, 16)
            pool.dma_start(bias_v[:, 512:640], b_in_d[2176:2304].partition_broadcast(P)).then_inc(misc_in, 16)
            pool.dma_start(rbias[:, :], r_bias_d.partition_broadcast(P)).then_inc(late_in, 16)
            pool.dma_start(fng[:, :], fng_d.partition_broadcast(P)).then_inc(late_in, 16)
            pool.dma_start(wr, w_router_d.rearrange("(k p) e -> p k e", p=P)).then_inc(late_in, 16)
            step(pool.memset(ident[:, :], 0.0))
            step(pool.memset(ones[:, :], 1.0))
            step(pool.memset(upper[:, :], 1.0))
            step(pool.memset(tri8[:, :], 1.0))
            step(pool.memset(eps, EPS))
            step(pool.memset(half_pi, math.pi / 2))
            step(pool.memset(sign, 1.0))
            for q in (0, 2):
                step(pool.memset(sign[32 * q:32 * q + 32], -1.0))
            step(pool.iota(iota_s[:, :], pattern=[[1, SLOTS]], base=0, channel_multiplier=0,
                           allow_small_or_imprecise_dtypes=True))
            step(pool.iota(tok1, pattern=[[P, TT]], base=1, channel_multiplier=1,
                           allow_small_or_imprecise_dtypes=True))
            step(pool.iota(dest1, pattern=[[P * TOP_K, TT]], base=1, channel_multiplier=TOP_K,
                           allow_small_or_imprecise_dtypes=True))
            step(pool.affine_select(out=upper[:, :], in_=upper[:, :], compare_op=ALU.is_gt, fill=0.0,
                                    base=0, pattern=[[1, P]], channel_multiplier=-1))
            t8 = tri8[:, :].rearrange("p (g h) -> p g h", g=8)
            step(pool.affine_select(out=t8, in_=t8, compare_op=ALU.is_gt, fill=0.0,
                                    base=0, pattern=[[1, 8], [-1, 8]], channel_multiplier=0))
            pool.affine_select(out=ident[:, :], in_=ident[:, :], compare_op=ALU.not_equal, fill=1.0,
                               base=0, pattern=[[-1, P]], channel_multiplier=1).then_inc(consts, 1)
            def gate_everywhere(n, src):
                pool.wait_ge(gate_row, n + 1)
                pool.dma_start(g_d[n, :].rearrange("(k p) -> p k", p=P), src,
                               allow_slow_non_contiguous=True).then_inc(gate_stored, 16)
                pool.wait_ge(gate_stored, 16 * (n + 1))
                if n:
                    pool.wait_ge(x2_ready, TT)
                pool.dma_start(gate_b[:, :], g_d[n, :].partition_broadcast(P)).then_inc(g_in, 16)

            gate_everywhere(0, gh)
            for t in range(TT):
                pool.wait_ge(xn_ready, TT + t + 1)
                pool.dma_start(xn2_d[t * P:(t + 1) * P, :], xg[:, t % 2, :]).then_inc(xn2_stored[t % 2], 16)
            gate_everywhere(1, mod[:, 5 * KD:6 * KD])
            for b in range(2):
                pool.wait_ge(xn2_stored[b], 32)

            token_bound, row_bound = pool.alloc_register("token_bound"), pool.alloc_register("row_bound")
            token_last, row_last = pool.alloc_register("token_last"), pool.alloc_register("row_last")
            pool.reg_mov(token_last, S - 2)
            pool.reg_mov(row_last, S * TOP_K - 2)

            def gather(e, j, first=False):
                pool.wait_ge(idx_ready, e + 1)
                if not first:
                    pool.wait_ge(xgT_done, e - 1)
                pool.reg_add(token_bound, token_last, 1)
                pool.indirect_dma_start(
                    out=xg[:, j % 2, :], out_offset=None, in_=xn2_d[:, :],
                    in_offset=bass.IndirectOffsetOnAxis(ap=idx_i[:, 2 * j:2 * j + 1], axis=0),
                    bounds_check=token_bound, oob_is_err=False).then_inc(gathered[j % 2], 16)

            def scatter(e, j):
                pool.wait_ge(y_ready, e + 1)
                pool.reg_add(row_bound, row_last, 1)
                pool.indirect_dma_start(
                    out=y_d[:, :], out_offset=bass.IndirectOffsetOnAxis(ap=idx_i[:, 2 * j + 1:2 * j + 2], axis=0),
                    in_=y_sb[:, j % 2, :], in_offset=None,
                    bounds_check=row_bound, oob_is_err=False).then_inc(scattered[j % 2], 16)

            pool.wait_ge(hs_ready, 2)
            pool.wait_ge(xT_done, 4 * TT)
            gather(0, 0, True)
            gather(1, 1, True)
            gather(2, 2)
            with pool.Fori(0, N_EXP // UNROLL - 1) as i:
                for j in range(UNROLL):
                    gather(UNROLL * i + j + 3, (j + 3) % UNROLL)
                    scatter(UNROLL * i + j, j)
            for j in range(UNROLL):
                if j == 0:
                    gather(N_EXP - 1, UNROLL - 1)
                scatter(N_EXP - UNROLL + j, j)

            pool.wait_ge(over_list, 1)
            for b in range(2):
                pool.wait_ge(scattered[b], 16 * (N_EXP // 2))
            pool.sem_inc(ov["left"], 1)
            n_over = pool.value_load(over_i[0:1, 32:33], min_val=0, max_val=MAX_OVER)
            with pool.Fori(0, MAX_OVER) as i:
                with pool.If(i < n_over):
                    pool.wait_ge(ov["idx"], i + 1)
                    pool.reg_add(token_bound, token_last, 1)
                    pool.indirect_dma_start(
                        out=xg[:, 0, :], out_offset=None, in_=xn2_d[:, :],
                        in_offset=bass.IndirectOffsetOnAxis(ap=idx_i[:, 0:1], axis=0),
                        bounds_check=token_bound, oob_is_err=False).then_inc(ov["gathered"], 16)
                    pool.wait_ge(ov["y"], i + 2)
                    pool.reg_add(row_bound, row_last, 1)
                    pool.indirect_dma_start(
                        out=y_d[:, :], out_offset=bass.IndirectOffsetOnAxis(ap=idx_i[:, 1:2], axis=0),
                        in_=y_sb[:, 0, :], in_offset=None,
                        bounds_check=row_bound, oob_is_err=False).then_inc(ov["scattered"], 16)
                    pool.wait_ge(ov["scattered"], 16 * (i + 1))
                    pool.sem_inc(ov["left"], 1)
            pool.sem_inc(over_done, 1)

        @block.scalar
        def _(act):
            vec = [(c_d[0, :], ROW_C, 8), (b_ada_d, ROW_ADA, 48), (n1_d, ROW_N1, 8), (n2_d, ROW_N2, 8),
                   (b_in_d, ROW_BIN, 18), (b_gate_d, ROW_BG, 16), (dag_d, ROW_DAG, 1)]
            for dram, r, n in vec:
                act.dma_start(rows[r:r + n, :], dram.rearrange("(k p) -> k p", p=P)).then_inc(rows_in, 16)

            for t in range(TT):
                act.wait_ge(x_in[t], 16)
                if t:
                    act.wait_ge(ss_ready, t)
                act.activation(square, x_sb[:, t, :], ACT.Square, accum_out=ss1[:, t:t + 1]).then_inc(ss_ready, 1)
            act.wait_ge(ss_ready, TT)
            act.wait_ge(consts, 1)
            act.activation(rs1, ss1, ACT.Sqrt, bias=eps, scale=1.0 / D).then_inc(std_ready, 1)
            act.wait_ge(cols_ready, 1)
            act.activation(cact, cols[:, ROW_C:ROW_C + 8], ACT.Silu).then_inc(cact_ready, 1)
            act.wait_ge(ang_ready, 1)
            act.activation(sin_t, ang, ACT.Sin, scale=sign).then_inc(rope_ready, 1)
            act.activation(cos_t, ang_abs, ACT.Sin, bias=half_pi, scale=-1.0).then_inc(rope_ready, 1)
            act.wait_ge(lam_ready, 1)
            act.activation(lam_e, lam_s, ACT.Exp).then_inc(lam_exp, 1)

            def empty_qk(j):
                n = tile_no["qk", j]
                b = bank(n % 2)
                c0 = ROW_BIN + (j if j < 8 else j + 4)
                act.wait_ge(tile_done, n + 1)
                act.activation(qk[:, j, :], b, ACT.Identity, bias=cols[:, c0:c0 + 1])
                if j >= 2:
                    act.wait_ge(roped, j - 1)
                for q in range(4):
                    r = q ^ 1
                    ins = act.activation(swapped[32 * r:32 * r + 32, j % 2, :], b[32 * q:32 * q + 32],
                                         ACT.Identity, bias=cols[32 * q:32 * q + 32, c0:c0 + 1])
                ins.then_inc(free_a, 1)

            for j in range(13):
                empty_qk(j)

            def exps(u):
                kind, h, i = att[u]
                sc = bank(2 + 2 * (u % 2), 2)
                s = att_s[:, 24 * (u % 2):24 * (u % 2) + 24]
                act.wait_ge(max_ready, u + 1)
                if u >= 2:
                    act.wait_ge(pT_done, t_steps[u - 1])
                if kind == "da":
                    w = (i + 1) * P
                    for m in range(2):
                        ins = act.activation(probs[:, u % 2, m * S:m * S + w], sc[:, m * S:m * S + w], ACT.Exp,
                                             bias=s[:, 2 + m:3 + m], scale=SCALE, accum_out=s[:, 4 + m:5 + m])
                else:
                    w = min(i + 1, 2) * P
                    for r in range(4):
                        act.activation(probs[:, u % 2, r * 256:r * 256 + w], sc[:, r * 256:r * 256 + w], ACT.Exp,
                                       bias=s[:, 4 + r:5 + r], scale=SCALE, accum_out=s[:, 8 + r:9 + r])
                    ins = act.activation(s[:, 16:20], s[:, 12:16], ACT.Exp)
                ins.then_inc(exp_done, 1)

            def turned(u):
                kind, h, i = att[u]
                nb = (i + 1) if kind == "da" else min(i + 1, 2) * 2
                for n in range(t_steps[u], t_steps[u] + (1 if kind == "da" else 2)):
                    act.wait_ge(pT_done, n + 1)
                    if n >= 2:
                        act.wait_ge(pv_done, n - 1)
                    act.activation(pT[:, n % 2, 0:nb * P], bank(T_BANK)[:, 0:nb * P], ACT.Copy).then_inc(pT_ready, 1)

            def gate_tile(j):
                n = tile_no["gate", j]
                act.wait_ge(tile_done, n + 1)
                act.activation(gates[:, j, :], bank(n % 2), ACT.Tanh, scale=0.5,
                               bias=cols[:, ROW_BG + j:ROW_BG + j + 1]).then_inc(free_a, 1)

            exps(0)
            act.wait_ge(roped, 13)
            for u in range(NU):
                if u + 1 < NU:
                    exps(u + 1)
                for kind, j in fill_of(u):
                    if kind == "gate":
                        gate_tile(j)
                turned(u)
                if att[u][0] == "da":
                    _, h, i = att[u]
                    act.wait_ge(o_ready, u + 1)
                    if u:
                        act.wait_ge(sq_done, u)
                    act.activation(rows[:, :], o_da[:, i, h, :], ACT.Square,
                                   accum_out=ssq[:, i * 4 + h:i * 4 + h + 1]).then_inc(sq_done, 1)
            act.wait_ge(sq_done, 16)
            act.activation(rsq, ssq, ACT.Sqrt, bias=eps, scale=1.0 / P).then_inc(da_std, 1)
            for n in range(8):
                act.wait_ge(yT_done, n + 1)
                if n < 4:
                    ins = act.activation(yT[:, 4 + n, :], bank(2 + n), ACT.Copy)
                else:
                    ins = act.activation(yT[:, n - 4, :], bank(n - 2), ACT.Copy, scale=dag)
                ins.then_inc(yT_ready, 1)

            for t in range(TT):
                act.wait_ge(x2_ready, t + 1)
                if t:
                    act.wait_ge(ss_ready, TT + t)
                act.activation(junk2, x_sb[:, t, :], ACT.Square, accum_out=ss2[:, t:t + 1]).then_inc(ss_ready, 1)
                act.wait_ge(ss_ready, TT + t + 1)
                act.activation(rs2[:, t:t + 1], ss2[:, t:t + 1], ACT.Sqrt, bias=eps, scale=1.0 / D).then_inc(std_ready, 1)
            n = tile_no["router", 0]
            act.wait_ge(tile_done, n + 1)
            act.wait_ge(xn2_stored[0], 32)
            act.activation(scores, bank(n % 2)[:, 0:TE], ACT.Sigmoid).then_inc(free_a, 1)
            for k in range(KF):
                n = tile_no["sh_gate", k]
                act.wait_ge(tile_done, n + 1)
                if k:
                    act.wait_ge(hs_ready, k)
                act.activation(sg, bank(n % 2), ACT.Silu).then_inc(free_a, 1)
            for j in range(2 * TT):
                n = tile_no["sh_down", j]
                act.wait_ge(tile_done, n + 1)
                act.activation(shared[:, j // 2, (j % 2) * S:(j % 2 + 1) * S], bank(n % 2), ACT.Copy).then_inc(free_a, 1)

            def turn_x(e, b, done, ready):
                act.wait_ge(done, e + 1)
                for k in range(KD // 2, KD):
                    ins = act.activation(xgT[:, b, k, :], bank(4, 2)[:, k * P:(k + 1) * P], ACT.Identity,
                                         bias=mod[:, 3 * KD + k:3 * KD + k + 1], scale=a2[:, k:k + 1])
                ins.then_inc(ready, 1)

            def silu(e, b, done, ready):
                act.wait_ge(done, e + 1)
                act.activation(hact[:, b, :, :].rearrange("p k s -> p (k s)"), bank(2 + b)[:, 0:KF * SLOTS],
                               ACT.Silu).then_inc(ready, 1)

            def weigh(e, b, w, done, ready):
                act.wait_ge(done, e + 1)
                act.activation(y_sb[:, b, 0:S], bank(0), ACT.Copy, scale=w)
                act.activation(y_sb[:, b, S:D], bank(1), ACT.Copy, scale=w).then_inc(ready, 1)

            def act_pass(i, last=False):
                for j in range(UNROLL):
                    e = UNROLL * i + j
                    if not last or j + 1 < UNROLL:
                        past(act, dn_done, e)
                        silu(e + 1, (j + 1) % 2, gu_done, silu_ready)
                    if not last or j + 2 < UNROLL:
                        act.wait_ge(gu_done, e + 1)
                        turn_x(e + 2, j % 2, xgT_done, xgT_act)
                    past(act, scattered[j % 2], 16 * (UNROLL // 2 * i + j // 2))
                    weigh(e, j % 2, idx_w[:, j:j + 1], dn_done, y_ready)

            act.wait_ge(over_list, 1)
            turn_x(0, 0, xgT_done, xgT_act)
            turn_x(1, 1, xgT_done, xgT_act)
            silu(0, 0, gu_done, silu_ready)
            act_pass(0)
            with act.Fori(1, N_EXP // UNROLL - 1) as i:
                act_pass(i)
            act_pass(N_EXP // UNROLL - 1, True)

            act.sem_inc(ov["y"], 1)
            n_over = act.value_load(over_i[0:1, 32:33], min_val=0, max_val=MAX_OVER)
            with act.Fori(0, MAX_OVER) as i:
                with act.If(i < n_over):
                    turn_x(i, 0, ov["xgT"], ov["xgT_act"])
                    silu(i, 0, ov["gu"], ov["silu"])
                    act.wait_ge(ov["left"], i + 1)
                    weigh(i + 1, 0, idx_w[:, 0:1], ov["dn"], ov["y"])

            for t in range(TT):
                act.wait_ge(x3_ready, t + 1)
                if t:
                    act.wait_ge(ss3_ready, t)
                act.activation(junk2, x_sb[:, t, :], ACT.Square, accum_out=ss3[:, t:t + 1]).then_inc(ss3_ready, 1)
                act.wait_ge(ss3_ready, t + 1)
                act.activation(rs3[:, t:t + 1], ss3[:, t:t + 1], ACT.Sqrt, bias=eps, scale=1.0 / D).then_inc(std3_ready, 1)

        @block.vector
        def _(dve):
            steps = [0]

            def step(ins):
                ins.then_inc(dve_step, 1)
                steps[0] = steps[0] + 1

            def settle():
                dve.wait_ge(dve_step, steps[0])

            dve.wait_ge(rows_T, 1)
            step(dve.tensor_copy(cols[:, :], bank(O_BANK)[:, 0:ROWS]))
            settle()
            dve.tensor_scalar(dag, cols[:, ROW_DAG:ROWS], 1.0 - LAMBDA_INIT, None, ALU.mult)
            dve.tensor_scalar(cols[:, ROW_BG:ROW_BG + 16], cols[:, ROW_BG:ROW_BG + 16], 0.5, None,
                              ALU.mult).then_inc(cols_ready, 1)

            dve.wait_ge(std_ready, 1)
            step(dve.reciprocal(rs1, rs1))
            settle()

            def normed(t, r):
                dve.tensor_scalar(xg[:, t % 2, :], x_sb[:, t, :], r[:, t:t + 1], None, ALU.mult).then_inc(xn_ready, 1)

            def turned_tile(t, g0):
                for g in (g0 + 2 * t, g0 + 2 * t + 1):
                    half = g % 2
                    dve.wait_ge(xT_done, g + 1)
                    dve.tensor_copy(hT[:, 4 * half:4 * half + 4, t * P:(t + 1) * P],
                                    bank(2 + g % 2).rearrange("p (k s) -> p k s", k=4)).then_inc(xT_free, 1)

            for t in range(TT):
                normed(t, rs1)
                if t:
                    turned_tile(t - 1, 0)
            turned_tile(TT - 1, 0)

            dve.wait_ge(misc_in, 16 * 6)
            step(dve.tensor_copy(ang_abs, pos_i))
            settle()
            step(dve.tensor_scalar(ang, ang_abs, invf, None, ALU.mult))
            settle()
            step(dve.tensor_scalar(rnd, ang, 1.0 / (2 * math.pi), ROUND, ALU.mult, ALU.add))
            settle()
            step(dve.tensor_scalar(rnd, rnd, ROUND, None, ALU.subtract))
            settle()
            for part in (TWO_PI_A, TWO_PI_B, TWO_PI_C):
                step(dve.scalar_tensor_tensor(out=ang, in0=rnd, scalar=-part, in1=ang, op0=ALU.mult, op1=ALU.add))
                settle()
            step(dve.tensor_scalar(ang, ang, PI_IN, -PI_IN, ALU.min, ALU.max))
            settle()
            dve.scalar_tensor_tensor(out=ang_abs, in0=ang, scalar=-1.0, in1=ang, op0=ALU.mult,
                                     op1=ALU.max).then_inc(ang_ready, 1)
            lv = lam[:, :].rearrange("p (a b d) -> p a b d", a=2, b=2)
            lp = lam[:, 0:2 * HD].rearrange("p (a d) -> p a d", a=2)
            step(dve.tensor_tensor(lp[:, 0, :], lv[:, 0, 0, :], lv[:, 0, 1, :], ALU.mult))
            settle()
            step(dve.tensor_tensor(lp[:, 1, :], lv[:, 1, 0, :], lv[:, 1, 1, :], ALU.mult))
            settle()
            dve.tensor_reduce(lam_s, lp, AX_X, ALU.add).then_inc(lam_ready, 1)
            dve.wait_ge(lam_exp, 1)
            dve.scalar_tensor_tensor(out=neglam, in0=lam_e[:, 1:2], scalar=-LAMBDA_INIT, in1=lam_e[:, 0:1],
                                     op0=ALU.add, op1=ALU.subtract)

            def ada_tile(u):
                n = tile_no["ada", u]
                dve.wait_ge(tile_done, n + 1)
                step(dve.tensor_tensor(mod[:, 2 * u:2 * u + 2], bank(n % 2)[:, 0:2],
                                       cols[:, ROW_ADA + 2 * u:ROW_ADA + 2 * u + 2], ALU.add))
                settle()
                dve.sem_inc(free_d, 1)

            def part(n):
                return mod[:, n * KD:(n + 1) * KD]

            for u in range(8):
                ada_tile(u)
            step(dve.scalar_tensor_tensor(out=a1, in0=part(1), scalar=1.0, in1=cols[:, ROW_N1:ROW_N1 + 8],
                                          op0=ALU.add, op1=ALU.mult))
            dve.wait_ge(xT_free, 2 * TT)
            settle()
            for k in range(KD):
                dve.tensor_scalar(hT[:, k, :], hT[:, k, :], a1[:, k:k + 1], part(0)[:, k:k + 1],
                                  ALU.mult, ALU.add).then_inc(h_ready, 1)

            dve.wait_ge(rope_ready, 2)
            for kind, j, _ in [t for t in tiles if t[0] in ("qk", "v")]:
                n = tile_no[kind, j]
                if kind == "qk":
                    count = sum(1 for t in tiles[:n + 1] if t[2] == "A")
                    dve.wait_ge(free_a, count)
                    dve.tensor_tensor(qk[:, j, :], qk[:, j, :], cos_t, ALU.mult)
                    step(dve.tensor_tensor(swapped[:, j % 2, :], swapped[:, j % 2, :], sin_t, ALU.mult))
                    settle()
                    dve.tensor_tensor(qk[:, j, :], qk[:, j, :], swapped[:, j % 2, :], ALU.add).then_inc(roped, 1)
                    continue
                dve.wait_ge(tile_done, n + 1)
                if j < 4:
                    c, t0 = 256 * (j // 2), 2 * (j % 2)
                    dve.tensor_tensor(v_sb[:, t0:t0 + 2, c:c + 256], bank(n % 2).rearrange("p (t c) -> p t c", t=2),
                                      bias_v[:, c:c + 256].unsqueeze(1).broadcast_to([P, 2, 256]),
                                      ALU.add).then_inc(free_d, 1)
                else:
                    dve.tensor_tensor(v_sb[:, :, 512:640], bank(n % 2).rearrange("p (t c) -> p t c", t=TT),
                                      bias_v[:, 512:640].unsqueeze(1).broadcast_to([P, TT, P]),
                                      ALU.add).then_inc(free_d, 1)
            dve.wait_ge(roped, 13)
            dve.tensor_copy(kdup[0:64], qk[64:128, 12, :])
            dve.tensor_copy(kdup[64:128], qk[0:64, 12, :]).then_inc(kdup_ready, 1)

            def by_bank(a):
                return a.rearrange("p (a b) -> p b a", b=2)

            def pairs(a):
                return a.rearrange("p (b a) -> p b a", b=2)

            def row_max(u):
                kind, h, i = att[u]
                s = att_s[:, 24 * (u % 2):24 * (u % 2) + 24]
                dve.wait_ge(s_done, u + 1)
                if kind == "da":
                    w = (i + 1) * P
                    sc = bank(2 + 2 * (u % 2), 2).rearrange("p (m c) -> p m c", m=2)
                    step(dve.memset(sc[0:CHUNK, :, w - CHUNK:w], MASKED))
                    settle()
                    step(dve.tensor_reduce(s[:, 0:2], sc[:, :, 0:w], AX_X, ALU.max))
                    settle()
                    dve.tensor_scalar(s[:, 2:4], s[:, 0:2], -SCALE, None, ALU.mult).then_inc(max_ready, 1)
                    return
                w = min(i + 1, 2) * P
                sc = bank(2 + 2 * (u % 2), 2).rearrange("p (m c) -> p m c", m=4)
                step(dve.memset(sc[0:CHUNK, :, w - CHUNK:w], MASKED))
                if i:
                    dve.memset(sc[0:CHUNK, :, 0:CHUNK], MASKED)
                    step(dve.memset(sc[CHUNK:P, :, 0:2 * CHUNK], MASKED))
                settle()
                step(dve.tensor_reduce(s[:, 0:4], sc[:, :, 0:w], AX_X, ALU.max))
                settle()
                sink = by_bank(sinks[:, 4 * h:4 * h + 4])
                step(dve.scalar_tensor_tensor(out=pairs(s[:, 0:4]), in0=pairs(s[:, 0:4]), scalar=SCALE, in1=sink,
                                              op0=ALU.mult, op1=ALU.max))
                settle()
                dve.tensor_scalar(s[:, 4:8], s[:, 0:4], -1.0, None, ALU.mult)
                dve.tensor_tensor(pairs(s[:, 12:16]), sink, pairs(s[:, 0:4]), ALU.subtract).then_inc(max_ready, 1)

            def combine(u):
                kind, h, i = att[u]
                s = att_s[:, 24 * (u % 2):24 * (u % 2) + 24]
                dve.wait_ge(exp_done, u + 1)
                if kind == "da":
                    w = (i + 1) * P
                    p0, p1 = probs[:, u % 2, 0:w], probs[:, u % 2, S:S + w]
                    step(dve.reciprocal(s[:, 6:8], s[:, 4:6]))
                    settle()
                    step(dve.tensor_scalar(p1, p1, s[:, 7:8], neglam, ALU.mult, ALU.mult))
                    settle()
                    dve.scalar_tensor_tensor(out=p0, in0=p0, scalar=s[:, 6:7], in1=p1, op0=ALU.mult,
                                             op1=ALU.add).then_inc(p_ready, 1)
                    return
                step(dve.tensor_tensor(s[:, 20:24], s[:, 8:12], s[:, 16:20], ALU.add))
                settle()
                step(dve.reciprocal(s[:, 20:24], s[:, 20:24]))

            def out_rows(u):
                kind, h, i = att[u]
                s = att_s[:, 24 * (u % 2):24 * (u % 2) + 24]
                dve.wait_ge(pv_done, t_steps[u] + (1 if kind == "da" else 2))
                if kind == "da":
                    dve.tensor_copy(o_da[:, i, h, :], bank(O_BANK)[:, 0:P]).then_inc(o_ready, 1)
                else:
                    settle()
                    dve.tensor_tensor(o_sw[:, i, 4 * h:4 * h + 4, :].rearrange("p (a b) v -> p b a v", b=2),
                                      bank(O_BANK)[:, 0:256].rearrange("p (b a v) -> p b a v", b=2, a=2),
                                      pairs(s[:, 20:24]).unsqueeze(3).broadcast_to([P, 2, 2, HD]),
                                      ALU.mult).then_inc(o_ready, 1)

            row_max(0)
            for u in range(NU):
                combine(u)
                if u + 1 < NU:
                    row_max(u + 1)
                for kind, j in fill_of(u):
                    if kind == "ada":
                        ada_tile(j)
                        if j == 11:
                            dve.tensor_scalar(gh, part(2), 0.5, None, ALU.mult).then_inc(gate_row, 1)
                        if j == 19:
                            dve.scalar_tensor_tensor(out=a2, in0=part(4), scalar=1.0, in1=cols[:, ROW_N2:ROW_N2 + 8],
                                                     op0=ALU.add, op1=ALU.mult)
                        if j == 23:
                            dve.sem_inc(gate_row, 1)
                out_rows(u)

            dve.wait_ge(da_std, 1)
            step(dve.reciprocal(rsq, rsq))
            settle()
            oda = O[:, 0:4 * S].rearrange("p (n v) -> p n v", v=P)
            dve.tensor_tensor(oda, oda, rsq.unsqueeze(2).broadcast_to([P, 16, P]), ALU.mult).then_inc(da_scaled, 1)

            for j in range(16):
                n = tile_no["branch", j]
                m, b = j // 2, j % 2
                dve.wait_ge(tile_done, n + 1)
                dve.scalar_tensor_tensor(out=gates[:, 8 * b + m, :], in0=gates[:, 8 * b + m, :], scalar=1.0,
                                         in1=bank(n % 2), op0=ALU.add, op1=ALU.mult).then_inc(free_d, 1)
                if b:
                    count = sum(1 for t in tiles[:n + 1] if t[2] == "D")
                    dve.wait_ge(free_d, count)
                    dve.tensor_tensor(gates[:, m, :], gates[:, m, :], gates[:, 8 + m, :], ALU.add).then_inc(merged, 1)

            dve.wait_ge(g_in, 16)

            def norm2(t):
                dve.wait_ge(std_ready, 1 + t + 1)
                step(dve.reciprocal(rs2[:, t:t + 1], rs2[:, t:t + 1]))
                settle()
                if t >= 2:
                    dve.wait_ge(xn2_stored[t % 2], 16)
                normed(t, rs2)
                turned_tile(t, 2 * TT)

            for t in range(TT):
                for half in range(2):
                    n = tile_no["out", 2 * t + half]
                    dve.wait_ge(tile_done, n + 1)
                    step(dve.tensor_tensor(mixed[:, half, :], bank(n % 2), gate_b[:, half * S:(half + 1) * S], ALU.mult))
                    settle()
                    dve.sem_inc(free_d, 1)
                    xs = x_sb[:, t, half * S:(half + 1) * S]
                    ins = dve.tensor_tensor(xs, xs, mixed[:, half, :], ALU.add)
                    step(ins) if half == 0 else ins.then_inc(x2_ready, 1)
                if t:
                    norm2(t - 1)
            norm2(TT - 1)
            dve.wait_ge(xT_free, 4 * TT)
            for k in range(KD):
                dve.tensor_scalar(hT[:, k, :], hT[:, k, :], a2[:, k:k + 1], part(3)[:, k:k + 1],
                                  ALU.mult, ALU.add).then_inc(h_ready, 1)

            dve.wait_ge(late_in, 48)
            n = tile_no["router", 0]
            dve.wait_ge(free_a, sum(1 for t in tiles[:n + 1] if t[2] == "A"))
            step(dve.tensor_tensor(te(choice), te(scores), rbias[:, :].unsqueeze(1).broadcast_to([P, TT, N_EXP]), ALU.add))
            settle()
            for g in range(TT * N_GRP):
                ins = dve.max(top8[:, 8 * g:8 * g + 8], choice[:, 8 * g:8 * g + 8])
            step(ins)
            settle()
            best = top8.rearrange("p (g k) -> p g k", k=8)
            gsc, grank = over_f[:, 0:32], over_f[:, 32:64]
            step(dve.tensor_tensor(gsc.unsqueeze(2), best[:, :, 0:1], best[:, :, 1:2], ALU.add))
            settle()
            def tgg(a):
                return a.rearrange("p (t g h) -> p t g h", t=TT, g=8)

            rival = gsc.rearrange("p (t h) -> p t h", t=TT).unsqueeze(2).broadcast_to([P, TT, 8, 8])
            own = gsc.rearrange("p (t g) -> p t g", t=TT).unsqueeze(3).broadcast_to([P, TT, 8, 8])
            dve.tensor_tensor(tgg(masked), rival, own, ALU.is_gt)
            step(dve.tensor_tensor(tgg(replaced), rival, own, ALU.is_equal))
            settle()
            step(dve.tensor_tensor(replaced.rearrange("p (t g) -> p t g", t=TT), replaced.rearrange("p (t g) -> p t g", t=TT),
                                   tri8[:, :].unsqueeze(1).broadcast_to([P, TT, 64]), ALU.mult))
            settle()
            step(dve.tensor_tensor(masked, masked, replaced, ALU.add))
            settle()
            step(dve.tensor_reduce(grank, masked.rearrange("p (g h) -> p g h", h=8), AX_X, ALU.add))
            settle()
            step(dve.tensor_scalar(grank, grank, float(TOP_G), None, ALU.is_lt))
            settle()
            kept = grank.unsqueeze(2).broadcast_to([P, TT * N_GRP, 8])
            g8 = lambda a: a.rearrange("p (g k) -> p g k", k=8)
            step(dve.tensor_tensor(g8(masked), g8(choice), kept, ALU.mult))
            step(dve.tensor_scalar(gsc, grank, 1.0, -MASKED, ALU.subtract, ALU.mult))
            settle()
            step(dve.tensor_tensor(g8(masked), g8(masked), gsc.unsqueeze(2).broadcast_to([P, TT * N_GRP, 8]), ALU.add))
            settle()
            for t in range(TT):
                ins = dve.max(top8[:, 8 * t:8 * t + 8], te(masked)[:, t, :])
            step(ins)
            settle()
            for t in range(TT):
                ins = dve.match_replace(te(replaced)[:, t, :], top8[:, 8 * t:8 * t + 8], te(masked)[:, t, :], 2 * MASKED)
            step(ins)
            settle()
            dve.tensor_tensor(chosen, replaced, masked, ALU.not_equal).then_inc(chosen_ready, 1)
            dve.wait_ge(chosen_ready, 1)
            step(dve.tensor_tensor(masked, scores, chosen, ALU.mult))
            for t in range(TT):
                ins = dve.tensor_tensor_scan(te(cum)[:, t, :], ones[:, 0:N_EXP], te(chosen)[:, t, :], 0.0, ALU.mult, ALU.add)
            step(ins)
            settle()
            step(dve.tensor_reduce(denom, te(masked), AX_X, ALU.add))
            step(dve.tensor_tensor(cum, cum, chosen, ALU.subtract))
            settle()
            step(dve.reciprocal(rden, denom))
            step(dve.tensor_copy(Z[:, :, :, 0], tok1.unsqueeze(2).broadcast_to([P, TT, N_EXP])))
            step(dve.tensor_tensor(Z[:, :, :, 1], te(cum), dest1.unsqueeze(2).broadcast_to([P, TT, N_EXP]), ALU.add))
            settle()
            step(dve.scalar_tensor_tensor(out=Z[:, :, :, 2], in0=te(masked), scalar=ROUTED_SCALE,
                                          in1=rden.unsqueeze(2).broadcast_to([P, TT, N_EXP]), op0=ALU.mult, op1=ALU.mult))

            def shared_act(k):
                n = tile_no["sh_up", k]
                dve.wait_ge(tile_done, n + 1)
                m = tile_no["sh_gate", k]
                dve.wait_ge(free_a, sum(1 for t in tiles[:m + 1] if t[2] == "A"))
                dve.tensor_tensor(hsT[:, k, :], sg, bank(n % 2), ALU.mult).then_inc(hs_ready, 1)

            shared_act(0)
            dve.wait_ge(hs_ready, 1)
            dve.sem_inc(free_d, 1)
            n = tile_no["rank", 0]
            dve.wait_ge(tile_done, n + 1)
            counts, over, cum_o = replaced[:, 0:64], replaced[:, 64:128], replaced[:, 128:192]
            step(dve.scalar_tensor_tensor(out=rank_m, in0=bank(n % 2)[:, 0:TE], scalar=1.0, in1=chosen, op0=ALU.add, op1=ALU.mult))
            step(dve.tensor_copy(counts, bank(n % 2)[:, TE:TE + N_EXP]))
            settle()
            dve.sem_inc(free_d, 1)
            step(dve.tensor_scalar(rank_m, rank_m, 1.0, None, ALU.subtract))
            settle()

            def column(e):
                return te(rank_m)[:, :, bass.ds(e, 1)].broadcast_to([P, TT, SLOTS])

            slots4 = iota_s[:, :].unsqueeze(1).broadcast_to([P, TT, SLOTS])

            def one_hot(e, b):
                dve.tensor_tensor(onehot[:, b, :, :], slots4, column(e), ALU.is_equal).then_inc(oh_ready, 1)

            def indices(j, ready):
                v = bank(IDX_BANK)[:, 0:3]
                step(dve.tensor_scalar(idx_f[:, 0:2], v[:, 0:2], 0.0, SKIP, ALU.is_equal, ALU.mult))
                settle()
                dve.tensor_copy(idx_w[:, j:j + 1], v[:, 2:3])
                dve.scalar_tensor_tensor(out=idx_i[:, 2 * j:2 * j + 2], in0=v[:, 0:2], scalar=-1.0, in1=idx_f[:, 0:2],
                                         op0=ALU.add, op1=ALU.add).then_inc(ready, 1)

            one_hot(0, 0)
            one_hot(1, 1)
            shared_act(1)
            dve.wait_ge(hs_ready, 2)
            dve.sem_inc(free_d, 1)
            for e in range(3):
                dve.wait_ge(idx_done, e + 1)
                indices(e, idx_ready)
                if e < 2:
                    one_hot(e + 2, e % 2)

            step(dve.tensor_scalar(over, counts, float(SLOTS), None, ALU.is_gt))
            settle()
            for m in (2, 3):
                step(dve.scalar_tensor_tensor(out=over, in0=counts, scalar=float(m * SLOTS), in1=over, op0=ALU.is_gt, op1=ALU.add))
                settle()
            step(dve.tensor_tensor_scan(cum_o, ones[:, 0:N_EXP], over, 0.0, ALU.mult, ALU.add))
            settle()
            step(dve.tensor_copy(over_i[:, 32:33], cum_o[:, N_EXP - 1:N_EXP]))
            step(dve.tensor_tensor(which, cum_o.unsqueeze(1).broadcast_to([P, 32, N_EXP]),
                                   iota_s[:, 0:32].unsqueeze(2).broadcast_to([P, 32, N_EXP]), ALU.is_le))
            settle()
            step(dve.tensor_reduce(over_f[:, 64:96], which, AX_X, ALU.add))
            settle()
            step(dve.tensor_copy(over_i[:, 0:32], over_f[:, 64:96]))
            step(dve.tensor_tensor(which, which, over.unsqueeze(1).broadcast_to([P, 32, N_EXP]), ALU.mult))
            settle()
            step(dve.tensor_reduce(over_f[:, 0:32], which, AX_X, ALU.add))
            settle()
            step(dve.tensor_tensor(over_f[:, 0:32], iota_s[:, 0:32], over_f[:, 0:32], ALU.subtract))
            settle()
            dve.tensor_scalar(over_f[:, 0:32], over_f[:, 0:32], float(SLOTS), float(SLOTS), ALU.mult,
                              ALU.add).then_inc(over_list, 1)

            def turn_x(e, b, done, ready):
                dve.wait_ge(done, e + 1)
                for k in range(KD // 2):
                    ins = dve.tensor_scalar(xgT[:, b, k, :], bank(4, 2)[:, k * P:(k + 1) * P], a2[:, k:k + 1],
                                            mod[:, 3 * KD + k:3 * KD + k + 1], ALU.mult, ALU.add)
                ins.then_inc(ready, 1)

            def gate_up(e, b, done, ready):
                dve.wait_ge(done, e + 1)
                h = hact[:, b, :, :].rearrange("p k s -> p (k s)")
                dve.tensor_tensor(h, h, bank(2 + b)[:, KF * SLOTS:2 * KF * SLOTS], ALU.mult).then_inc(ready, 1)

            def dve_pass(i, last=False):
                for j in range(UNROLL):
                    e = UNROLL * i + j
                    if not last or j + 3 < UNROLL:
                        dve.wait_ge(idx_done, e + 4)
                        past(dve, scattered[(j + 1) % 2], 16 * (UNROLL // 2 * i + (j + 1) // 2))
                        indices((j + 3) % UNROLL, idx_ready)
                    if not last or j + 1 < UNROLL:
                        gate_up(e + 1, (j + 1) % 2, silu_ready, hact_ready)
                    if not last or j + 2 < UNROLL:
                        dve.wait_ge(gu_done, e + 1)
                        turn_x(e + 2, j % 2, xgT_done, xgT_dve)
                    if not last:
                        dve.wait_ge(idx_done, e + 3)
                        one_hot(e + 4, j % 2)

            turn_x(0, 0, xgT_done, xgT_dve)
            turn_x(1, 1, xgT_done, xgT_dve)
            gate_up(0, 0, silu_ready, hact_ready)
            passes = N_EXP // UNROLL - 1
            before = steps[0]
            dve_pass(0)
            with dve.Fori(1, passes) as i:
                steps[0] = UNROLL * i + before
                dve_pass(i)
            steps[0] = before + UNROLL * passes
            dve_pass(passes, True)

            dve.wait_ge(scattered[0], 16 * (N_EXP // 2))
            dve.wait_ge(scattered[1], 16 * (N_EXP // 2))
            n_over = dve.value_load(over_i[0:1, 32:33], min_val=0, max_val=MAX_OVER)
            before = steps[0]
            with dve.Fori(0, MAX_OVER) as i:
                with dve.If(i < n_over):
                    e = dve.value_load(over_i[0:1, bass.ds(i, 1)], min_val=0, max_val=N_EXP - 1)
                    steps[0] = i + before
                    dve.wait_ge(ov["left"], i + 1)
                    dve.scalar_tensor_tensor(out=onehot[:, 0, :, :], in0=slots4, scalar=over_f[:, bass.ds(i, 1)],
                                             in1=column(e), op0=ALU.add, op1=ALU.is_equal).then_inc(ov["oh"], 1)
                    dve.wait_ge(ov["idxT"], i + 1)
                    indices(0, ov["idx"])
                    turn_x(i, 0, ov["xgT"], ov["xgT_dve"])
                    gate_up(i, 0, ov["silu"], ov["hact"])
            total = O[:, 0:D]
            sums = 0

            def final(t):
                dve.wait_ge(std3_ready, t + 1)
                dve.reciprocal(rs3[:, t:t + 1], rs3[:, t:t + 1]).then_inc(rs3_ready, 1)
                dve.wait_ge(rs3_ready, t + 1)
                dve.scalar_tensor_tensor(out=x_sb[:, t, :], in0=x_sb[:, t, :], scalar=rs3[:, t:t + 1], in1=fng[:, :],
                                         op0=ALU.mult, op1=ALU.mult).then_inc(fin_ready, 1)

            dve.wait_ge(g_in, 32)
            for t in range(TT):
                rows_k = wring[:, (t % 2) * 8 * D:(t % 2 + 1) * 8 * D].rearrange("p (k d) -> p d k", k=TOP_K)
                dve.wait_ge(y_in[t % 2], 16 * (t // 2 + 1))
                if t:
                    dve.wait_ge(x3_ready, t)
                dve.tensor_reduce(total, rows_k, AX_X, ALU.add).then_inc(summed, 1)
                dve.wait_ge(summed, t + 1)
                sums += 2
                dve.tensor_tensor(total, total, shared[:, t, :], ALU.add).then_inc(sum_step, 1)
                dve.wait_ge(sum_step, sums - 1)
                dve.tensor_tensor(total, total, gate_b[:, :], ALU.mult).then_inc(sum_step, 1)
                dve.wait_ge(sum_step, sums)
                dve.tensor_tensor(x_sb[:, t, :], x_sb[:, t, :], total, ALU.add).then_inc(x3_ready, 1)
                if t:
                    final(t - 1)
            final(TT - 1)

        @block.tensor
        def _(pe):
            def weights(kind, u):
                n = unit_no[kind, u]
                pe.wait_ge(landed[n % RING], 16 * (n // RING + 1))
                return n % RING

            pe.wait_ge(rows_in, 16 * 7)
            pe.wait_ge(consts, 1)
            pe.transpose(bank(O_BANK)[:, 0:ROWS], rows[0:ROWS, :], ident[0:ROWS, 0:ROWS]).then_inc(rows_T, 1)

            def turn(t, g0):
                for half in range(2):
                    g = g0 + 2 * t + half
                    pe.wait_ge(xn_ready, g0 // 2 + t + 1)
                    if g >= 2:
                        pe.wait_ge(xT_free, g - 1)
                    for k in range(4):
                        mm = pe.transpose(bank(2 + g % 2)[:, k * P:(k + 1) * P],
                                          xg[:, t % 2, (4 * half + k) * P:(4 * half + k + 1) * P], ident[:, :])
                    mm.then_inc(xT_done, 1)

            for t in range(TT):
                turn(t, 0)

            def ada(u):
                n = tile_no["ada", u]
                s = weights("ada", u)
                w = as_k(s, KD)
                freed(pe, n)
                for c in range(2):
                    for k in range(KD):
                        mm = pe.matmul(bank(n % 2)[:, c:c + 1], w[:, k, c * P:(c + 1) * P], cact[:, k:k + 1],
                                       start=(k == 0), stop=(k == KD - 1))
                mm.then_inc(tile_done, 1)
                pe.wait_ge(tile_done, n + 1)
                pe.sem_inc(w_used, 1)

            pe.wait_ge(cact_ready, 1)
            for u in range(8):
                ada(u)

            def dense(n, w, c, rhs, ks, last):
                freed(pe, n)
                for k in range(ks):
                    mm = pe.matmul(bank(n % 2), w[:, k, c * P:(c + 1) * P], rhs(k), start=(k == 0), stop=(k == ks - 1))
                mm.then_inc(tile_done, 1)
                if last:
                    pe.wait_ge(tile_done, n + 1)
                    pe.sem_inc(w_used, 1)

            def h_tile(kind, j, unit, c, last):
                s = weights(*unit)
                dense(tile_no[kind, j], as_k(s, KD), c, lambda k: hT[:, k, :], KD, last)

            pe.wait_ge(h_ready, KD)
            for u in range(9):
                if u in (4, 5, 8):
                    s = weights("in", u)
                    w = as_k(s, KD)
                    for half in range(2 if u < 8 else 1):
                        j = 2 * (u - 4) + half if u < 8 else 4
                        if u == 8:
                            h_tile("qk", 12, ("in", 8), 0, False)
                        n = tile_no["v", j]
                        freed(pe, n)
                        tts = (2 * half, 2 * half + 1) if u < 8 else range(TT)
                        c0, cw = (0, 256) if u < 8 else (128, 128)
                        for m, t in enumerate(tts):
                            for k in range(KD):
                                mm = pe.matmul(bank(n % 2)[:, m * cw:(m + 1) * cw], hT[:, k, t * P:(t + 1) * P],
                                               w[:, k, c0:c0 + cw], start=(k == 0), stop=(k == KD - 1))
                        mm.then_inc(tile_done, 1)
                    pe.wait_ge(tile_done, n + 1)
                    pe.sem_inc(w_used, 1)
                else:
                    j0 = 2 * u if u < 4 else 2 * u - 4
                    h_tile("qk", j0, ("in", u), 0, False)
                    h_tile("qk", j0 + 1, ("in", u), 1, True)

            def scores_of(u):
                kind, h, i = att[u]
                sc = bank(2 + 2 * (u % 2), 2)
                if u >= 2:
                    pe.wait_ge(exp_done, u - 1)
                if kind == "da":
                    for m in range(2):
                        a = slice(64 * m, 64 * m + 64)
                        mm = pe.matmul(sc[:, m * S:m * S + (i + 1) * P], qk[a, h, i * P:(i + 1) * P],
                                       qk[a, 4 + h, 0:(i + 1) * P], start=True, stop=True)
                else:
                    k0, w = max(i - 1, 0) * P, min(i + 1, 2) * P
                    for r in range(4):
                        n = 4 * h + r
                        a = slice(64 * (n % 2), 64 * (n % 2) + 64)
                        keys = qk[a, 12, :] if n % 2 == h else kdup[a]
                        c0 = r % 2 * S + r // 2 * 256
                        mm = pe.matmul(sc[:, c0:c0 + w], qk[a, 8 + n // 2, i * P:(i + 1) * P],
                                       keys[:, k0:k0 + w], start=True, stop=True)
                mm.then_inc(s_done, 1)

            def values_of(u):
                kind, h, i = att[u]
                if kind == "da":
                    pe.wait_ge(p_ready, u + 1)
                else:
                    pe.wait_ge(exp_done, u + 1)
                nb = i + 1 if kind == "da" else min(i + 1, 2)
                for half in range(1 if kind == "da" else 2):
                    n = t_steps[u] + half
                    if n:
                        pe.wait_ge(pT_ready, n)
                    blocks = ([(0, b) for b in range(nb)] if kind == "da"
                              else [(256 * (2 * half + r), b) for r in range(2) for b in range(nb)])
                    for m, (c0, b) in enumerate(blocks):
                        mm = pe.transpose(bank(T_BANK)[:, m * P:(m + 1) * P],
                                          probs[:, u % 2, c0 + b * P:c0 + (b + 1) * P], ident[:, :])
                    mm.then_inc(pT_done, 1)
                    pe.wait_ge(pT_ready, n + 1)
                    if half == 0 and u:
                        pe.wait_ge(o_ready, u)
                    if kind == "da":
                        for b in range(nb):
                            mm = pe.matmul(bank(O_BANK)[:, 0:P], pT[:, n % 2, b * P:(b + 1) * P],
                                           v_sb[:, b, h * P:(h + 1) * P], start=(b == 0), stop=(b == nb - 1))
                    else:
                        k0 = max(i - 1, 0)
                        for r in range(2):
                            o0 = (2 * half + r) * HD
                            for b in range(nb):
                                m = r * nb + b
                                mm = pe.matmul(bank(O_BANK)[:, o0:o0 + HD], pT[:, n % 2, m * P:(m + 1) * P],
                                               v_sb[:, k0 + b, 512 + HD * h:512 + HD * h + HD],
                                               start=(b == 0), stop=(b == nb - 1))
                    mm.then_inc(pv_done, 1)

            pe.wait_ge(roped, 13)
            pe.wait_ge(kdup_ready, 1)
            v_count = sum(1 for t in tiles[:tile_no["v", 4] + 1] if t[2] == "D")
            pe.wait_ge(free_d, v_count)
            scores_of(0)
            for u in range(NU):
                if u + 1 < NU:
                    scores_of(u + 1)
                for kind, j in fill_of(u):
                    if kind == "ada":
                        ada(j)
                    else:
                        h_tile("gate", j, ("gate", j // 2), j % 2, j % 2 == 1)
                values_of(u)

            pe.wait_ge(o_ready, NU)
            for n in range(8):
                if n == 4:
                    pe.wait_ge(da_scaled, 1)
                if n >= 4:
                    pe.wait_ge(yT_ready, n - 3)
                src = O[:, 4 * S:8 * S] if n < 4 else O[:, 0:4 * S]
                for t in range(TT):
                    c = t * S + (n % 4) * P
                    mm = pe.transpose(bank(2 + n % 4)[:, t * P:(t + 1) * P], src[:, c:c + P], ident[:, :])
                mm.then_inc(yT_done, 1)
            pe.wait_ge(yT_ready, 8)
            for m in range(8):
                for b, kind in enumerate(("branch_a", "branch_b")):
                    s = weights(kind, m // 4)
                    dense(tile_no["branch", 2 * m + b], as_k(s, 4), m % 4, lambda k, b=b: yT[:, 4 * b + k, :], 4, m % 4 == 3)

            w_out = [as_k(weights("out", u), 2) for u in range(4)]
            pe.wait_ge(merged, 8)
            for t in range(TT):
                for half in range(2):
                    n = tile_no["out", 2 * t + half]
                    freed(pe, n)
                    for k in range(KD):
                        mm = pe.matmul(bank(n % 2), gates[:, k, t * P:(t + 1) * P],
                                       w_out[k // 2][:, k % 2, half * S:(half + 1) * S], start=(k == 0), stop=(k == KD - 1))
                    mm.then_inc(tile_done, 1)
                if t == TT - 1:
                    pe.wait_ge(tile_done, n + 1)
                    pe.sem_inc(w_used, 4)
                if t:
                    turn(t - 1, 2 * TT)
            turn(TT - 1, 2 * TT)

            pe.wait_ge(h_ready, 2 * KD)
            pe.wait_ge(late_in, 48)
            n = tile_no["router", 0]
            freed(pe, n)
            for t in range(TT):
                for k in range(KD):
                    mm = pe.matmul(bank(n % 2)[:, t * N_EXP:(t + 1) * N_EXP], hT[:, k, t * P:(t + 1) * P], wr[:, k, :],
                                   start=(k == 0), stop=(k == KD - 1))
            mm.then_inc(tile_done, 1)
            h_tile("sh_gate", 0, ("sh_gate", 0), 0, False)
            h_tile("sh_up", 0, ("sh_up", 0), 0, False)
            n = tile_no["rank", 0]
            freed(pe, n)
            pe.wait_ge(chosen_ready, 1)
            for t in range(TT + 1):
                parts = [(ones, q) for q in range(min(t, TT))] + ([(upper, t)] if t < TT else [])
                for m, (lhs, q) in enumerate(parts):
                    mm = pe.matmul(bank(n % 2)[:, t * N_EXP:(t + 1) * N_EXP], lhs[:, :], te(chosen)[:, q, :],
                                   start=(m == 0), stop=(m == len(parts) - 1))
            mm.then_inc(tile_done, 1)
            h_tile("sh_gate", 1, ("sh_gate", 0), 1, True)
            h_tile("sh_up", 1, ("sh_up", 0), 1, True)

            def slot_tokens(e, b, done):
                for t in range(TT):
                    mm = pe.matmul(bank(IDX_BANK)[:, 0:3], onehot[:, b, t, :],
                                   Z[:, t, bass.ds(e, 1), :].rearrange("p a c -> p (a c)"), start=(t == 0), stop=(t == TT - 1))
                mm.then_inc(done, 1)

            def tokens(e, b):
                pe.wait_ge(oh_ready, e + 1)
                past(pe, idx_ready, e)
                slot_tokens(e, b, idx_done)

            for e in range(3):
                tokens(e, e % 2)
            s = weights("sh_down", 0)
            w = as_k(s, KF)
            pe.wait_ge(hs_ready, 2)
            for t in range(TT):
                for half in range(2):
                    n = tile_no["sh_down", 2 * t + half]
                    freed(pe, n)
                    for k in range(KF):
                        mm = pe.matmul(bank(n % 2), hsT[:, k, t * P:(t + 1) * P], w[:, k, half * S:(half + 1) * S],
                                       start=(k == 0), stop=(k == KF - 1))
                    mm.then_inc(tile_done, 1)
            pe.wait_ge(tile_done, n + 1)
            pe.sem_inc(w_used, 1)

            def turn_tokens(b, done):
                for k in range(KD):
                    mm = pe.transpose(bank(4, 2)[:, k * P:(k + 1) * P], xg[:, b, k * P:(k + 1) * P], ident[:, :])
                mm.then_inc(done, 1)

            def gate_up(b, gate, up, done):
                for c, w in enumerate((gate, up)):
                    for m in range(KF):
                        o = (KF * c + m) * SLOTS
                        for k in range(KD):
                            mm = pe.matmul(bank(2 + b)[:, o:o + SLOTS], w[:, k, m * P:(m + 1) * P], xgT[:, b, k, :],
                                           start=(k == 0), stop=(k == KD - 1))
                mm.then_inc(done, 1)

            def down(b, w, done):
                for half in range(2):
                    for k in range(KF):
                        mm = pe.matmul(bank(half), hact[:, b, k, :], w[:, k, half * S:(half + 1) * S],
                                       start=(k == 0), stop=(k == KF - 1))
                mm.then_inc(done, 1)

            dense_uses = [sum(1 for n in range(len(units)) if n % RING == s) if s < RING else 0 for s in range(12)]

            def arrived(i, s):
                pe.wait_ge(landed[s], 16 * (i + 1 + dense_uses[s]))

            def turn_expert(e, i, j):
                pe.wait_ge(gathered[j % 2], 16 * (UNROLL // 2 * i + j // 2 + 1))
                past(pe, xgT_dve, e)
                past(pe, xgT_act, e)
                turn_tokens(j % 2, xgT_done)

            def gate_up_expert(e, i, j):
                pe.wait_ge(xgT_dve, e + 1)
                pe.wait_ge(xgT_act, e + 1)
                arrived(i, 3 * j)
                arrived(i, 3 * j + 1)
                gate_up(j % 2, as_k(3 * j, KD), as_k(3 * j + 1, KD), gu_done)

            def pe_pass(i, last=False):
                for j in range(UNROLL):
                    e = UNROLL * i + j
                    if not last or j + 3 < UNROLL:
                        tokens(e + 3, (j + 3) % 2)
                    if not last or j + 1 < UNROLL:
                        past(pe, hact_ready, e)
                        gate_up_expert(e + 1, i + (j + 1) // UNROLL, (j + 1) % UNROLL)
                    if not last or j + 2 < UNROLL:
                        turn_expert(e + 2, i + (j + 2) // UNROLL, (j + 2) % UNROLL)
                    pe.wait_ge(hact_ready, e + 1)
                    past(pe, y_ready, e)
                    arrived(i, 3 * j + 2)
                    down(j % 2, as_k(3 * j + 2, KF), dn_done)

            pe.wait_ge(free_a, sum(1 for t in tiles if t[2] == "A"))
            turn_expert(0, 0, 0)
            turn_expert(1, 0, 1)
            gate_up_expert(0, 0, 0)
            pe_pass(0)
            with pe.Fori(1, N_EXP // UNROLL - 1) as i:
                pe_pass(i)
            pe_pass(N_EXP // UNROLL - 1, True)

            pe.sem_inc(ov["dn"], 1)
            n_over = pe.value_load(over_i[0:1, 32:33], min_val=0, max_val=MAX_OVER)
            pe.wait_ge(y_ready, N_EXP)
            with pe.Fori(0, MAX_OVER) as i:
                with pe.If(i < n_over):
                    e = pe.value_load(over_i[0:1, bass.ds(i, 1)], min_val=0, max_val=N_EXP - 1)
                    pe.wait_ge(ov["oh"], i + 1)
                    slot_tokens(e, 0, ov["idxT"])
                    pe.wait_ge(ov["gathered"], 16 * (i + 1))
                    turn_tokens(0, ov["xgT"])
                    pe.wait_ge(ov["xgT_dve"], i + 1)
                    pe.wait_ge(ov["xgT_act"], i + 1)
                    pe.wait_ge(ov_landed[0], 16 * (i + 1))
                    pe.wait_ge(ov_landed[1], 16 * (i + 1))
                    gate_up(0, as_k(0, KD), as_k(1, KD), ov["gu"])
                    pe.wait_ge(ov["hact"], i + 1)
                    pe.wait_ge(ov["y"], i + 1)
                    pe.wait_ge(ov_landed[2], 16 * (i + 1))
                    down(0, as_k(2, KF), ov["dn"])


_INS = ["x", "c", "positions", "norm1_g", "norm2_g", "w_ada", "b_ada", "w_in", "b_in", "da_lambda", "da_norm_g",
        "sw_sinks", "w_branch_a", "w_branch_b", "w_gate", "b_gate", "w_out", "w_router", "router_bias",
        "w_exp_gate", "w_exp_up", "w_exp_down", "w_sh_gate", "w_sh_up", "w_sh_down", "final_norm_g"]
_WHOLE = ("c", "positions", "final_norm_g")


def kernel(**inputs):
    import numpy as _np
    import concourse.bacc as _bacc
    from concourse import mybir as _mybir
    from concourse.bass_utils import run_bass_kernel_spmd as _run

    nc = _bacc.Bacc("TRN2", target_bir_lowering=False, num_devices=1)
    arrays, args = {}, []

    def give(name, a):
        arrays[f"in_{name}_dram"] = a
        args.append(nc.dram_tensor(f"in_{name}_dram", a.shape, _mybir.dt.from_np(a.dtype), kind="ExternalInput").ap())

    for name in _INS:
        a = _np.ascontiguousarray(inputs[name])
        give(name, a if name in _WHOLE else a[0])
    freq = 1.0 / (10000.0 ** (_np.arange(0, HD, 2) / HD))
    give("inv_freq", _np.tile(freq, 4).astype(_np.float32).reshape(P, 1))
    args.append(nc.dram_tensor("out_0_dram", (S, D), _mybir.dt.float32, kind="ExternalOutput").ap())
    build(nc, *args)
    r = _run(nc, [arrays], core_ids=[0])
    return r.results[0]["out_0_dram"].reshape(1, S, D)
```

```python
import math
from contextlib import ExitStack

import concourse.bass as bass
from concourse import mybir

ALU = mybir.AluOpType
ACT = mybir.ActivationFunctionType
F32 = mybir.dt.float32
F32R = mybir.dt.float32r
I32 = mybir.dt.int32
AX_X = mybir.AxisListType.X

P = 128
D = 1024
S = 512
KD = D // P
TT = S // P
HD = 64
CHUNK = 64
DA_HEADS = 4
SW_HEADS = 8
SW_KV = 2
N_EXP = 64
N_GRP = 8
TOP_K = 8
TOP_G = 4
FF = 256
KF = FF // P
SLOTS = 128
MAX_OVER = 31
ROUTED_SCALE = 2.5
EPS = 1e-6
LAMBDA_INIT = 0.8 - 0.6 * math.exp(-0.3 * 0)
SCALE = HD ** -0.5
MASKED = -1e30
SKIP = 1e6

TWO_PI_A = 6.28125
TWO_PI_B = round((2 * math.pi - TWO_PI_A) * 2 ** 20) / 2 ** 20
TWO_PI_C = 2 * math.pi - TWO_PI_A - TWO_PI_B
ROUND = 1.5 * 2 ** 23
PI_IN = 3.1415925

ROW_C, ROW_ADA, ROW_N1, ROW_N2, ROW_BIN, ROW_BG, ROW_DAG, ROWS = 0, 8, 56, 64, 72, 90, 106, 107

RING = 6
UNIT = 2048
PE_ROWS = 3
UNROLL = 8
DEPTH = 4
AHEAD = 5


def weight_units():
    units = [("ada", u, u % RING, None) for u in range(8)]
    pair = lambda p: (2 * p, 2 * p + 1)
    units += [("in", u) + pair((u + 1) % 3) for u in range(9)]
    for j in range(8):
        units += [("gate", j) + pair(1 + j % 2), ("ada", 8 + 2 * j, 0, None), ("ada", 9 + 2 * j, 1, None)]
    units += [("branch_a", 0) + pair(1), ("branch_b", 0) + pair(0), ("branch_a", 1) + pair(3), ("branch_b", 1) + pair(4)]
    units += [("out", 0) + pair(5), ("out", 1) + pair(2), ("out", 2) + pair(1), ("out", 3) + pair(0)]
    return units


def attention_units():
    return ([("da", h, i) for h in range(DA_HEADS) for i in range(TT)]
            + [("sw", g, i) for g in range(SW_KV) for i in range(TT)])


def filler(n):
    gate = ("gate", n // 2, n % 2)
    ada = ("ada", 8 + n // 2, 0)
    return {0: [gate], 1: [gate, ada], 2: [ada, gate], 3: [gate]}[n % 4]


def gate_tiles():
    return [(kind, j) for n in range(32) for kind, j, half in filler(n) if kind == "ada" or half == 0]


def psum_tiles():
    tiles = [("ada", u, "D") for u in range(8)]
    tiles += [("qk", j, "A") for j in range(8)]
    tiles += [("v", j, "D") for j in range(4)]
    tiles += [("qk", j, "A") for j in range(8, 13)]
    tiles += [("v", 4, "D"), ("v", 5, "D")]
    tiles += [(k, u, "A" if k == "gate" else "D") for k, u in gate_tiles()]
    tiles += [("branch", j, "D") for j in range(16)]
    tiles += [("out", j, "D") for j in range(2 * TT)]
    tiles += [("sh_gate", 0, "A"), ("sh_up", 0, "D"), ("rank", 0, "D"), ("sh_gate", 1, "A"), ("sh_up", 1, "D")]
    return tiles


def build(nc, x_d, c_d, pos_d, n1_d, n2_d, w_ada_d, b_ada_d, w_in_d, b_in_d, lam_d, dag_d, sinks_d,
          w_ba_d, w_bb_d, w_gate_d, b_gate_d, w_out_d, w_router_d, r_bias_d, w_eg_d, w_eu_d, w_ed_d,
          w_sg_d, w_su_d, w_sd_d, fng_d, inv_freq_d, out_d):
    units = weight_units()
    unit_no = {(kind, u): n for n, (kind, u, _, _) in enumerate(units)}
    products = [n for n, u in enumerate(units) if u[0] != "ada"]

    def fills(n, s):
        return sum(1 for u in units[:n + 1] if u[2] == s)

    tiles = psum_tiles()
    tile_no = {(k, i): n for n, (k, i, _) in enumerate(tiles)}
    att = attention_units()
    NU = len(att)

    t_steps = []
    n_steps = 0
    for kind, _, _ in att:
        t_steps.append(n_steps)
        n_steps += 1 if kind == "da" else 2

    assert n_steps == 32

    def steps_of(u):
        return range(t_steps[u], t_steps[u] + (1 if att[u][0] == "da" else 2)) if u < NU else ()

    xn2_d = nc.dram_tensor("xn2_scratch", (S, D), F32, kind="Internal").ap()
    y_d = nc.dram_tensor("expert_rows", (S * TOP_K, D), F32, kind="Internal").ap()

    with ExitStack() as ctx:
        def sb(name, cols, dt=F32):
            return ctx.enter_context(nc.sbuf_tensor(name, [P, cols], dt))

        def sem(name):
            return ctx.enter_context(nc.semaphore(name))

        def same_space(*names_cols):
            with ExitStack() as inner:
                return [inner.enter_context(nc.sbuf_tensor(name, [P, c], F32R)) for name, c in names_cols]

        def by_k(a):
            return a[:, :].rearrange("p (k s) -> p k s", k=KD)

        split = same_space(*[(f"w_{'hi' if s % 2 else 'lo'}{s // 2}", UNIT) for s in range(12)])
        wring = sb("wring", 12 * UNIT)
        h_hi, = map(by_k, same_space(("h_hi", KD * S)))
        x_sb = sb("x_sb", TT * D)[:, :].rearrange("p (t d) -> p t d", t=TT)
        h_lo, = map(by_k, same_space(("h_lo", KD * S)))
        hT = sb("hT", KD * S)[:, :].rearrange("p (k s) -> p k s", k=KD)
        m_lo, m_hi = map(by_k, same_space(("m_lo", KD * S), ("m_hi", KD * S)))
        G = sb("G", 16 * S)
        O = sb("O", 8 * S)
        xg = sb("xg", 2 * D)[:, :].rearrange("p (b d) -> p b d", b=2)
        gate_b = sb("gate_b", D)
        gate2_b = sb("gate2_b", D)
        fng = gate_b
        bias_v = sb("bias_v", 640)
        wr = sb("wr", KD * N_EXP)[:, :].rearrange("p (k e) -> p k e", k=KD)
        hsT = [bias_v[:, 0:S], wr.rearrange("p k e -> p (k e)")]
        hact = sb("hact", 2 * KF * SLOTS)[:, :].rearrange("p (b k s) -> p b k s", b=2, k=KF)
        ident = sb("ident", P)
        rows = sb("rows", P)
        cols = sb("cols", ROWS)
        mod = sb("mod", 48)
        small = sb("small", 160)

        def slot(s):
            return wring[:, s * UNIT:(s + 1) * UNIT]

        late = wring[:, RING * UNIT:12 * UNIT]
        qk = late[:, 0:13 * S].rearrange("p (j s) -> p j s", j=13)
        y_hi, y_lo = h_hi, h_lo
        v_sb = late[:, 13 * S:13 * S + TT * 640].rearrange("p (t c) -> p t c", t=TT)
        probs = late[:, 18 * S:22 * S].rearrange("p (b c) -> p b c", b=2)
        pT = late[:, 22 * S:24 * S].rearrange("p (b c) -> p b c", b=2)

        gates = G[:, :].rearrange("p (j s) -> p j s", j=16)
        cos_t, sin_t = gates[:, 12, :], gates[:, 13, :]
        swapped = gates[:, 14:16, :]
        ang, rnd = gates[:, 8, :], gates[:, 9, :]
        pos_i, ang_abs = gates[:, 10, :].bitcast(I32), gates[:, 11, :]
        square = G[:, 0:D]
        x_exp = G[:, 0:DEPTH * D].rearrange("p (b d) -> p b d", b=DEPTH)
        xgT = G[:, TT * D:TT * D + 2 * D].rearrange("p (b k s) -> p b k s", b=2, k=KD)
        y_sb = G[:, TT * D + 2 * D:TT * D + 4 * D].rearrange("p (b d) -> p b d", b=2)
        y_bufs = [y_sb[:, 0, :], y_sb[:, 1, :], xg[:, 0, :], xg[:, 1, :]]

        kdup = xg[:, 0, 0:S]
        o_da = O[:, 0:4 * S].rearrange("p (i h v) -> p i h v", i=TT, h=DA_HEADS)
        o_sw = O[:, 4 * S:8 * S].rearrange("p (i h v) -> p i h v", i=TT, h=SW_HEADS)
        mixed = O[:, 0:2 * S].rearrange("p (b s) -> p b s", b=2)
        junk2 = O[:, 2 * S:4 * S]
        sg = O[:, 2 * S:3 * S]
        which = O[:, 2 * S:6 * S].rearrange("p (i e) -> p i e", i=32)
        TE = TT * N_EXP

        def rt(n, width=TE):
            return O[:, 4 * S + n * TE:4 * S + n * TE + width]

        def te(a):
            return a.rearrange("p (t e) -> p t e", t=TT)

        scores, choice, masked, replaced = rt(0), rt(1), rt(2), rt(3)
        chosen, cum, rank_m = rt(4), rt(5), rt(6)
        logits_T = rt(4, 2 * TE)
        top8 = O[:, 0:TE]
        Z = O[:, TE:4 * TE].rearrange("p (t e c) -> p t e c", t=TT, c=3)
        onehot = sb("onehot", 2 * TT * SLOTS)[:, :].rearrange("p (b t s) -> p b t s", b=2, t=TT)
        accs = onehot.rearrange("p b t s -> p (b t s)").rearrange("p (b a c) -> p b a c", b=2, a=2)
        iota_s = sb("iota_s", SLOTS)
        upper = sb("upper", P)
        ones = sb("ones", P)
        tri8 = sb("tri8", 64)
        rbias = sb("rbias", N_EXP)
        idx_i = ctx.enter_context(nc.sbuf_tensor("idx_i", [P, 2 * UNROLL], I32))
        idx_w = sb("idx_w", UNROLL)
        idx_f = sb("idx_f", 2 * 3)
        over_i = ctx.enter_context(nc.sbuf_tensor("over_i", [P, 40], I32))
        over_f = sb("over_f", 3 * 32)
        att_s = sb("att_s", 2 * 24)
        lam = gates[:, 7, 0:256]

        at = [0]

        def col(n):
            at[0] += n
            return small[:, at[0] - n:at[0]]

        cact, a1, a2 = col(8), col(8), col(8)
        eps, half_pi, sign, invf = col(1), col(1), col(1), col(1)
        ss1, rs1, ss2, rs2, ss3, rs3 = col(4), col(4), col(4), col(4), col(4), col(4)
        ssq, rsq = col(16), col(16)
        lam_s, lam_e, neglam = col(2), col(2), col(1)
        sinks = col(8)
        tok1, dest1 = col(4), col(4)
        denom, rden = col(4), col(4)
        dag = col(1)

        psum = ctx.enter_context(nc.psum_tensor("psum", [P, 8 * 512], F32))

        def bank(b, n=1):
            return psum[:, b * 512:(b + n) * 512]

        T_BANK, O_BANK, IDX_BANK = 6, 7, 6

        kdup_ready = sem("kdup_ready")
        x_in = [sem(f"x_in{t}") for t in range(TT)]
        rows_in, pos_in, misc_in, late_in = sem("rows_in"), sem("pos_in"), sem("misc_in"), sem("late_in")
        acc_ready = sem("acc_ready")
        landed = [sem(f"landed{s}") for s in range(12)]
        w_used = sem("w_used")
        consts = sem("consts")
        pool_step, dve_step, act_step = sem("pool_step"), sem("dve_step"), sem("act_step")
        rows_T, cols_ready, cact_ready = sem("rows_T"), sem("cols_ready"), sem("cact_ready")
        ss_ready, std_ready = sem("ss_ready"), sem("std_ready")
        xn_ready, xT_done, xT_free = sem("xn_ready"), sem("xT_done"), sem("xT_free")
        h_ready, h_hi_ready, h_lo_ready = sem("h_ready"), sem("h_hi_ready"), sem("h_lo_ready")
        w_hi_ready, w_lo_ready = sem("w_hi_ready"), sem("w_lo_ready")
        m_hi_ready, m_lo_ready = sem("m_hi_ready"), sem("m_lo_ready")
        h2_dve, h2_act = sem("h2_dve"), sem("h2_act")
        logits_done, logits_ready, logits_turned = sem("logits_done"), sem("logits_ready"), sem("logits_turned")
        scores_ready = sem("scores_ready")
        ang_ready, rope_ready = sem("ang_ready"), sem("rope_ready")
        tile_done, free_a, free_d = sem("tile_done"), sem("free_a"), sem("free_d")
        roped, v_ready, lam_ready, lam_exp = sem("roped"), sem("v_ready"), sem("lam_ready"), sem("lam_exp")
        s_done, max_ready, exp_done, p_ready = sem("s_done"), sem("max_ready"), sem("exp_done"), sem("p_ready")
        pT_done, pT_ready, pv_done, o_ready = sem("pT_done"), sem("pT_ready"), sem("pv_done"), sem("o_ready")
        sq_done, da_std, da_scaled = sem("sq_done"), sem("da_std"), sem("da_scaled")
        yT_done, y_hi_ready, y_lo_ready = sem("yT_done"), sem("y_hi_ready"), sem("y_lo_ready")
        fng_in = sem("fng_in")
        merged_b, merged = sem("merged_b"), sem("merged")
        x2_ready = sem("x2_ready")
        xn2_stored = [sem(f"xn2_stored{t}") for t in range(2)]
        chosen_ready, routed = sem("chosen_ready"), sem("routed")
        sg_ready, hs_ready = sem("sg_ready"), sem("hs_ready")
        oh_ready, idx_done, idx_ready = sem("oh_ready"), sem("idx_done"), sem("idx_ready")
        gathered = [sem(f"gathered{b}") for b in range(DEPTH)]
        xgT_done, xgT_dve, xgT_act = sem("xgT_done"), sem("xgT_dve"), sem("xgT_act")
        gu_done, dn_done = sem("gu_done"), sem("dn_done")
        silu_ready, hact_ready = sem("silu_ready"), sem("hact_ready")
        y_ready = sem("y_ready")
        scattered = [sem(f"scattered{b}") for b in range(DEPTH)]
        over_list, over_done = sem("over_list"), sem("over_done")
        ov_landed = [sem(f"ov_landed{q}") for q in range(6)]
        sd_done, sd_free = sem("sd_done"), sem("sd_free")
        y_in = [sem(f"y_in{b}") for b in range(3)]
        x3_ready, rs3_ready, sum_step = sem("x3_ready"), sem("rs3_ready"), sem("sum_step")
        summed, ss3_ready, std3_ready, fin_ready = sem("summed"), sem("ss3_ready"), sem("std3_ready"), sem("fin_ready")
        out_done = [sem(f"out_done{t}") for t in range(TT)]

        block = ctx.enter_context(nc.Block())

        def freed(eng, n):
            if n >= 2:
                owner = tiles[n - 2][2]
                count = sum(1 for t in tiles[:n - 1] if t[2] == owner)
                eng.wait_ge(free_a if owner == "A" else free_d, count)

        def slot_left(eng, n, s):
            before = [m for m in range(n) if s in units[m][2:]]
            if not before:
                if s >= RING:
                    eng.wait_ge(o_ready, NU)
                return
            m = before[-1]
            if units[m][0] == "ada":
                eng.wait_ge(acc_ready, units[m][1] + 1)
            else:
                eng.wait_ge(w_used, products.index(m) + 1)

        def past(eng, semaphore, n):
            if not isinstance(n, int) or n > 0:
                eng.wait_ge(semaphore, n)

        RINGS = N_EXP // DEPTH
        OVER_PASSES = (MAX_OVER + DEPTH) // DEPTH

        def y_back(t):
            return G[:, :] if t % 3 == 2 else wring[:, (4 + 4 * (t % 3)) * UNIT:(8 + 4 * (t % 3)) * UNIT]

        def expert_unit(src, e):
            return src[bass.ds(e, 1)].rearrange("a (k p) f -> p (a k) f", p=P)

        def as_k(s, k):
            return slot(s).rearrange("p (k f) -> p k f", k=k)

        @block.sync
        def _(sp):
            def param_rows(eng, vecs):
                for dram, r, n in vecs:
                    eng.dma_start(rows[r:r + n, :], dram.rearrange("(k p) -> k p", p=P)).then_inc(rows_in, 16)

            param_rows(sp, [(c_d[0, :], ROW_C, 8), (b_ada_d, ROW_ADA, 48), (n1_d, ROW_N1, 8), (n2_d, ROW_N2, 8),
                            (b_in_d, ROW_BIN, 18), (b_gate_d, ROW_BG, 16), (dag_d, ROW_DAG, 1)])
            for t in range(TT):
                sp.dma_start(x_sb[:, t, :], x_d[t * P:(t + 1) * P, :]).then_inc(x_in[t], 16)
            src = {
                "ada": (w_ada_d, 256), "in": (w_in_d, 256), "gate": (w_gate_d, 256),
                "branch_a": (w_ba_d, 512), "branch_b": (w_bb_d, 512),
            }
            for n, (kind, u, q, _) in enumerate(units):
                slot_left(sp, n, q)
                if kind == "out":
                    dram = w_out_d[u * 2 * P:(u + 1) * 2 * P, :].rearrange("(k p) n -> p k n", p=P)
                else:
                    w, width = src[kind]
                    dram = w[:, u * width:(u + 1) * width].rearrange("(k p) n -> p k n", p=P)
                sp.dma_start(as_k(q, dram.shape[1]), dram).then_inc(landed[q], 16)
            sp.wait_ge(tile_done, tile_no["branch", 15] + 1)
            for t in range(TT):
                sp.dma_start(x_sb[:, t, :], x_d[t * P:(t + 1) * P, :]).then_inc(x_in[t], 16)

            def load_shared(q, w, k):
                sp.dma_start(as_k(q, k), w.rearrange("(k p) n -> p k n", p=P)).then_inc(landed[q], 16)

            def load_gate_up(e, j):
                q = 3 * (j % DEPTH)
                sp.dma_start(as_k(q, KD), expert_unit(w_eg_d, e)).then_inc(landed[q], 16)
                sp.dma_start(as_k(q + 1, KD), expert_unit(w_eu_d, e)).then_inc(landed[q + 1], 16)

            def load_down(e, j):
                q = 3 * (j % DEPTH) + 2
                sp.dma_start(as_k(q, KF), expert_unit(w_ed_d, e)).then_inc(landed[q], 16)

            load_shared(9, w_sg_d, KD)
            load_gate_up(2, 2)
            load_down(2, 2)
            sp.wait_ge(w_used, len(products))
            load_shared(10, w_su_d, KD)
            for j in (0, 1):
                load_gate_up(j, j)
                load_down(j, j)
            sp.wait_ge(tile_done, tile_no["sh_up", 0] + 1)
            load_gate_up(3, 3)
            load_down(3, 3)

            def load_pass(i, js):
                for j in js:
                    e = UNROLL * i + j
                    sp.wait_ge(gu_done, e - DEPTH + 1)
                    load_gate_up(e, j)
                    sp.wait_ge(dn_done, e - DEPTH + 1)
                    load_down(e, j)

            load_pass(0, range(DEPTH, UNROLL))
            with sp.Fori(1, N_EXP // UNROLL) as i:
                load_pass(i, range(UNROLL))
            sp.wait_ge(dn_done, N_EXP - DEPTH + 1)
            for q, (w, k) in enumerate(((w_sg_d, KD), (w_su_d, KD), (w_sd_d, KF))):
                load_shared(q, w, k)
            sp.wait_ge(over_list, 1)
            n_over = sp.value_load(over_i[0:1, 32:33], min_val=0, max_val=MAX_OVER)
            with sp.Fori(0, OVER_PASSES) as ii:
                with sp.If(DEPTH * ii < n_over):
                    for u in range(DEPTH):
                        i = DEPTH * ii + u
                        with sp.If(i < n_over):
                            e = sp.value_load(over_i[0:1, bass.ds(i, 1)], min_val=0, max_val=N_EXP - 1)
                            sp.wait_ge(dn_done, N_EXP - 1 + i)
                            for q, (w, k) in enumerate(((w_eg_d, KD), (w_eu_d, KD), (w_ed_d, KF))):
                                sp.dma_start(as_k(3 + 3 * (u % 2) + q, k),
                                             expert_unit(w, e)).then_inc(ov_landed[3 * (u % 2) + q], 16)
            for b in range(DEPTH):
                sp.wait_ge(scattered[b], 16 * RINGS)
            sp.wait_ge(over_done, 1)
            for t in range(TT):
                if t >= 3:
                    sp.wait_ge(summed, t - 2)
                    sp.wait_ge(sd_done, 2 * t - 4)
                sp.dma_start(y_back(t), y_d[t * P * TOP_K:(t + 1) * P * TOP_K, :].rearrange("(p k) d -> p (k d)", k=TOP_K)
                             ).then_inc(y_in[t % 3], 16)
            for t in range(TT):
                sp.wait_ge(fin_ready, t + 1)
                sp.dma_start(out_d[t * P:(t + 1) * P, :], x_sb[:, t, :]).then_inc(out_done[t], 16)
            for t in range(TT):
                sp.wait_ge(out_done[t], 16)

        @block.gpsimd
        def _(pool):
            steps = 0

            def step(ins):
                nonlocal steps
                steps += 1
                ins.then_inc(pool_step, 1)
                pool.wait_ge(pool_step, steps)

            pool.dma_start(pos_i, pos_d[0, :].partition_broadcast(P)).then_inc(pos_in, 16)
            pool.dma_start(invf, inv_freq_d).then_inc(pos_in, 16)
            pool.dma_start(lam[:, :], lam_d.rearrange("a d -> (a d)").partition_broadcast(P)).then_inc(misc_in, 16)
            pool.dma_start(sinks, sinks_d.partition_broadcast(P)).then_inc(misc_in, 16)
            pool.dma_start(bias_v[:, 0:512], b_in_d[1024:1536].partition_broadcast(P)).then_inc(misc_in, 16)
            pool.dma_start(bias_v[:, 512:640], b_in_d[2176:2304].partition_broadcast(P)).then_inc(misc_in, 16)
            pool.dma_start(rbias[:, :], r_bias_d.partition_broadcast(P)).then_inc(late_in, 16)
            for dst, part in ((gate_b, 2), (gate2_b, 5)):
                pool.dma_start(dst[:, :], b_ada_d[part * D:(part + 1) * D].partition_broadcast(P)).then_inc(late_in, 16)
            pool.dma_start(wr, w_router_d.rearrange("(k p) e -> p k e", p=P)).then_inc(late_in, 16)
            step(pool.memset(ident[:, :], 0.0))
            step(pool.memset(ones[:, :], 1.0))
            step(pool.memset(upper[:, :], 1.0))
            step(pool.memset(tri8[:, :], 1.0))
            step(pool.memset(eps, EPS))
            step(pool.memset(half_pi, math.pi / 2))
            step(pool.memset(sign, 1.0))
            for q in (0, 2):
                step(pool.memset(sign[32 * q:32 * q + 32], -1.0))
            step(pool.iota(iota_s[:, :], pattern=[[1, SLOTS]], base=0, channel_multiplier=0,
                           allow_small_or_imprecise_dtypes=True))
            step(pool.iota(tok1, pattern=[[P, TT]], base=1, channel_multiplier=1,
                           allow_small_or_imprecise_dtypes=True))
            step(pool.iota(dest1, pattern=[[P * TOP_K, TT]], base=1, channel_multiplier=TOP_K,
                           allow_small_or_imprecise_dtypes=True))
            step(pool.affine_select(out=upper[:, :], in_=upper[:, :], compare_op=ALU.is_gt, fill=0.0,
                                    base=0, pattern=[[1, P]], channel_multiplier=-1))
            t8 = tri8[:, :].rearrange("p (g h) -> p g h", g=8)
            step(pool.affine_select(out=t8, in_=t8, compare_op=ALU.is_gt, fill=0.0,
                                    base=0, pattern=[[1, 8], [-1, 8]], channel_multiplier=0))
            pool.affine_select(out=ident[:, :], in_=ident[:, :], compare_op=ALU.not_equal, fill=1.0,
                               base=0, pattern=[[-1, P]], channel_multiplier=1).then_inc(consts, 1)
            def lo_weights(d):
                _, _, q, hi = units[products[d]]
                pool.wait_ge(w_hi_ready, d + 1)
                pool.tensor_tensor(split[q][:, :], slot(q), split[hi][:, :].bitcast(F32), ALU.subtract).then_inc(w_lo_ready, 1)

            n_lo = len(products)
            for d in range(n_lo - 2):
                lo_weights(d)
            for m in range(KD):
                if m in (5, 6):
                    lo_weights(n_lo - 7 + m)
                pool.wait_ge(m_hi_ready, m + 1)
                pool.tensor_tensor(m_lo[:, m, :], gates[:, m, :], m_hi[:, m, :].bitcast(F32), ALU.subtract).then_inc(m_lo_ready, 1)
            for t in range(TT):
                pool.wait_ge(xn_ready, TT + t + 1)
                pool.dma_start(xn2_d[t * P:(t + 1) * P, :], xg[:, t % 2, :]).then_inc(xn2_stored[t % 2], 16)
            pool.wait_ge(x2_ready, TT)
            pool.dma_start(fng[:, :], fng_d.partition_broadcast(P)).then_inc(fng_in, 16)
            for b in range(2):
                pool.wait_ge(xn2_stored[b], 32)

            token_bound, row_bound = pool.alloc_register("token_bound"), pool.alloc_register("row_bound")
            token_last, row_last = pool.alloc_register("token_last"), pool.alloc_register("row_last")
            pool.reg_mov(token_last, S - 2)
            pool.reg_mov(row_last, S * TOP_K - 2)

            def gather(e, j):
                pool.wait_ge(idx_ready, e + 1)
                if not isinstance(e, int) or e >= DEPTH:
                    pool.wait_ge(xgT_done, e - DEPTH + 1)
                pool.reg_add(token_bound, token_last, 1)
                pool.indirect_dma_start(
                    out=x_exp[:, j % DEPTH, :], out_offset=None, in_=xn2_d[:, :],
                    in_offset=bass.IndirectOffsetOnAxis(ap=idx_i[:, 2 * j:2 * j + 1], axis=0),
                    bounds_check=token_bound, oob_is_err=False).then_inc(gathered[j % DEPTH], 16)

            def scatter(e, j):
                pool.wait_ge(y_ready, e + 1)
                pool.reg_add(row_bound, row_last, 1)
                pool.indirect_dma_start(
                    out=y_d[:, :], out_offset=bass.IndirectOffsetOnAxis(ap=idx_i[:, 2 * j + 1:2 * j + 2], axis=0),
                    in_=y_bufs[j % DEPTH], in_offset=None,
                    bounds_check=row_bound, oob_is_err=False).then_inc(scattered[j % DEPTH], 16)

            pool.wait_ge(tile_done, tile_no["out", 2 * TT - 1] + 1)
            for e in range(AHEAD):
                gather(e, e)

            def pool_pass(i):
                for j in range(UNROLL):
                    e = UNROLL * i + j
                    gather(e + AHEAD, (j + AHEAD) % UNROLL)
                    scatter(e, j)

            with pool.Fori(0, N_EXP // UNROLL - 1) as i:
                pool_pass(i)
            pool.wait_ge(over_list, 1)
            n_over = pool.value_load(over_i[0:1, 32:33], min_val=0, max_val=MAX_OVER)
            for j in range(UNROLL):
                e = N_EXP - UNROLL + j
                if j + AHEAD < UNROLL:
                    gather(e + AHEAD, j + AHEAD)
                if j >= UNROLL - 2:
                    i = j - UNROLL + 2
                    with pool.If(i < n_over):
                        gather(N_EXP + i, i)
                scatter(e, j)

            with pool.Fori(0, OVER_PASSES) as ii:
                with pool.If(DEPTH * ii < n_over):
                    for u in range(DEPTH):
                        i = DEPTH * ii + u
                        with pool.If(i < n_over):
                            with pool.If(i + 2 < n_over):
                                gather(N_EXP + 2 + i, (u + 2) % DEPTH)
                            scatter(N_EXP + i, u)
                            pool.wait_ge(scattered[u], 16 * (ii + RINGS + 1))
            pool.sem_inc(over_done, 1)

        @block.scalar
        def _(act):
            for t in range(TT):
                act.wait_ge(x_in[t], 16)
                if t:
                    act.wait_ge(ss_ready, t)
                act.activation(square, x_sb[:, t, :], ACT.Square, accum_out=ss1[:, t:t + 1]).then_inc(ss_ready, 1)
            act.wait_ge(ss_ready, TT)
            act.wait_ge(consts, 1)
            act.activation(rs1, ss1, ACT.Sqrt, bias=eps, scale=1.0 / D).then_inc(std_ready, 1)
            act.wait_ge(cols_ready, 1)
            act.activation(cact, cols[:, ROW_C:ROW_C + 8], ACT.Silu).then_inc(cact_ready, 1)

            def turned(t, g0):
                for g in (g0 + 2 * t, g0 + 2 * t + 1):
                    half = g % 2
                    act.wait_ge(xT_done, g + 1)
                    act.activation(hT[:, 4 * half:4 * half + 4, t * P:(t + 1) * P],
                                   bank(2 + g % 2).rearrange("p (k s) -> p k s", k=4), ACT.Copy).then_inc(xT_free, 1)

            def hi_weights(kind, u):
                n = unit_no[kind, u]
                _, _, q, hi = units[n]
                act.wait_ge(landed[q], 16 * fills(n, q))
                slot_left(act, n, hi)
                act.activation(split[hi][:, :], slot(q), ACT.Copy).then_inc(w_hi_ready, 1)

            for t in range(TT):
                turned(t, 0)
            hi_weights("in", 0)
            hi_weights("in", 1)
            act.wait_ge(ang_ready, 1)
            act.activation(sin_t, ang, ACT.Sin, scale=sign).then_inc(rope_ready, 1)
            act.activation(cos_t, ang_abs, ACT.Sin, bias=half_pi, scale=-1.0).then_inc(rope_ready, 1)
            for k in range(KD):
                act.wait_ge(h_ready, k + 1)
                act.activation(h_hi[:, k, :], hT[:, k, :], ACT.Copy).then_inc(h_hi_ready, 1)
            hi_weights("in", 2)
            act.wait_ge(lam_ready, 1)
            act.activation(lam_e, lam_s, ACT.Exp).then_inc(lam_exp, 1)

            def empty_qk(j):
                n = tile_no["qk", j]
                b = bank(n % 2)
                c0 = ROW_BIN + (j if j < 8 else j + 4)
                act.wait_ge(tile_done, n + 1)
                act.activation(qk[:, j, :], b, ACT.Identity, bias=cols[:, c0:c0 + 1])
                if j >= 2:
                    act.wait_ge(roped, j - 1)
                for q in range(4):
                    r = q ^ 1
                    ins = act.activation(swapped[32 * r:32 * r + 32, j % 2, :], b[32 * q:32 * q + 32],
                                         ACT.Identity, bias=cols[32 * q:32 * q + 32, c0:c0 + 1])
                ins.then_inc(free_a, 1)

            for u in range(9):
                for j in ((12,) if u == 8 else () if u in (4, 5) else (2 * u, 2 * u + 1) if u < 4 else (2 * u - 4, 2 * u - 3)):
                    empty_qk(j)
                if u + 3 < 9:
                    hi_weights("in", u + 3)
                elif u == 6:
                    hi_weights("gate", 0)

            def exps(u):
                kind, h, i = att[u]
                sc = bank(2 + 2 * (u % 2), 2)
                s = att_s[:, 24 * (u % 2):24 * (u % 2) + 24]
                act.wait_ge(max_ready, u + 1)
                if u >= 2:
                    act.wait_ge(pT_done, t_steps[u - 1])
                if kind == "da":
                    w = (i + 1) * P
                    for m in range(2):
                        ins = act.activation(probs[:, u % 2, m * S:m * S + w], sc[:, m * S:m * S + w], ACT.Exp,
                                             bias=s[:, 2 + m:3 + m], scale=SCALE, accum_out=s[:, 4 + m:5 + m])
                else:
                    w = min(i + 1, 2) * P
                    for r in range(4):
                        act.activation(probs[:, u % 2, r * 256:r * 256 + w], sc[:, r * 256:r * 256 + w], ACT.Exp,
                                       bias=s[:, 4 + r:5 + r], scale=SCALE, accum_out=s[:, 8 + r:9 + r])
                    ins = act.activation(s[:, 16:20], s[:, 12:16], ACT.Exp)
                ins.then_inc(exp_done, 1)

            def probs_turned(u, n):
                kind, h, i = att[u]
                nb = (i + 1) if kind == "da" else min(i + 1, 2) * 2
                act.wait_ge(pT_done, n + 1)
                if n >= 2:
                    act.wait_ge(pv_done, n - 1)
                act.activation(pT[:, n % 2, 0:nb * P], bank(T_BANK)[:, 0:nb * P], ACT.Copy).then_inc(pT_ready, 1)

            def gate_tile(j):
                n = tile_no["gate", j]
                act.wait_ge(tile_done, n + 1)
                act.activation(gates[:, j, :], bank(n % 2), ACT.Tanh, scale=0.5,
                               bias=cols[:, ROW_BG + j:ROW_BG + j + 1]).then_inc(free_a, 1)

            def squares(u):
                _, h, i = att[u]
                act.wait_ge(o_ready, u + 1)
                if u:
                    act.wait_ge(sq_done, u)
                act.activation(rows[:, :], o_da[:, i, h, :], ACT.Square,
                               accum_out=ssq[:, i * 4 + h:i * 4 + h + 1]).then_inc(sq_done, 1)

            exps(0)
            exps(1)
            act.wait_ge(roped, 13)
            for u in range(NU):
                for n in steps_of(u):
                    probs_turned(u, n)
                    if n % 2:
                        j = n // 2
                        gate_tile(j)
                        if j % 2 == 0:
                            hi_weights(*(("gate", j // 2 + 1) if j < 14 else ("branch_a", 0)))
                if u + 2 < NU:
                    exps(u + 2)
                if u and att[u - 1][0] == "da":
                    squares(u - 1)
            hi_weights("branch_b", 0)
            act.wait_ge(sq_done, 16)
            act.activation(rsq, ssq, ACT.Sqrt, bias=eps, scale=1.0 / P).then_inc(da_std, 1)
            for n in range(8):
                act.wait_ge(yT_done, n + 1)
                if n < 4:
                    ins = act.activation(y_hi[:, 4 + n, :], bank(2 + n), ACT.Copy)
                else:
                    ins = act.activation(y_hi[:, n - 4, :], bank(n - 2), ACT.Copy, scale=dag)
                ins.then_inc(y_hi_ready, 1)
            for u in (("branch_a", 1), ("branch_b", 1), ("out", 0), ("out", 1)):
                hi_weights(*u)
            for m in range(KD):
                if m in (5, 6):
                    hi_weights("out", m - 3)
                act.wait_ge(merged, m + 1)
                act.activation(m_hi[:, m, :], gates[:, m, :], ACT.Copy).then_inc(m_hi_ready, 1)

            for t in range(TT):
                act.wait_ge(x2_ready, t + 1)
                if t:
                    act.wait_ge(ss_ready, TT + t)
                act.activation(junk2, x_sb[:, t, :], ACT.Square, accum_out=ss2[:, t:t + 1]).then_inc(ss_ready, 1)
                act.wait_ge(ss_ready, TT + t + 1)
                act.activation(rs2[:, t:t + 1], ss2[:, t:t + 1], ACT.Sqrt, bias=eps, scale=1.0 / D).then_inc(std_ready, 1)
                act.wait_ge(xT_done, 2 * TT + 2 * t + 2)
                for k in range(KD // 2, KD):
                    ins = act.activation(hT[:, k, t * P:(t + 1) * P], bank(3)[:, (k - 4) * P:(k - 3) * P], ACT.Identity,
                                         bias=mod[:, 3 * KD + k:3 * KD + k + 1], scale=a2[:, k:k + 1])
                ins.then_inc(h2_act, 1)
                act.wait_ge(logits_done, t + 1)
                act.activation(logits_T[0:N_EXP, t * P:(t + 1) * P], bank(4)[0:N_EXP, t * P:(t + 1) * P],
                               ACT.Copy).then_inc(logits_ready, 1)
            act.wait_ge(logits_turned, 1)
            act.activation(scores, bank(5)[:, 0:TE], ACT.Sigmoid).then_inc(scores_ready, 1)

            def shared_gate(k):
                n = tile_no["sh_gate", k]
                act.wait_ge(tile_done, n + 1)
                act.activation(sg, bank(n % 2), ACT.Silu).then_inc(free_a, 1)

            shared_gate(0)

            def turn_x(e, b):
                act.wait_ge(xgT_done, e + 1)
                for k in range(KD // 2, KD):
                    ins = act.activation(xgT[:, b, k, :], bank(4, 2)[:, k * P:(k + 1) * P], ACT.Identity,
                                         bias=mod[:, 3 * KD + k:3 * KD + k + 1], scale=a2[:, k:k + 1])
                ins.then_inc(xgT_act, 1)

            def silu(e, b):
                act.wait_ge(gu_done, e + 1)
                act.activation(hact[:, b, :, :].rearrange("p k s -> p (k s)"), bank(2 + b)[:, 0:KF * SLOTS],
                               ACT.Silu).then_inc(silu_ready, 1)

            def weigh(e, y, w):
                act.wait_ge(dn_done, e + 1)
                act.activation(y[:, 0:S], bank(0), ACT.Copy, scale=w)
                act.activation(y[:, S:D], bank(1), ACT.Copy, scale=w).then_inc(y_ready, 1)

            def act_pass(i, last=False):
                for j in range(UNROLL):
                    e = UNROLL * i + j
                    if not last or j + 1 < UNROLL:
                        past(act, dn_done, e)
                        silu(e + 1, (j + 1) % 2)
                    if not last or j + 2 < UNROLL:
                        act.wait_ge(gu_done, e + 1)
                        turn_x(e + 2, j % 2)
                    past(act, scattered[j % DEPTH], 16 * (UNROLL // DEPTH * i + j // DEPTH))
                    weigh(e, y_bufs[j % DEPTH], idx_w[:, j:j + 1])

            turn_x(0, 0)
            turn_x(1, 1)
            silu(0, 0)
            act_pass(0)
            with act.Fori(1, N_EXP // UNROLL - 1) as i:
                act_pass(i)
            act_pass(N_EXP // UNROLL - 1, True)

            act.wait_ge(over_list, 1)
            n_over = act.value_load(over_i[0:1, 32:33], min_val=0, max_val=MAX_OVER)
            with act.If(0 < n_over):
                turn_x(N_EXP, 0)
            shared_gate(1)
            with act.Fori(0, OVER_PASSES) as ii:
                with act.If(DEPTH * ii < n_over):
                    for u in range(DEPTH):
                        i = DEPTH * ii + u
                        with act.If(i < n_over):
                            act.wait_ge(dn_done, N_EXP - 1 + i)
                            silu(N_EXP + i, u % 2)
                            with act.If(i + 1 < n_over):
                                act.wait_ge(gu_done, N_EXP + i)
                                turn_x(N_EXP + i + 1, (u + 1) % 2)
                            act.wait_ge(scattered[u], 16 * (ii + RINGS))
                            weigh(N_EXP + i, y_bufs[u], idx_w[:, u:u + 1])

            for t in range(TT):
                act.wait_ge(x3_ready, t + 1)
                if t:
                    act.wait_ge(ss3_ready, t)
                act.activation(junk2, x_sb[:, t, :], ACT.Square, accum_out=ss3[:, t:t + 1]).then_inc(ss3_ready, 1)
                act.wait_ge(ss3_ready, t + 1)
                act.activation(rs3[:, t:t + 1], ss3[:, t:t + 1], ACT.Sqrt, bias=eps, scale=1.0 / D).then_inc(std3_ready, 1)

        @block.vector
        def _(dve):
            steps = [0]

            def step(ins):
                ins.then_inc(dve_step, 1)
                steps[0] = steps[0] + 1

            def settle():
                dve.wait_ge(dve_step, steps[0])

            dve.wait_ge(pos_in, 32)
            step(dve.tensor_copy(ang_abs, pos_i))
            settle()
            step(dve.tensor_scalar(ang, ang_abs, invf, None, ALU.mult))
            settle()
            step(dve.tensor_scalar(rnd, ang, 1.0 / (2 * math.pi), ROUND, ALU.mult, ALU.add))
            settle()
            step(dve.tensor_scalar(rnd, rnd, ROUND, None, ALU.subtract))
            settle()
            for part in (TWO_PI_A, TWO_PI_B, TWO_PI_C):
                step(dve.scalar_tensor_tensor(out=ang, in0=rnd, scalar=-part, in1=ang, op0=ALU.mult, op1=ALU.add))
                settle()
            step(dve.tensor_scalar(ang, ang, PI_IN, -PI_IN, ALU.min, ALU.max))
            settle()
            dve.scalar_tensor_tensor(out=ang_abs, in0=ang, scalar=-1.0, in1=ang, op0=ALU.mult,
                                     op1=ALU.max).then_inc(ang_ready, 1)
            dve.wait_ge(rows_T, 1)
            step(dve.tensor_copy(cols[:, :], bank(O_BANK)[:, 0:ROWS]))
            settle()
            dve.tensor_scalar(dag, cols[:, ROW_DAG:ROWS], 1.0 - LAMBDA_INIT, None, ALU.mult)
            dve.tensor_scalar(cols[:, ROW_BG:ROW_BG + 16], cols[:, ROW_BG:ROW_BG + 16], 0.5, None,
                              ALU.mult).then_inc(cols_ready, 1)

            dve.wait_ge(std_ready, 1)
            step(dve.reciprocal(rs1, rs1))
            settle()

            def normed(t, r):
                dve.tensor_scalar(xg[:, t % 2, :], x_sb[:, t, :], r[:, t:t + 1], None, ALU.mult).then_inc(xn_ready, 1)

            for t in range(TT):
                if t >= 2:
                    dve.wait_ge(xT_done, 2 * t - 2)
                normed(t, rs1)

            def part(n):
                return mod[:, n * KD:(n + 1) * KD]

            def ada_sum(u):
                n = unit_no["ada", u]
                q = units[n][2]
                w = as_k(q, KD)
                dve.wait_ge(landed[q], 16 * fills(n, q))
                if u >= 2:
                    dve.wait_ge(tile_done, tile_no["ada", u - 2] + 1)
                for k in range(KD):
                    acc = accs[:, u % 2, k % 2, :]
                    if k < 2:
                        step(dve.tensor_scalar(acc, w[:, k, :], cact[:, k:k + 1], None, ALU.mult))
                    else:
                        dve.wait_ge(dve_step, steps[0] - 1)
                        step(dve.scalar_tensor_tensor(out=acc, in0=w[:, k, :], scalar=cact[:, k:k + 1], in1=acc,
                                                      op0=ALU.mult, op1=ALU.add))
                settle()
                dve.tensor_tensor(accs[:, u % 2, 0, :], accs[:, u % 2, 0, :], accs[:, u % 2, 1, :],
                                  ALU.add).then_inc(acc_ready, 1)

            def ada_tile(u):
                n = tile_no["ada", u]
                dve.wait_ge(tile_done, n + 1)
                if u // 4 in (2, 5):
                    g = (gate_b if u // 4 == 2 else gate2_b)[:, u % 4 * 256:(u % 4 + 1) * 256]
                    dve.tensor_tensor(g, g, bank(n % 2)[:, 0:256], ALU.add).then_inc(free_d, 1)
                else:
                    dve.tensor_tensor(mod[:, 2 * u:2 * u + 2], bank(n % 2)[:, 0:2],
                                      cols[:, ROW_ADA + 2 * u:ROW_ADA + 2 * u + 2], ALU.add).then_inc(free_d, 1)

            dve.wait_ge(cact_ready, 1)
            for u in range(8):
                ada_sum(u)
                if u:
                    ada_tile(u - 1)
            ada_tile(7)
            dve.wait_ge(free_d, 8)
            step(dve.scalar_tensor_tensor(out=a1, in0=part(1), scalar=1.0, in1=cols[:, ROW_N1:ROW_N1 + 8],
                                          op0=ALU.add, op1=ALU.mult))
            dve.wait_ge(xT_free, 2 * TT)
            settle()
            for k in range(KD + 1):
                if k < KD:
                    dve.tensor_scalar(hT[:, k, :], hT[:, k, :], a1[:, k:k + 1], part(0)[:, k:k + 1],
                                      ALU.mult, ALU.add).then_inc(h_ready, 1)
                if k:
                    dve.wait_ge(h_hi_ready, k)
                    dve.tensor_tensor(h_lo[:, k - 1, :], hT[:, k - 1, :], h_hi[:, k - 1, :].bitcast(F32),
                                      ALU.subtract).then_inc(h_lo_ready, 1)
            dve.wait_ge(misc_in, 16 * 4)
            lv = lam[:, :].rearrange("p (a b d) -> p a b d", a=2, b=2)
            lp = lam[:, 0:2 * HD].rearrange("p (a d) -> p a d", a=2)
            step(dve.tensor_tensor(lp[:, 0, :], lv[:, 0, 0, :], lv[:, 0, 1, :], ALU.mult))
            settle()
            step(dve.tensor_tensor(lp[:, 1, :], lv[:, 1, 0, :], lv[:, 1, 1, :], ALU.mult))
            settle()
            dve.tensor_reduce(lam_s, lp, AX_X, ALU.add).then_inc(lam_ready, 1)
            dve.wait_ge(lam_exp, 1)
            dve.scalar_tensor_tensor(out=neglam, in0=lam_e[:, 1:2], scalar=-LAMBDA_INIT, in1=lam_e[:, 0:1],
                                     op0=ALU.add, op1=ALU.subtract)

            dve.wait_ge(rope_ready, 2)
            for kind, j, _ in [t for t in tiles if t[0] in ("qk", "v")]:
                n = tile_no[kind, j]
                if kind == "qk":
                    count = sum(1 for t in tiles[:n + 1] if t[2] == "A")
                    dve.wait_ge(free_a, count)
                    dve.tensor_tensor(qk[:, j, :], qk[:, j, :], cos_t, ALU.mult)
                    step(dve.tensor_tensor(swapped[:, j % 2, :], swapped[:, j % 2, :], sin_t, ALU.mult))
                    settle()
                    dve.tensor_tensor(qk[:, j, :], qk[:, j, :], swapped[:, j % 2, :], ALU.add).then_inc(roped, 1)
                    continue
                dve.wait_ge(tile_done, n + 1)
                if j < 4:
                    c, t0 = 256 * (j // 2), 2 * (j % 2)
                    dve.tensor_tensor(v_sb[:, t0:t0 + 2, c:c + 256], bank(n % 2).rearrange("p (t c) -> p t c", t=2),
                                      bias_v[:, c:c + 256].unsqueeze(1).broadcast_to([P, 2, 256]),
                                      ALU.add).then_inc(free_d, 1)
                else:
                    t0 = 2 * (j - 4)
                    dve.tensor_tensor(v_sb[:, t0:t0 + 2, 512:640],
                                      bank(n % 2).rearrange("p (t c) -> p t c", t=2)[:, :, 128:256],
                                      bias_v[:, 512:640].unsqueeze(1).broadcast_to([P, 2, P]),
                                      ALU.add).then_inc(free_d, 1)
            dve.wait_ge(roped, 13)
            dve.tensor_copy(kdup[0:64], qk[64:128, 12, :])
            dve.tensor_copy(kdup[64:128], qk[0:64, 12, :]).then_inc(kdup_ready, 1)

            def by_bank(a):
                return a.rearrange("p (a b) -> p b a", b=2)

            def pairs(a):
                return a.rearrange("p (b a) -> p b a", b=2)

            def row_max(u):
                kind, h, i = att[u]
                s = att_s[:, 24 * (u % 2):24 * (u % 2) + 24]
                dve.wait_ge(s_done, u + 1)
                if kind == "da":
                    w = (i + 1) * P
                    sc = bank(2 + 2 * (u % 2), 2).rearrange("p (m c) -> p m c", m=2)
                    step(dve.memset(sc[0:CHUNK, :, w - CHUNK:w], MASKED))
                    settle()
                    step(dve.tensor_reduce(s[:, 0:2], sc[:, :, 0:w], AX_X, ALU.max))
                    settle()
                    dve.tensor_scalar(s[:, 2:4], s[:, 0:2], -SCALE, None, ALU.mult).then_inc(max_ready, 1)
                    return
                w = min(i + 1, 2) * P
                sc = bank(2 + 2 * (u % 2), 2).rearrange("p (m c) -> p m c", m=4)
                step(dve.memset(sc[0:CHUNK, :, w - CHUNK:w], MASKED))
                if i:
                    dve.memset(sc[0:CHUNK, :, 0:CHUNK], MASKED)
                    step(dve.memset(sc[CHUNK:P, :, 0:2 * CHUNK], MASKED))
                settle()
                step(dve.tensor_reduce(s[:, 0:4], sc[:, :, 0:w], AX_X, ALU.max))
                settle()
                sink = by_bank(sinks[:, 4 * h:4 * h + 4])
                step(dve.scalar_tensor_tensor(out=pairs(s[:, 0:4]), in0=pairs(s[:, 0:4]), scalar=SCALE, in1=sink,
                                              op0=ALU.mult, op1=ALU.max))
                settle()
                dve.tensor_scalar(s[:, 4:8], s[:, 0:4], -1.0, None, ALU.mult)
                dve.tensor_tensor(pairs(s[:, 12:16]), sink, pairs(s[:, 0:4]), ALU.subtract).then_inc(max_ready, 1)

            def combine(u):
                kind, h, i = att[u]
                s = att_s[:, 24 * (u % 2):24 * (u % 2) + 24]
                dve.wait_ge(exp_done, u + 1)
                if kind == "da":
                    w = (i + 1) * P
                    p0, p1 = probs[:, u % 2, 0:w], probs[:, u % 2, S:S + w]
                    step(dve.reciprocal(s[:, 6:8], s[:, 4:6]))
                    settle()
                    step(dve.tensor_scalar(p1, p1, s[:, 7:8], neglam, ALU.mult, ALU.mult))
                    settle()
                    dve.scalar_tensor_tensor(out=p0, in0=p0, scalar=s[:, 6:7], in1=p1, op0=ALU.mult,
                                             op1=ALU.add).then_inc(p_ready, 1)
                    return
                dve.wait_ge(o_ready, u - 1)
                step(dve.tensor_tensor(s[:, 20:24], s[:, 8:12], s[:, 16:20], ALU.add))
                settle()
                step(dve.reciprocal(s[:, 20:24], s[:, 20:24]))

            def out_rows(u):
                kind, h, i = att[u]
                s = att_s[:, 24 * (u % 2):24 * (u % 2) + 24]
                dve.wait_ge(pv_done, t_steps[u] + (1 if kind == "da" else 2))
                if kind == "da":
                    dve.tensor_copy(o_da[:, i, h, :], bank(O_BANK)[:, 0:P]).then_inc(o_ready, 1)
                else:
                    settle()
                    dve.tensor_tensor(o_sw[:, i, 4 * h:4 * h + 4, :].rearrange("p (a b) v -> p b a v", b=2),
                                      bank(O_BANK)[:, 0:256].rearrange("p (b a v) -> p b a v", b=2, a=2),
                                      pairs(s[:, 20:24]).unsqueeze(3).broadcast_to([P, 2, 2, HD]),
                                      ALU.mult).then_inc(o_ready, 1)

            def ada_of(u):
                return [j for n in steps_of(u) for kind, j, _ in filler(n) if kind == "ada"]

            dve.wait_ge(late_in, 64)
            row_max(0)
            row_max(1)
            for j in ada_of(0):
                ada_sum(j)
            combine(0)
            for u in range(NU):
                if u + 1 < NU:
                    combine(u + 1)
                if u + 2 < NU:
                    row_max(u + 2)
                for j in ada_of(u + 1):
                    ada_sum(j)
                for j in ada_of(u):
                    ada_tile(j)
                out_rows(u)
            dve.wait_ge(free_d, sum(1 for t in tiles[:tile_no["ada", 23] + 1] if t[2] == "D"))
            dve.tensor_scalar(gate_b[:, :], gate_b[:, :], 0.5, None, ALU.mult)
            dve.scalar_tensor_tensor(out=a2, in0=part(4), scalar=1.0, in1=cols[:, ROW_N2:ROW_N2 + 8],
                                     op0=ALU.add, op1=ALU.mult)

            dve.wait_ge(da_std, 1)
            step(dve.reciprocal(rsq, rsq))
            settle()
            oda = O[:, 0:4 * S].rearrange("p (n v) -> p n v", v=P)
            dve.tensor_tensor(oda, oda, rsq.unsqueeze(2).broadcast_to([P, 16, P]), ALU.mult).then_inc(da_scaled, 1)
            for n in range(8):
                dve.wait_ge(y_hi_ready, n + 1)
                if n < 4:
                    ins = dve.tensor_tensor(y_lo[:, 4 + n, :], bank(2 + n), y_hi[:, 4 + n, :].bitcast(F32), ALU.subtract)
                else:
                    ins = dve.scalar_tensor_tensor(out=y_lo[:, n - 4, :], in0=bank(n - 2), scalar=dag,
                                                   in1=y_hi[:, n - 4, :].bitcast(F32), op0=ALU.mult, op1=ALU.subtract)
                ins.then_inc(y_lo_ready, 1)

            for j in range(16):
                n = tile_no["branch", j]
                m, b = j // 2, j % 2
                dve.wait_ge(tile_done, n + 1)
                dve.scalar_tensor_tensor(out=gates[:, 8 * b + m, :], in0=gates[:, 8 * b + m, :], scalar=1.0,
                                         in1=bank(n % 2), op0=ALU.add, op1=ALU.mult).then_inc(free_d, 1)
                if b:
                    count = sum(1 for t in tiles[:n + 1] if t[2] == "D")
                    dve.wait_ge(free_d, count)
                    dve.tensor_tensor(gates[:, m, :], gates[:, m, :], gates[:, 8 + m, :], ALU.add).then_inc(merged, 1)


            def norm2(t):
                dve.wait_ge(std_ready, 1 + t + 1)
                step(dve.reciprocal(rs2[:, t:t + 1], rs2[:, t:t + 1]))
                settle()
                if t >= 2:
                    dve.wait_ge(xn2_stored[t % 2], 16)
                    dve.wait_ge(xT_done, 2 * TT + 2 * t - 2)
                normed(t, rs2)

            def turned2(t):
                dve.wait_ge(xT_done, 2 * TT + 2 * t + 1)
                for k in range(KD // 2):
                    ins = dve.tensor_scalar(hT[:, k, t * P:(t + 1) * P], bank(2)[:, k * P:(k + 1) * P], a2[:, k:k + 1],
                                            part(3)[:, k:k + 1], ALU.mult, ALU.add)
                ins.then_inc(h2_dve, 1)

            for t in range(TT):
                for half in range(2):
                    n = tile_no["out", 2 * t + half]
                    dve.wait_ge(tile_done, n + 1)
                    step(dve.tensor_tensor(mixed[:, half, :], bank(n % 2), gate_b[:, half * S:(half + 1) * S], ALU.mult))
                    settle()
                    dve.sem_inc(free_d, 1)
                    dve.wait_ge(x_in[t], 32)
                    xs = x_sb[:, t, half * S:(half + 1) * S]
                    ins = dve.tensor_tensor(xs, xs, mixed[:, half, :], ALU.add)
                    step(ins) if half == 0 else ins.then_inc(x2_ready, 1)
                    if t and half == 0:
                        turned2(t - 1)
                norm2(t)
            turned2(TT - 1)

            dve.wait_ge(scores_ready, 1)
            step(dve.tensor_tensor(te(choice), te(scores), rbias[:, :].unsqueeze(1).broadcast_to([P, TT, N_EXP]), ALU.add))
            settle()
            for g in range(TT * N_GRP):
                ins = dve.max(top8[:, 8 * g:8 * g + 8], choice[:, 8 * g:8 * g + 8])
            step(ins)
            settle()
            best = top8.rearrange("p (g k) -> p g k", k=8)
            gsc, grank = over_f[:, 0:32], over_f[:, 32:64]
            step(dve.tensor_tensor(gsc.unsqueeze(2), best[:, :, 0:1], best[:, :, 1:2], ALU.add))
            settle()
            def tgg(a):
                return a.rearrange("p (t g h) -> p t g h", t=TT, g=8)

            rival = gsc.rearrange("p (t h) -> p t h", t=TT).unsqueeze(2).broadcast_to([P, TT, 8, 8])
            own = gsc.rearrange("p (t g) -> p t g", t=TT).unsqueeze(3).broadcast_to([P, TT, 8, 8])
            dve.tensor_tensor(tgg(masked), rival, own, ALU.is_gt)
            step(dve.tensor_tensor(tgg(replaced), rival, own, ALU.is_equal))
            settle()
            step(dve.tensor_tensor(replaced.rearrange("p (t g) -> p t g", t=TT), replaced.rearrange("p (t g) -> p t g", t=TT),
                                   tri8[:, :].unsqueeze(1).broadcast_to([P, TT, 64]), ALU.mult))
            settle()
            step(dve.tensor_tensor(masked, masked, replaced, ALU.add))
            settle()
            step(dve.tensor_reduce(grank, masked.rearrange("p (g h) -> p g h", h=8), AX_X, ALU.add))
            settle()
            step(dve.tensor_scalar(grank, grank, float(TOP_G), None, ALU.is_lt))
            settle()
            kept = grank.unsqueeze(2).broadcast_to([P, TT * N_GRP, 8])
            g8 = lambda a: a.rearrange("p (g k) -> p g k", k=8)
            step(dve.tensor_tensor(g8(masked), g8(choice), kept, ALU.mult))
            step(dve.tensor_scalar(gsc, grank, 1.0, -MASKED, ALU.subtract, ALU.mult))
            settle()
            step(dve.tensor_tensor(g8(masked), g8(masked), gsc.unsqueeze(2).broadcast_to([P, TT * N_GRP, 8]), ALU.add))
            settle()
            for t in range(TT):
                ins = dve.max(top8[:, 8 * t:8 * t + 8], te(masked)[:, t, :])
            step(ins)
            settle()
            for t in range(TT):
                ins = dve.match_replace(te(replaced)[:, t, :], top8[:, 8 * t:8 * t + 8], te(masked)[:, t, :], 2 * MASKED)
            step(ins)
            settle()
            dve.tensor_tensor(chosen, replaced, masked, ALU.not_equal).then_inc(chosen_ready, 1)
            dve.wait_ge(chosen_ready, 1)
            step(dve.tensor_tensor(masked, scores, chosen, ALU.mult))
            for t in range(TT):
                ins = dve.tensor_tensor_scan(te(cum)[:, t, :], ones[:, 0:N_EXP], te(chosen)[:, t, :], 0.0, ALU.mult, ALU.add)
            step(ins)
            settle()
            step(dve.tensor_reduce(denom, te(masked), AX_X, ALU.add))
            step(dve.tensor_tensor(cum, cum, chosen, ALU.subtract))
            settle()
            step(dve.reciprocal(rden, denom))
            step(dve.tensor_copy(Z[:, :, :, 0], tok1.unsqueeze(2).broadcast_to([P, TT, N_EXP])))
            step(dve.tensor_tensor(Z[:, :, :, 1], te(cum), dest1.unsqueeze(2).broadcast_to([P, TT, N_EXP]), ALU.add))
            settle()
            step(dve.scalar_tensor_tensor(out=Z[:, :, :, 2], in0=te(masked), scalar=ROUTED_SCALE,
                                          in1=rden.unsqueeze(2).broadcast_to([P, TT, N_EXP]), op0=ALU.mult, op1=ALU.mult))

            def shared_act(k):
                n = tile_no["sh_up", k]
                dve.wait_ge(tile_done, n + 1)
                m = tile_no["sh_gate", k]
                dve.wait_ge(free_a, sum(1 for t in tiles[:m + 1] if t[2] == "A"))
                dve.tensor_tensor(hsT[k], sg, bank(n % 2), ALU.mult).then_inc(hs_ready, 1)
                dve.wait_ge(hs_ready, k + 1)
                dve.sem_inc(free_d, 1)

            shared_act(0)
            n = tile_no["rank", 0]
            dve.wait_ge(tile_done, n + 1)
            counts, over, cum_o = cum[:, 0:64], cum[:, 64:128], cum[:, 128:192]
            step(dve.scalar_tensor_tensor(out=rank_m, in0=bank(n % 2)[:, 0:TE], scalar=1.0, in1=chosen, op0=ALU.add, op1=ALU.mult))
            step(dve.tensor_copy(counts, bank(n % 2)[:, TE:TE + N_EXP]))
            settle()
            dve.sem_inc(free_d, 1)
            step(dve.tensor_scalar(rank_m, rank_m, 1.0, None, ALU.subtract))
            settle()

            def column(e):
                return te(rank_m)[:, :, bass.ds(e, 1)].broadcast_to([P, TT, SLOTS])

            slots4 = iota_s[:, :].unsqueeze(1).broadcast_to([P, TT, SLOTS])

            def one_hot(e, b):
                if not isinstance(e, int) or e >= 2:
                    dve.wait_ge(idx_done, e - 1)
                dve.tensor_tensor(onehot[:, b, :, :], slots4, column(e), ALU.is_equal).then_inc(oh_ready, 1)

            def indices(e, j):
                v = bank(IDX_BANK)[:, 0:3]
                dve.wait_ge(idx_done, e + 1)
                step(dve.tensor_scalar(idx_f[:, 0:2], v[:, 0:2], 0.0, SKIP, ALU.is_equal, ALU.mult))
                settle()
                dve.tensor_copy(idx_w[:, j:j + 1], v[:, 2:3])
                dve.scalar_tensor_tensor(out=idx_i[:, 2 * j:2 * j + 2], in0=v[:, 0:2], scalar=-1.0, in1=idx_f[:, 0:2],
                                         op0=ALU.add, op1=ALU.add).then_inc(idx_ready, 1)

            one_hot(0, 0)
            for e in range(AHEAD):
                one_hot(e + 1, (e + 1) % 2)
                indices(e, e)

            def turn_x(e, b):
                dve.wait_ge(xgT_done, e + 1)
                for k in range(KD // 2):
                    ins = dve.tensor_scalar(xgT[:, b, k, :], bank(4, 2)[:, k * P:(k + 1) * P], a2[:, k:k + 1],
                                            mod[:, 3 * KD + k:3 * KD + k + 1], ALU.mult, ALU.add)
                ins.then_inc(xgT_dve, 1)

            def gate_up(e, b):
                dve.wait_ge(silu_ready, e + 1)
                h = hact[:, b, :, :].rearrange("p k s -> p (k s)")
                dve.tensor_tensor(h, h, bank(2 + b)[:, KF * SLOTS:2 * KF * SLOTS], ALU.mult).then_inc(hact_ready, 1)

            def overflow_list(part):
                if part == 0:
                    step(dve.tensor_scalar(over, counts, float(SLOTS), None, ALU.is_gt))
                    settle()
                    for m in (2, 3):
                        step(dve.scalar_tensor_tensor(out=over, in0=counts, scalar=float(m * SLOTS), in1=over,
                                                      op0=ALU.is_gt, op1=ALU.add))
                        settle()
                    step(dve.tensor_tensor_scan(cum_o, ones[:, 0:N_EXP], over, 0.0, ALU.mult, ALU.add))
                    settle()
                    step(dve.tensor_copy(over_i[:, 32:33], cum_o[:, N_EXP - 1:N_EXP]))
                elif part == 1:
                    step(dve.tensor_tensor(which, cum_o.unsqueeze(1).broadcast_to([P, 32, N_EXP]),
                                           iota_s[:, 0:32].unsqueeze(2).broadcast_to([P, 32, N_EXP]), ALU.is_le))
                elif part == 2:
                    step(dve.tensor_reduce(over_f[:, 64:96], which, AX_X, ALU.add))
                    settle()
                    step(dve.tensor_copy(over_i[:, 0:32], over_f[:, 64:96]))
                elif part == 3:
                    step(dve.tensor_tensor(which, which, over.unsqueeze(1).broadcast_to([P, 32, N_EXP]), ALU.mult))
                elif part == 4:
                    step(dve.tensor_reduce(over_f[:, 0:32], which, AX_X, ALU.add))
                    settle()
                    step(dve.tensor_tensor(over_f[:, 0:32], iota_s[:, 0:32], over_f[:, 0:32], ALU.subtract))
                    settle()
                    dve.tensor_scalar(over_f[:, 0:32], over_f[:, 0:32], float(SLOTS), float(SLOTS), ALU.mult,
                                      ALU.add).then_inc(over_list, 1)

            def over_one_hot(i, b):
                e = dve.value_load(over_i[0:1, bass.ds(i, 1)], min_val=0, max_val=N_EXP - 1)
                dve.wait_ge(idx_done, N_EXP - 1 + i)
                dve.scalar_tensor_tensor(out=onehot[:, b, :, :], in0=slots4, scalar=over_f[:, bass.ds(i, 1)],
                                         in1=column(e), op0=ALU.add, op1=ALU.is_equal).then_inc(oh_ready, 1)

            def over_indices(i, u, before):
                steps[0] = i + before
                indices(N_EXP + i, u)

            def dve_pass(i, last=False, n_over=None):
                for j in range(UNROLL):
                    e = UNROLL * i + j
                    if last and j >= UNROLL - 3:
                        for m in (0, 1):
                            at_j = j - (UNROLL - 3) - m
                            if at_j in (0, 1):
                                with dve.If(m < n_over):
                                    if at_j == 0:
                                        over_one_hot(m, m)
                                    else:
                                        dve.wait_ge(scattered[m], 16 * (RINGS - 1))
                                        over_indices(m, m, all_steps)
                    if not last or j + AHEAD < UNROLL:
                        q = j + AHEAD - UNROLL
                        past(dve, scattered[q % DEPTH], 16 * (UNROLL // DEPTH * i + q // DEPTH + 1))
                        indices(e + AHEAD, (j + AHEAD) % UNROLL)
                    if not last or j + 1 < UNROLL:
                        gate_up(e + 1, (j + 1) % 2)
                    if not last or j + 2 < UNROLL:
                        dve.wait_ge(gu_done, e + 1)
                        turn_x(e + 2, j % 2)
                    if not last or j + AHEAD + 1 < UNROLL:
                        one_hot(e + AHEAD + 1, (j + AHEAD + 1) % 2)
                    if isinstance(i, int) and i == 0:
                        overflow_list(j)

            turn_x(0, 0)
            turn_x(1, 1)
            gate_up(0, 0)

            passes = N_EXP // UNROLL - 1
            dve_pass(0)
            before = steps[0] - UNROLL
            with dve.Fori(1, passes) as i:
                steps[0] = UNROLL * i + before
                dve_pass(i)
            steps[0] = before + UNROLL * passes
            n_over = dve.value_load(over_i[0:1, 32:33], min_val=0, max_val=MAX_OVER)
            all_steps = before + N_EXP - AHEAD
            dve_pass(passes, True, n_over)
            with dve.If(0 < n_over):
                turn_x(N_EXP, 0)
            shared_act(1)
            with dve.Fori(0, OVER_PASSES) as ii:
                with dve.If(DEPTH * ii < n_over):
                    for u in range(DEPTH):
                        i = DEPTH * ii + u
                        with dve.If(i < n_over):
                            with dve.If(i + 2 < n_over):
                                over_one_hot(i + 2, u % 2)
                                dve.wait_ge(scattered[(u + 2) % DEPTH], 16 * (ii + RINGS + (u + 2) // DEPTH))
                                over_indices(i + 2, (u + 2) % DEPTH, all_steps)
                            gate_up(N_EXP + i, u % 2)
                            with dve.If(i + 1 < n_over):
                                dve.wait_ge(gu_done, N_EXP + i)
                                turn_x(N_EXP + i + 1, (u + 1) % 2)

            total = O[:, 0:D]
            sums = 0

            def final(t):
                dve.wait_ge(std3_ready, t + 1)
                dve.reciprocal(rs3[:, t:t + 1], rs3[:, t:t + 1]).then_inc(rs3_ready, 1)
                dve.wait_ge(rs3_ready, t + 1)
                dve.scalar_tensor_tensor(out=x_sb[:, t, :], in0=x_sb[:, t, :], scalar=rs3[:, t:t + 1], in1=fng[:, :],
                                         op0=ALU.mult, op1=ALU.mult).then_inc(fin_ready, 1)

            dve.wait_ge(fng_in, 16)
            for t in range(TT):
                rows_k = y_back(t).rearrange("p (k d) -> p d k", k=TOP_K)[:, :, 0:TOP_K - PE_ROWS]
                dve.wait_ge(y_in[t % 3], 16 * (t // 3 + 1))
                if t:
                    dve.wait_ge(x3_ready, t)
                dve.tensor_reduce(total, rows_k, AX_X, ALU.add).then_inc(summed, 1)
                dve.wait_ge(summed, t + 1)
                for half in range(2):
                    n = 2 * t + half
                    dve.wait_ge(sd_done, n + 1)
                    th = total[:, half * S:(half + 1) * S]
                    dve.tensor_tensor(th, th, bank(4 + n % 4), ALU.add).then_inc(sd_free, 1)
                sums += 1
                dve.wait_ge(sd_free, 2 * t + 2)
                dve.tensor_tensor(total, total, gate2_b[:, :], ALU.mult).then_inc(sum_step, 1)
                dve.wait_ge(sum_step, sums)
                dve.tensor_tensor(x_sb[:, t, :], x_sb[:, t, :], total, ALU.add).then_inc(x3_ready, 1)
                if t:
                    final(t - 1)
            final(TT - 1)

        @block.tensor
        def _(pe):
            def weights(kind, u):
                n = unit_no[kind, u]
                _, _, q, hi = units[n]
                pe.wait_ge(w_lo_ready, products.index(n) + 1)
                return split[hi], split[q]

            def three(out, lhs, rhs, first, last):
                pe.matmul(out, lhs[0], rhs[0], start=first, stop=False)
                pe.matmul(out, lhs[0], rhs[1], start=False, stop=False)
                return pe.matmul(out, lhs[1], rhs[0], start=False, stop=last)

            pe.wait_ge(rows_in, 16 * 7)
            pe.wait_ge(consts, 1)
            pe.transpose(bank(O_BANK)[:, 0:ROWS], rows[0:ROWS, :], ident[0:ROWS, 0:ROWS]).then_inc(rows_T, 1)

            def turn(t, g0):
                for half in range(2):
                    g = g0 + 2 * t + half
                    pe.wait_ge(xn_ready, g0 // 2 + t + 1)
                    if g >= 2:
                        pe.wait_ge(xT_free, g - 1)
                    for k in range(4):
                        mm = pe.transpose(bank(2 + g % 2)[:, k * P:(k + 1) * P],
                                          xg[:, t % 2, (4 * half + k) * P:(4 * half + k + 1) * P], ident[:, :])
                    mm.then_inc(xT_done, 1)

            for t in range(TT):
                turn(t, 0)

            def ada(u):
                n = tile_no["ada", u]
                pe.wait_ge(acc_ready, u + 1)
                freed(pe, n)
                acc = accs[:, u % 2, 0, :]
                if u // 4 in (2, 5):
                    mm = pe.matmul(bank(n % 2)[:, 0:256], ones[:, :], acc, start=True, stop=True)
                else:
                    for c in range(2):
                        mm = pe.matmul(bank(n % 2)[:, c:c + 1], acc[:, c * P:(c + 1) * P], ones[:, 0:1],
                                       start=True, stop=True)
                mm.then_inc(tile_done, 1)

            for u in range(8):
                ada(u)

            def dense(n, w, c, rhs, ks, last):
                freed(pe, n)
                for k in range(ks):
                    mm = pe.matmul(bank(n % 2), w[:, k, c * P:(c + 1) * P], rhs(k), start=(k == 0), stop=(k == ks - 1))
                mm.then_inc(tile_done, 1)
                if last:
                    pe.wait_ge(tile_done, n + 1)
                    pe.sem_inc(w_used, 1)

            def product_tile(n, w, c, x, k0, ks, last, half=None):
                if half != 1:
                    freed(pe, n)
                w = [part[:, :].rearrange("p (k f) -> p k f", k=ks) for part in w]
                for k in range(ks) if half is None else range(half * ks // 2, (half + 1) * ks // 2):
                    mm = three(bank(n % 2), [part[:, k, c * P:(c + 1) * P] for part in w],
                               [part[:, k0 + k, :] for part in x], k == 0, k == ks - 1)
                if half == 0:
                    return
                mm.then_inc(tile_done, 1)
                if last:
                    pe.wait_ge(tile_done, n + 1)
                    pe.sem_inc(w_used, 1)

            def h_tile(kind, j, unit, c, last):
                product_tile(tile_no[kind, j], weights(*unit), c, (h_hi, h_lo), 0, KD, last)

            pe.wait_ge(h_lo_ready, KD)
            for u in range(9):
                if u in (4, 5, 8):
                    w = [part[:, :].rearrange("p (k f) -> p k f", k=KD) for part in weights("in", u)]
                    if u == 8:
                        h_tile("qk", 12, ("in", 8), 0, False)
                    for half in range(2):
                        n = tile_no["v", 2 * (u - 4) + half if u < 8 else 4 + half]
                        freed(pe, n)
                        for m in range(2):
                            t = 2 * half + m
                            for k in range(KD):
                                mm = three(bank(n % 2)[:, m * 256:(m + 1) * 256],
                                           [part[:, k, t * P:(t + 1) * P] for part in (h_hi, h_lo)],
                                           [part[:, k, :] for part in w], k == 0, k == KD - 1)
                        mm.then_inc(tile_done, 1)
                    pe.wait_ge(tile_done, n + 1)
                    pe.sem_inc(w_used, 1)
                else:
                    j0 = 2 * u if u < 4 else 2 * u - 4
                    h_tile("qk", j0, ("in", u), 0, False)
                    h_tile("qk", j0 + 1, ("in", u), 1, True)

            def scores_of(u):
                kind, h, i = att[u]
                sc = bank(2 + 2 * (u % 2), 2)
                if u >= 2:
                    pe.wait_ge(exp_done, u - 1)
                if kind == "da":
                    for m in range(2):
                        a = slice(64 * m, 64 * m + 64)
                        mm = pe.matmul(sc[:, m * S:m * S + (i + 1) * P], qk[a, h, i * P:(i + 1) * P],
                                       qk[a, 4 + h, 0:(i + 1) * P], start=True, stop=True)
                else:
                    k0, w = max(i - 1, 0) * P, min(i + 1, 2) * P
                    for r in range(4):
                        n = 4 * h + r
                        a = slice(64 * (n % 2), 64 * (n % 2) + 64)
                        keys = qk[a, 12, :] if n % 2 == h else kdup[a]
                        c0 = r % 2 * S + r // 2 * 256
                        mm = pe.matmul(sc[:, c0:c0 + w], qk[a, 8 + n // 2, i * P:(i + 1) * P],
                                       keys[:, k0:k0 + w], start=True, stop=True)
                mm.then_inc(s_done, 1)

            def turn_probs(u, n):
                kind, h, i = att[u]
                half = n - t_steps[u]
                nb = i + 1 if kind == "da" else min(i + 1, 2)
                if n:
                    pe.wait_ge(pT_ready, n)
                blocks = ([(0, b) for b in range(nb)] if kind == "da"
                          else [(256 * (2 * half + r), b) for r in range(2) for b in range(nb)])
                for m, (c0, b) in enumerate(blocks):
                    mm = pe.transpose(bank(T_BANK)[:, m * P:(m + 1) * P],
                                      probs[:, u % 2, c0 + b * P:c0 + (b + 1) * P], ident[:, :])
                mm.then_inc(pT_done, 1)

            def values(u, n):
                kind, h, i = att[u]
                half = n - t_steps[u]
                nb = i + 1 if kind == "da" else min(i + 1, 2)
                pe.wait_ge(pT_ready, n + 1)
                if half == 0 and u:
                    pe.wait_ge(o_ready, u)
                if kind == "da":
                    for b in range(nb):
                        mm = pe.matmul(bank(O_BANK)[:, 0:P], pT[:, n % 2, b * P:(b + 1) * P],
                                       v_sb[:, b, h * P:(h + 1) * P], start=(b == 0), stop=(b == nb - 1))
                else:
                    k0 = max(i - 1, 0)
                    for r in range(2):
                        o0 = (2 * half + r) * HD
                        for b in range(nb):
                            m = r * nb + b
                            mm = pe.matmul(bank(O_BANK)[:, o0:o0 + HD], pT[:, n % 2, m * P:(m + 1) * P],
                                           v_sb[:, k0 + b, 512 + HD * h:512 + HD * h + HD],
                                           start=(b == 0), stop=(b == nb - 1))
                mm.then_inc(pv_done, 1)

            pe.wait_ge(roped, 13)
            pe.wait_ge(kdup_ready, 1)
            v_count = sum(1 for t in tiles[:tile_no["v", 4] + 1] if t[2] == "D")
            pe.wait_ge(free_d, v_count)
            scores_of(0)
            scores_of(1)
            for u in range(NU):
                if att[u][0] == "da":
                    pe.wait_ge(p_ready, u + 1)
                else:
                    pe.wait_ge(exp_done, u + 1)
                if u + 2 < NU:
                    scores_of(u + 2)
                for n in steps_of(u):
                    turn_probs(u, n)
                    for kind, j, half in filler(n):
                        if kind == "ada":
                            ada(j)
                        else:
                            product_tile(tile_no["gate", j], weights("gate", j // 2), j % 2, (h_hi, h_lo), 0, KD,
                                         j % 2 == 1, half)
                    values(u, n)

            pe.wait_ge(o_ready, NU)
            for n in range(8):
                if n == 4:
                    pe.wait_ge(da_scaled, 1)
                if n >= 4:
                    pe.wait_ge(y_lo_ready, n - 3)
                src = O[:, 4 * S:8 * S] if n < 4 else O[:, 0:4 * S]
                for t in range(TT):
                    c = t * S + (n % 4) * P
                    mm = pe.transpose(bank(2 + n % 4)[:, t * P:(t + 1) * P], src[:, c:c + P], ident[:, :])
                mm.then_inc(yT_done, 1)
            pe.wait_ge(y_lo_ready, 8)
            for m in range(8):
                for b, kind in enumerate(("branch_a", "branch_b")):
                    product_tile(tile_no["branch", 2 * m + b], weights(kind, m // 4), m % 4, (y_hi, y_lo), 4 * b, 4, m % 4 == 3)

            def turn2(t):
                pe.wait_ge(xn_ready, TT + t + 1)
                for half, left in enumerate((h2_dve, h2_act)):
                    if t:
                        pe.wait_ge(left, t)
                    for k in range(4):
                        mm = pe.transpose(bank(2 + half)[:, k * P:(k + 1) * P],
                                          xg[:, t % 2, (4 * half + k) * P:(4 * half + k + 1) * P], ident[:, :])
                    mm.then_inc(xT_done, 1)

            def router(t):
                pe.wait_ge(h2_dve, t + 1)
                pe.wait_ge(h2_act, t + 1)
                if t == 0:
                    pe.wait_ge(late_in, 64)
                for k in range(KD):
                    mm = pe.matmul(bank(4)[0:N_EXP, t * P:(t + 1) * P], wr[:, k, :], hT[:, k, t * P:(t + 1) * P],
                                   start=(k == 0), stop=(k == KD - 1))
                mm.then_inc(logits_done, 1)

            w_out = [[part[:, :].rearrange("p (k f) -> p k f", k=2) for part in weights("out", u)] for u in range(4)]
            pe.wait_ge(m_lo_ready, KD)
            for t in range(TT):
                for half in range(2):
                    n = tile_no["out", 2 * t + half]
                    freed(pe, n)
                    for k in range(KD):
                        mm = three(bank(n % 2), [part[:, k, t * P:(t + 1) * P] for part in (m_hi, m_lo)],
                                   [part[:, k % 2, half * S:(half + 1) * S] for part in w_out[k // 2]], k == 0, k == KD - 1)
                    mm.then_inc(tile_done, 1)
                    if t and half == 0:
                        turn2(t - 1)
                if t:
                    router(t - 1)
            pe.wait_ge(tile_done, n + 1)
            pe.sem_inc(w_used, 4)
            turn2(TT - 1)
            router(TT - 1)
            pe.wait_ge(logits_ready, TT)
            for t in range(TT):
                mm = pe.transpose(bank(5)[:, t * N_EXP:(t + 1) * N_EXP], logits_T[0:N_EXP, t * P:(t + 1) * P],
                                  ident[0:N_EXP, 0:N_EXP])
            mm.then_inc(logits_turned, 1)

            def shared_tiles(k, q):
                for c, kind in enumerate(("sh_gate", "sh_up")):
                    dense(tile_no[kind, k], as_k(q + c, KD), k, lambda k: hT[:, k, :], KD, False)

            for q in (9, 10):
                pe.wait_ge(landed[q], 16 * (fills(len(units), q) + 1))
            shared_tiles(0, 9)
            n = tile_no["rank", 0]
            freed(pe, n)
            pe.wait_ge(chosen_ready, 1)
            def ranks(lhs, to, src, width, first, last):
                return pe.matmul(bank(n % 2)[:, to * N_EXP:(to + width) * N_EXP], lhs[:, :],
                                 chosen[:, src * N_EXP:(src + width) * N_EXP], start=first, stop=last)

            ranks(upper, 0, 0, TT, True, False)
            for d in range(1, TT):
                ranks(ones, d, 0, TT - d, False, d == TT - 1)
            for t in range(TT):
                mm = ranks(ones, TT, t, 1, t == 0, t == TT - 1)
            mm.then_inc(tile_done, 1)

            def tokens(e, b, payload=None):
                pe.wait_ge(oh_ready, e + 1)
                past(pe, idx_ready, e)
                z = Z[:, :, bass.ds(e if payload is None else payload, 1), :]
                for t in range(TT):
                    mm = pe.matmul(bank(IDX_BANK)[:, 0:3], onehot[:, b, t, :],
                                   z[:, t, :, :].rearrange("p a c -> p (a c)"), start=(t == 0), stop=(t == TT - 1))
                mm.then_inc(idx_done, 1)

            for e in range(AHEAD):
                tokens(e, e % 2)

            def turn_tokens(e, x):
                past(pe, xgT_dve, e)
                past(pe, xgT_act, e)
                for k in range(KD):
                    mm = pe.transpose(bank(4, 2)[:, k * P:(k + 1) * P], x[:, k * P:(k + 1) * P], ident[:, :])
                mm.then_inc(xgT_done, 1)

            def gate_up(e, b, q):
                pe.wait_ge(xgT_dve, e + 1)
                pe.wait_ge(xgT_act, e + 1)
                for c in range(2):
                    w = as_k(q + c, KD)
                    for m in range(KF):
                        o = (KF * c + m) * SLOTS
                        for k in range(KD):
                            mm = pe.matmul(bank(2 + b)[:, o:o + SLOTS], w[:, k, m * P:(m + 1) * P], xgT[:, b, k, :],
                                           start=(k == 0), stop=(k == KD - 1))
                mm.then_inc(gu_done, 1)

            def down(e, b, q):
                pe.wait_ge(hact_ready, e + 1)
                past(pe, y_ready, e)
                w = as_k(q, KF)
                for half in range(2):
                    for k in range(KF):
                        mm = pe.matmul(bank(half), hact[:, b, k, :], w[:, k, half * S:(half + 1) * S],
                                       start=(k == 0), stop=(k == KF - 1))
                mm.then_inc(dn_done, 1)

            dense_uses = [fills(len(units), s) + int(s in (9, 10)) for s in range(12)]

            def round_of(i, j):
                return UNROLL // DEPTH * i + j // DEPTH + 1

            def arrived(i, j, part):
                q = 3 * (j % DEPTH) + part
                pe.wait_ge(landed[q], 16 * (round_of(i, j) + dense_uses[q]))

            def turn_expert(e, i, j):
                pe.wait_ge(gathered[j % DEPTH], 16 * round_of(i, j))
                turn_tokens(e, x_exp[:, j % DEPTH, :])

            def gate_up_expert(e, i, j):
                arrived(i, j, 0)
                arrived(i, j, 1)
                gate_up(e, j % 2, 3 * (j % DEPTH))

            def over_tokens(i, b):
                e = pe.value_load(over_i[0:1, bass.ds(i, 1)], min_val=0, max_val=N_EXP - 1)
                tokens(N_EXP + i, b, e)

            def pe_pass(i, last=False, n_over=None):
                for j in range(UNROLL):
                    e = UNROLL * i + j
                    if last and j >= UNROLL - 2:
                        m = j - UNROLL + 2
                        with pe.If(m < n_over):
                            over_tokens(m, m)
                    if not last or j + AHEAD < UNROLL:
                        tokens(e + AHEAD, (j + AHEAD) % 2)
                    if not last or j + 1 < UNROLL:
                        past(pe, hact_ready, e)
                        gate_up_expert(e + 1, i, j + 1)
                    if not last or j + 2 < UNROLL:
                        turn_expert(e + 2, i, j + 2)
                    arrived(i, j, 2)
                    down(e, j % 2, 3 * (j % DEPTH) + 2)

            turn_expert(0, 0, 0)
            turn_expert(1, 0, 1)
            gate_up_expert(0, 0, 0)
            pe.wait_ge(free_d, sum(1 for t in tiles[:tile_no["rank", 0] + 1] if t[2] == "D"))
            pe_pass(0)
            with pe.Fori(1, N_EXP // UNROLL - 1) as i:
                pe_pass(i)
            n_over = pe.value_load(over_i[0:1, 32:33], min_val=0, max_val=MAX_OVER)
            pe_pass(N_EXP // UNROLL - 1, True, n_over)

            def over_turn(i, u, round4):
                pe.wait_ge(gathered[u], 16 * round4)
                turn_tokens(N_EXP + i, x_exp[:, u, :])

            with pe.If(0 < n_over):
                over_turn(0, 0, RINGS + 1)
            pe.wait_ge(y_ready, N_EXP)
            for q in (0, 1):
                pe.wait_ge(landed[q], 16 * (dense_uses[q] + RINGS + 1))
            shared_tiles(1, 0)
            pe.wait_ge(hs_ready, KF)
            with pe.Fori(0, OVER_PASSES) as ii:
                with pe.If(DEPTH * ii < n_over):
                    for u in range(DEPTH):
                        i = DEPTH * ii + u
                        q, round2 = 3 * (u % 2), 2 * ii + u // 2 + 1
                        with pe.If(i < n_over):
                            with pe.If(i + 2 < n_over):
                                over_tokens(i + 2, u % 2)
                            pe.wait_ge(ov_landed[q], 16 * round2)
                            pe.wait_ge(ov_landed[q + 1], 16 * round2)
                            pe.wait_ge(hact_ready, N_EXP - 1 + i)
                            gate_up(N_EXP + i, u % 2, 3 + q)
                            with pe.If(i + 1 < n_over):
                                over_turn(i + 1, (u + 1) % DEPTH, ii + RINGS + 1 + (u + 1) // DEPTH)
                            pe.wait_ge(ov_landed[q + 2], 16 * round2)
                            down(N_EXP + i, u % 2, 3 + q + 2)

            pe.wait_ge(landed[2], 16 * (dense_uses[2] + RINGS + 1))
            pe.wait_ge(xgT_dve, n_over + N_EXP)
            pe.wait_ge(xgT_act, n_over + N_EXP)
            w = as_k(2, KF)

            def shared_down(t):
                for half in range(2):
                    n = 2 * t + half
                    if n >= 4:
                        pe.wait_ge(sd_free, n - 3)
                    for k in range(KF):
                        pe.matmul(bank(4 + n % 4), hsT[k][:, t * P:(t + 1) * P], w[:, k, half * S:(half + 1) * S],
                                  start=(k == 0), stop=False)

            shared_down(0)
            for t in range(TT):
                if t + 1 < TT:
                    shared_down(t + 1)
                pe.wait_ge(y_in[t % 3], 16 * (t // 3 + 1))
                rows_k = y_back(t).rearrange("p (k d) -> p k d", k=TOP_K)
                for half in range(2):
                    for k in range(TOP_K - PE_ROWS, TOP_K):
                        mm = pe.matmul(bank(4 + (2 * t + half) % 4), ident[:, :], rows_k[:, k, half * S:(half + 1) * S],
                                       start=False, stop=(k == TOP_K - 1))
                    mm.then_inc(sd_done, 1)


_INS = ["x", "c", "positions", "norm1_g", "norm2_g", "w_ada", "b_ada", "w_in", "b_in", "da_lambda", "da_norm_g",
        "sw_sinks", "w_branch_a", "w_branch_b", "w_gate", "b_gate", "w_out", "w_router", "router_bias",
        "w_exp_gate", "w_exp_up", "w_exp_down", "w_sh_gate", "w_sh_up", "w_sh_down", "final_norm_g"]
_WHOLE = ("c", "positions", "final_norm_g")


def kernel(**inputs):
    import numpy as _np
    import concourse.bacc as _bacc
    from concourse import mybir as _mybir
    from concourse.bass_utils import run_bass_kernel_spmd as _run

    nc = _bacc.Bacc("TRN2", target_bir_lowering=False, num_devices=1)
    arrays, args = {}, []

    def give(name, a):
        arrays[f"in_{name}_dram"] = a
        args.append(nc.dram_tensor(f"in_{name}_dram", a.shape, _mybir.dt.from_np(a.dtype), kind="ExternalInput").ap())

    for name in _INS:
        a = _np.ascontiguousarray(inputs[name])
        give(name, a if name in _WHOLE else a[0])
    freq = 1.0 / (10000.0 ** (_np.arange(0, HD, 2) / HD))
    give("inv_freq", _np.tile(freq, 4).astype(_np.float32).reshape(P, 1))
    args.append(nc.dram_tensor("out_0_dram", (S, D), _mybir.dt.float32, kind="ExternalOutput").ap())
    build(nc, *args)
    r = _run(nc, [arrays], core_ids=[0])
    return r.results[0]["out_0_dram"].reshape(1, S, D)
```

```python
import math
from contextlib import ExitStack

import concourse.bass as bass
from concourse import mybir

ALU = mybir.AluOpType
ACT = mybir.ActivationFunctionType
F32 = mybir.dt.float32
F32R = mybir.dt.float32r
BF16 = mybir.dt.bfloat16
I32 = mybir.dt.int32
AX_X = mybir.AxisListType.X

P = 128
D = 1024
S = 512
KD = D // P
TT = S // P
HD = 64
CHUNK = 64
DA_HEADS = 4
SW_HEADS = 8
SW_KV = 2
N_EXP = 64
N_GRP = 8
TOP_K = 8
TOP_G = 4
FF = 256
KF = FF // P
SLOTS = 128
MAX_OVER = 31
ROUTED_SCALE = 2.5
EPS = 1e-6
LAMBDA_INIT = 0.8 - 0.6 * math.exp(-0.3 * 0)
SCALE = HD ** -0.5
MASKED = -1e30
PARTS = 7
SKIP = 1e6

TWO_PI_A = 6.28125
TWO_PI_B = round((2 * math.pi - TWO_PI_A) * 2 ** 20) / 2 ** 20
TWO_PI_C = 2 * math.pi - TWO_PI_A - TWO_PI_B
ROUND = 1.5 * 2 ** 23
PI_IN = 3.1415925

ROW_C, ROW_ADA, ROW_N1, ROW_N2, ROW_BIN, ROW_BG, ROW_DAG, ROWS = 0, 8, 56, 64, 72, 90, 106, 107

RING = 6
UNIT = 2048
DIRECT = (2, 5)
PE_ROWS = 3
UNROLL = 8
DEPTH = 4
AHEAD = 5


def weight_units():
    pair = lambda p: (2 * p, 2 * p + 1)
    units = [("ada", u, RING + u, None) for u in range(6)] + [("in", 0) + pair(1)]
    units += [("ada", 6, 0, None), ("ada", 7, 1, None)]
    units += [("in", u) + pair((u + 1) % 3) for u in range(1, 9)]
    for j in range(8):
        units += [("gate", j) + pair(1 + j % 2), ("ada", 8 + 2 * j, 0, None), ("ada", 9 + 2 * j, 1, None)]
    units += [("branch_a", 0) + pair(1), ("branch_b", 0) + pair(0), ("branch_a", 1) + pair(3), ("branch_b", 1) + pair(4)]
    units += [("out", 0) + pair(5), ("out", 1) + pair(2), ("out", 2) + pair(1), ("out", 3) + pair(0)]
    return units


def attention_units():
    return ([("da", h, i) for h in range(DA_HEADS) for i in range(TT)]
            + [("sw", g, i) for g in range(SW_KV) for i in range(TT)])


def filler(n):
    gate = ("gate", n // 2, n % 2)
    ada = ("ada", 8 + n // 2, 0)
    return {0: [gate], 1: [gate, ada], 2: [ada, gate], 3: [gate]}[n % 4]


def gate_tiles():
    return [(kind, j) for n in range(32) for kind, j, half in filler(n) if kind == "ada" or half == 0]


def psum_tiles():
    tiles = [("ada", u, "D") for u in range(8)]
    tiles += [("qk", j, "A") for j in range(8)]
    tiles += [("v", j, "D") for j in range(4)]
    tiles += [("qk", j, "A") for j in range(8, 13)]
    tiles += [("v", 4, "D"), ("v", 5, "D")]
    tiles += [(k, u, "A" if k == "gate" else "D") for k, u in gate_tiles()]
    tiles += [("branch", j, "D") for j in range(16)]
    tiles += [("out", j, "D") for j in range(2 * TT)]
    tiles += [("sh_gate", 0, "A"), ("sh_up", 0, "D"), ("sh_gate", 1, "A"), ("sh_up", 1, "D")]
    return tiles


def build(nc, x_d, c_d, pos_d, n1_d, n2_d, w_ada_d, b_ada_d, w_in_d, b_in_d, lam_d, dag_d, sinks_d,
          w_ba_d, w_bb_d, w_gate_d, b_gate_d, w_out_d, w_router_d, r_bias_d, w_eg_d, w_eu_d, w_ed_d,
          w_sg_d, w_su_d, w_sd_d, fng_d, inv_freq_d, out_d):
    units = weight_units()
    unit_no = {(kind, u): n for n, (kind, u, _, _) in enumerate(units)}
    by_vector = [u for u in range(24) if u not in DIRECT]
    products = [n for n, u in enumerate(units) if u[0] != "ada"]

    def fills(n, s):
        return sum(1 for u in units[:n + 1] if u[2] == s)

    tiles = psum_tiles()
    tile_no = {(k, i): n for n, (k, i, _) in enumerate(tiles)}
    att = attention_units()
    NU = len(att)

    t_steps = []
    n_steps = 0
    for kind, _, _ in att:
        t_steps.append(n_steps)
        n_steps += 1 if kind == "da" else 2

    assert n_steps == 32

    def steps_of(u):
        return range(t_steps[u], t_steps[u] + (1 if att[u][0] == "da" else 2)) if u < NU else ()

    xn2_d = nc.dram_tensor("xn2_scratch", (S, D), F32, kind="Internal").ap()
    y_d = nc.dram_tensor("expert_rows", (S * TOP_K, D), F32, kind="Internal").ap()

    with ExitStack() as ctx:
        def sb(name, cols, dt=F32):
            return ctx.enter_context(nc.sbuf_tensor(name, [P, cols], dt))

        def sem(name):
            return ctx.enter_context(nc.semaphore(name))

        def same_space(*names_cols):
            with ExitStack() as inner:
                return [inner.enter_context(nc.sbuf_tensor(name, [P, c], F32R)) for name, c in names_cols]

        def by_k(a):
            return a[:, :].rearrange("p (k s) -> p k s", k=KD)

        split = same_space(*[(f"w_{'hi' if s % 2 else 'lo'}{s // 2}", UNIT) for s in range(12)])
        wring = sb("wring", 12 * UNIT)
        h_hi, = map(by_k, same_space(("h_hi", KD * S)))
        x_sb = sb("x_sb", TT * D)[:, :].rearrange("p (t d) -> p t d", t=TT)
        h_lo, = map(by_k, same_space(("h_lo", KD * S)))
        hT = sb("hT", KD * S)[:, :].rearrange("p (k s) -> p k s", k=KD)
        m_lo, m_hi = map(by_k, same_space(("m_lo", KD * S), ("m_hi", KD * S)))
        G = sb("G", 16 * S)
        O = sb("O", 8 * S)
        xg = sb("xg", 2 * D)[:, :].rearrange("p (b d) -> p b d", b=2)
        gate_b = sb("gate_b", D)
        gate2_b = sb("gate2_b", D)
        fng = gate_b
        bias_v = sb("bias_v", 640)
        wr = sb("wr", KD * N_EXP)[:, :].rearrange("p (k e) -> p k e", k=KD)
        hsT = [bias_v[:, 0:S], wr.rearrange("p k e -> p (k e)")]
        hact = sb("hact", 2 * KF * SLOTS)[:, :].rearrange("p (b k s) -> p b k s", b=2, k=KF)
        ident = sb("ident", P)
        rows = sb("rows", P)
        cols = sb("cols", ROWS)
        mod = sb("mod", 48)
        small = sb("small", 160)

        def slot(s):
            return wring[:, s * UNIT:(s + 1) * UNIT]

        late = wring[:, RING * UNIT:12 * UNIT]
        qk = late[:, 0:13 * S].rearrange("p (j s) -> p j s", j=13)
        y_hi, y_lo = h_hi, h_lo
        v_sb = late[:, 13 * S:13 * S + TT * 640].rearrange("p (t c) -> p t c", t=TT)
        probs = late[:, 18 * S:22 * S].rearrange("p (b c) -> p b c", b=2)
        pT = late[:, 22 * S:24 * S].rearrange("p (b c) -> p b c", b=2)

        gates = G[:, :].rearrange("p (j s) -> p j s", j=16)
        cos_t, sin_t = gates[:, 12, :], gates[:, 13, :]
        swapped = gates[:, 14:16, :]
        ang, rnd = gates[:, 8, :], gates[:, 9, :]
        pos_i, ang_abs = gates[:, 10, :].bitcast(I32), gates[:, 11, :]
        square = G[:, 0:D]
        x_exp = G[:, 0:DEPTH * D].rearrange("p (b d) -> p b d", b=DEPTH)
        xgT = G[:, TT * D:TT * D + 2 * D].rearrange("p (b k s) -> p b k s", b=2, k=KD)
        y_sb = G[:, TT * D + 2 * D:TT * D + 4 * D].rearrange("p (b d) -> p b d", b=2)
        y_bufs = [y_sb[:, 0, :], y_sb[:, 1, :], xg[:, 0, :], xg[:, 1, :]]

        kdup = xg[:, 0, 0:S]
        o_da = O[:, 0:4 * S].rearrange("p (i h v) -> p i h v", i=TT, h=DA_HEADS)
        o_sw = O[:, 4 * S:8 * S].rearrange("p (i h v) -> p i h v", i=TT, h=SW_HEADS)
        mixed = O[:, 0:2 * S].rearrange("p (b s) -> p b s", b=2)
        junk2 = O[:, 2 * S:4 * S]
        sg = O[:, 2 * S:3 * S]
        which = O[:, 2 * S:6 * S].rearrange("p (i e) -> p i e", i=32)
        TE = TT * N_EXP

        def rt(n, width=TE):
            return O[:, 4 * S + n * TE:4 * S + n * TE + width]

        def te(a):
            return a.rearrange("p (t e) -> p t e", t=TT)

        scores, choice, masked, replaced = rt(0), rt(1), rt(2), rt(3)
        chosen, cum, rank_m = rt(4), rt(5), rt(6)
        logits_T = rt(4, 2 * TE)
        top8 = O[:, 3 * S:3 * S + TE]
        Z = O[:, 0:TE * PARTS // 2].bitcast(BF16).rearrange("p (t e c) -> p t e c", t=TT, c=PARTS)
        sums_onehot = sb("sums_onehot", 4 * 256)
        onehot = sums_onehot[:, 0:TT * SLOTS].bitcast(BF16).rearrange("p (b t s) -> p b t s", b=2, t=TT)
        accs = sums_onehot[:, :].rearrange("p (b a c) -> p b a c", b=2, a=2)
        iota_s = sb("iota_s", SLOTS)
        upper = sb("upper", P)
        ones = sb("ones", P)
        tri8 = sb("tri8", 64)
        rbias = sb("rbias", N_EXP)
        idx_i = ctx.enter_context(nc.sbuf_tensor("idx_i", [P, 2 * UNROLL], I32))
        idx_w = sb("idx_w", UNROLL)
        idx_f = sb("idx_f", 4)
        over_i = ctx.enter_context(nc.sbuf_tensor("over_i", [P, 40], I32))
        over_f = sb("over_f", 3 * 32)
        att_s = sb("att_s", 2 * 24)
        lam = gates[:, 7, 0:256]

        at = [0]

        def col(n):
            at[0] += n
            return small[:, at[0] - n:at[0]]

        cact, a1, a2 = col(8), col(8), col(8)
        eps, half_pi, sign, invf = col(1), col(1), col(1), col(1)
        ss1, rs1, ss2, rs2, ss3, rs3 = col(4), col(4), col(4), col(4), col(4), col(4)
        ssq, rsq = col(16), col(16)
        lam_s, lam_e, neglam = col(2), col(2), col(1)
        sinks = col(8)
        tok1, dest1 = col(4), col(4)
        denom, rden = col(4), col(4)
        dag = col(1)
        warm = col(1)

        psum = ctx.enter_context(nc.psum_tensor("psum", [P, 8 * 512], F32))

        def bank(b, n=1):
            return psum[:, b * 512:(b + n) * 512]

        T_BANK, O_BANK, IDX_BANK, RANK_BANK = 6, 7, 6, 7

        kdup_ready = sem("kdup_ready")
        x_in = [sem(f"x_in{t}") for t in range(TT)]
        rows_in, pos_in, misc_in, late_in = sem("rows_in"), sem("pos_in"), sem("misc_in"), sem("late_in")
        acc_ready = sem("acc_ready")
        landed = [sem(f"landed{s}") for s in range(12)]
        consts, ident_ready = sem("consts"), sem("ident_ready")
        pool_step, dve_step, act_step = sem("pool_step"), sem("dve_step"), sem("act_step")
        rows_T, cols_ready, cact_ready = sem("rows_T"), sem("cols_ready"), sem("cact_ready")
        ss_ready, std_ready = sem("ss_ready"), sem("std_ready")
        xn_ready, xT_done, xT_free = sem("xn_ready"), sem("xT_done"), sem("xT_free")
        h_ready, h_hi_ready, h_lo_ready = sem("h_ready"), sem("h_hi_ready"), sem("h_lo_ready")
        w_hi_ready, w_lo_ready = sem("w_hi_ready"), sem("w_lo_ready")
        m_hi_ready, m_lo_ready = sem("m_hi_ready"), sem("m_lo_ready")
        h2_dve, h2_act = sem("h2_dve"), sem("h2_act")
        logits_done, logits_ready, logits_turned = sem("logits_done"), sem("logits_ready"), sem("logits_turned")
        scores_ready, rank_done = sem("scores_ready"), sem("rank_done")
        ang_ready, rope_ready = sem("ang_ready"), sem("rope_ready")
        tile_done, free_a, free_d = sem("tile_done"), sem("free_a"), sem("free_d")
        roped, v_ready, lam_ready, lam_exp = sem("roped"), sem("v_ready"), sem("lam_ready"), sem("lam_exp")
        s_done, max_ready, exp_done, p_ready = sem("s_done"), sem("max_ready"), sem("exp_done"), sem("p_ready")
        pT_done, pT_ready, pv_done, o_ready = sem("pT_done"), sem("pT_ready"), sem("pv_done"), sem("o_ready")
        sq_done, da_std, da_scaled = sem("sq_done"), sem("da_std"), sem("da_scaled")
        yT_done, y_hi_ready, y_lo_ready = sem("yT_done"), sem("y_hi_ready"), sem("y_lo_ready")
        fng_in = sem("fng_in")
        merged_b, merged = sem("merged_b"), sem("merged")
        x2_ready = sem("x2_ready")
        xn2_stored = [sem(f"xn2_stored{t}") for t in range(2)]
        chosen_ready = sem("chosen_ready")
        sg_ready, hs_ready = sem("sg_ready"), sem("hs_ready")
        oh_ready, idx_done, idx_ready, idx_step = sem("oh_ready"), sem("idx_done"), sem("idx_ready"), sem("idx_step")
        gathered = [sem(f"gathered{b}") for b in range(DEPTH)]
        xgT_done, xgT_dve, xgT_act = sem("xgT_done"), sem("xgT_dve"), sem("xgT_act")
        gu_done, dn_done = sem("gu_done"), sem("dn_done")
        silu_ready, hact_ready = sem("silu_ready"), sem("hact_ready")
        y_ready = sem("y_ready")
        scattered = [sem(f"scattered{b}") for b in range(DEPTH)]
        z_ready = sem("z_ready")
        over_list, over_done = sem("over_list"), sem("over_done")
        ov_landed = [sem(f"ov_landed{q}") for q in range(6)]
        sd_done, sd_free = sem("sd_done"), sem("sd_free")
        y_in = [sem(f"y_in{b}") for b in range(TT - 1)]
        last_in = [sem(f"last_in{b}") for b in range(3)]
        x3_ready, rs3_ready, sum_step = sem("x3_ready"), sem("rs3_ready"), sem("sum_step")
        summed, ss3_ready, std3_ready, fin_ready = sem("summed"), sem("ss3_ready"), sem("std3_ready"), sem("fin_ready")
        out_done = [sem(f"out_done{t}") for t in range(TT)]

        block = ctx.enter_context(nc.Block())

        def freed(eng, n):
            if n >= 2:
                owner = tiles[n - 2][2]
                count = sum(1 for t in tiles[:n - 1] if t[2] == owner)
                eng.wait_ge(free_a if owner == "A" else free_d, count)

        def last_tile(kind, u):
            if kind == "in":
                if u in (4, 5, 8):
                    return tile_no["v", 5 if u == 8 else 2 * u - 7]
                return tile_no["qk", 2 * u + 1 if u < 4 else 2 * u - 3]
            if kind == "gate":
                return tile_no["gate", 2 * u + 1]
            if kind == "out":
                return tile_no["out", 2 * TT - 1]
            return tile_no["branch", 2 * (4 * u + 3) + (kind == "branch_b")]

        def slot_left(eng, n, s):
            if units[n][0] in ("branch_a", "branch_b", "out") and s >= RING:
                eng.wait_ge(o_ready, NU)
                return
            before = [m for m in range(n) if s in units[m][2:]]
            if not before:
                return
            m = before[-1]
            kind, u = units[m][:2]
            if kind == "ada" and u in DIRECT:
                eng.wait_ge(tile_done, tile_no["ada", u] + 1)
            elif kind == "ada":
                eng.wait_ge(acc_ready, by_vector.index(u) + 1)
            else:
                eng.wait_ge(tile_done, last_tile(kind, u) + 1)

        def past(eng, semaphore, n):
            if not isinstance(n, int) or n > 0:
                eng.wait_ge(semaphore, n)

        RINGS = N_EXP // DEPTH
        DVE_ROWS = TOP_K - PE_ROWS
        LAST_PARTS = ((DVE_ROWS, TOP_K), (0, DVE_ROWS - 2), (DVE_ROWS - 2, DVE_ROWS))
        OVER_PASSES = (MAX_OVER + DEPTH) // DEPTH

        def y_back(t):
            return G[:, :] if t % 3 == 2 else wring[:, (4 + 4 * (t % 3)) * UNIT:(8 + 4 * (t % 3)) * UNIT]

        def expert_unit(src, e):
            return src[bass.ds(e, 1)].rearrange("a (k p) f -> p (a k) f", p=P)

        def as_k(s, k):
            return slot(s).rearrange("p (k f) -> p k f", k=k)

        @block.sync
        def _(sp):
            def param_rows(eng, vecs):
                for dram, r, n in vecs:
                    eng.dma_start(rows[r:r + n, :], dram.rearrange("(k p) -> k p", p=P)).then_inc(rows_in, 16)

            param_rows(sp, [(c_d[0, :], ROW_C, 8), (b_ada_d, ROW_ADA, 48), (n1_d, ROW_N1, 8), (n2_d, ROW_N2, 8),
                            (b_in_d, ROW_BIN, 18), (b_gate_d, ROW_BG, 16), (dag_d, ROW_DAG, 1)])
            src = {
                "ada": (w_ada_d, 256), "in": (w_in_d, 256), "gate": (w_gate_d, 256),
                "branch_a": (w_ba_d, 512), "branch_b": (w_bb_d, 512),
            }
            for n, (kind, u, q, _) in enumerate(units):
                if n == 2:
                    for t in range(TT):
                        sp.dma_start(x_sb[:, t, :], x_d[t * P:(t + 1) * P, :]).then_inc(x_in[t], 16)
                slot_left(sp, n, q)
                if kind == "out":
                    dram = w_out_d[u * 2 * P:(u + 1) * 2 * P, :].rearrange("(k p) n -> p k n", p=P)
                else:
                    w, width = src[kind]
                    dram = w[:, u * width:(u + 1) * width].rearrange("(k p) n -> p k n", p=P)
                sp.dma_start(as_k(q, dram.shape[1]), dram).then_inc(landed[q], 16)
            sp.wait_ge(tile_done, tile_no["branch", 15] + 1)
            for t in range(TT):
                sp.dma_start(x_sb[:, t, :], x_d[t * P:(t + 1) * P, :]).then_inc(x_in[t], 16)

            def load_shared(q, w, k):
                sp.dma_start(as_k(q, k), w.rearrange("(k p) n -> p k n", p=P)).then_inc(landed[q], 16)

            def load_gate_up(e, j):
                q = 3 * (j % DEPTH)
                sp.dma_start(as_k(q, KD), expert_unit(w_eg_d, e)).then_inc(landed[q], 16)
                sp.dma_start(as_k(q + 1, KD), expert_unit(w_eu_d, e)).then_inc(landed[q + 1], 16)

            def load_down(e, j):
                q = 3 * (j % DEPTH) + 2
                sp.dma_start(as_k(q, KF), expert_unit(w_ed_d, e)).then_inc(landed[q], 16)

            load_shared(9, w_sg_d, KD)
            load_gate_up(2, 2)
            load_down(2, 2)
            sp.wait_ge(tile_done, tile_no["out", 2 * TT - 1] + 1)
            load_shared(10, w_su_d, KD)
            for j in (0, 1):
                load_gate_up(j, j)
                load_down(j, j)
            load_down(3, 3)
            sp.wait_ge(tile_done, tile_no["sh_gate", 0] + 1)
            sp.dma_start(as_k(9, KD), expert_unit(w_eg_d, 3)).then_inc(landed[9], 16)
            sp.wait_ge(tile_done, tile_no["sh_up", 0] + 1)
            for b in range(3):
                sp.wait_ge(gathered[b], 16)
            sp.dma_start(as_k(10, KD), expert_unit(w_eu_d, 3)).then_inc(landed[10], 16)

            def next_gate_up(e, j):
                sp.wait_ge(gu_done, e - DEPTH + 1)
                load_gate_up(e, j)

            def load_pass(i, js, last=False):
                for j in js:
                    e = UNROLL * i + j
                    if not last or j + 1 < UNROLL:
                        next_gate_up(e + 1, j + 1)
                    sp.wait_ge(dn_done, e - DEPTH + 1)
                    load_down(e, j)

            next_gate_up(DEPTH, DEPTH)
            load_pass(0, range(DEPTH, UNROLL))
            with sp.Fori(1, N_EXP // UNROLL - 1) as i:
                load_pass(i, range(UNROLL))
            load_pass(N_EXP // UNROLL - 1, range(UNROLL), True)
            sp.wait_ge(dn_done, N_EXP - DEPTH + 1)
            for q, (w, k) in enumerate(((w_sg_d, KD), (w_su_d, KD), (w_sd_d, KF))):
                load_shared(q, w, k)
            sp.wait_ge(over_list, 1)
            n_over = sp.value_load(over_i[0:1, 32:33], min_val=0, max_val=MAX_OVER)
            with sp.Fori(0, OVER_PASSES) as ii:
                with sp.If(DEPTH * ii < n_over):
                    for u in range(DEPTH):
                        i = DEPTH * ii + u
                        with sp.If(i < n_over):
                            e = sp.value_load(over_i[0:1, bass.ds(i, 1)], min_val=0, max_val=N_EXP - 1)
                            sp.wait_ge(dn_done, N_EXP - 1 + i)
                            for q, (w, k) in enumerate(((w_eg_d, KD), (w_eu_d, KD), (w_ed_d, KF))):
                                sp.dma_start(as_k(3 + 3 * (u % 2) + q, k),
                                             expert_unit(w, e)).then_inc(ov_landed[3 * (u % 2) + q], 16)
            for b in range(DEPTH):
                sp.wait_ge(scattered[b], 16 * RINGS)
            sp.wait_ge(over_done, n_over + 1)
            for t in range(TT):
                if t >= 3:
                    sp.wait_ge(summed, t - 2)
                    sp.wait_ge(sd_done, 2 * t - 4)
                back = y_back(t).rearrange("p (k d) -> p k d", k=TOP_K)
                rows_t = y_d[t * P * TOP_K:(t + 1) * P * TOP_K, :].rearrange("(p k) d -> p k d", k=TOP_K)
                if t < TT - 1:
                    sp.dma_start(back, rows_t).then_inc(y_in[t], 16)
                else:
                    for (k0, k1), landed_part in zip(LAST_PARTS, last_in):
                        sp.dma_start(back[:, k0:k1, :], rows_t[:, k0:k1, :]).then_inc(landed_part, 16)
            for t in range(TT):
                sp.wait_ge(fin_ready, t + 1)
                sp.dma_start(out_d[t * P:(t + 1) * P, :], x_sb[:, t, :]).then_inc(out_done[t], 16)
            for t in range(TT):
                sp.wait_ge(out_done[t], 16)

        @block.gpsimd
        def _(pool):
            steps = 0

            def step(ins):
                nonlocal steps
                steps += 1
                ins.then_inc(pool_step, 1)
                pool.wait_ge(pool_step, steps)

            pool.dma_start(pos_i, pos_d[0, :].partition_broadcast(P)).then_inc(pos_in, 16)
            pool.dma_start(invf, inv_freq_d).then_inc(pos_in, 16)
            step(pool.memset(ident[:, :], 0.0))
            step(pool.affine_select(out=ident[:, :], in_=ident[:, :], compare_op=ALU.not_equal, fill=1.0,
                                    base=0, pattern=[[-1, P]], channel_multiplier=1))
            pool.sem_inc(ident_ready, 1)
            step(pool.memset(ones[:, :], 1.0))
            step(pool.memset(upper[:, :], 1.0))
            step(pool.memset(tri8[:, :], 1.0))
            step(pool.memset(eps, EPS))
            step(pool.memset(half_pi, math.pi / 2))
            step(pool.memset(sign, 1.0))
            for q in (0, 2):
                step(pool.memset(sign[32 * q:32 * q + 32], -1.0))
            step(pool.iota(iota_s[:, :], pattern=[[1, SLOTS]], base=0, channel_multiplier=0,
                           allow_small_or_imprecise_dtypes=True))
            step(pool.iota(tok1, pattern=[[P, TT]], base=1, channel_multiplier=1,
                           allow_small_or_imprecise_dtypes=True))
            step(pool.iota(dest1, pattern=[[P * TOP_K, TT]], base=1, channel_multiplier=TOP_K,
                           allow_small_or_imprecise_dtypes=True))
            step(pool.affine_select(out=upper[:, :], in_=upper[:, :], compare_op=ALU.is_gt, fill=0.0,
                                    base=0, pattern=[[1, P]], channel_multiplier=-1))
            t8 = tri8[:, :].rearrange("p (g h) -> p g h", g=8)
            pool.affine_select(out=t8, in_=t8, compare_op=ALU.is_gt, fill=0.0,
                               base=0, pattern=[[1, 8], [-1, 8]], channel_multiplier=0).then_inc(consts, 1)
            pool.dma_start(lam[:, :], lam_d.rearrange("a d -> (a d)").partition_broadcast(P)).then_inc(misc_in, 16)
            pool.dma_start(sinks, sinks_d.partition_broadcast(P)).then_inc(misc_in, 16)
            def lo_weights(d):
                _, _, q, hi = units[products[d]]
                pool.wait_ge(w_hi_ready, d + 1)
                pool.tensor_tensor(split[q][:, :], slot(q), split[hi][:, :].bitcast(F32), ALU.subtract).then_inc(w_lo_ready, 1)

            n_lo = len(products)
            for d in range(3):
                lo_weights(d)
            pool.dma_start(bias_v[:, 0:512], b_in_d[1024:1536].partition_broadcast(P)).then_inc(late_in, 16)
            pool.dma_start(bias_v[:, 512:640], b_in_d[2176:2304].partition_broadcast(P)).then_inc(late_in, 16)
            pool.dma_start(rbias[:, :], r_bias_d.partition_broadcast(P)).then_inc(late_in, 16)
            for dst, part in ((gate_b, 2), (gate2_b, 5)):
                pool.dma_start(dst[:, :], b_ada_d[part * D:(part + 1) * D].partition_broadcast(P)).then_inc(late_in, 16)
            pool.dma_start(wr, w_router_d.rearrange("(k p) e -> p k e", p=P)).then_inc(late_in, 16)
            for d in range(3, n_lo - 2):
                lo_weights(d)
            for m in range(KD):
                if m in (4, 5):
                    lo_weights(n_lo - 6 + m)
                pool.wait_ge(m_hi_ready, m + 1)
                pool.tensor_tensor(m_lo[:, m, :], gates[:, m, :], m_hi[:, m, :].bitcast(F32), ALU.subtract).then_inc(m_lo_ready, 1)
            for t in range(TT):
                pool.wait_ge(xn_ready, TT + t + 1)
                pool.dma_start(xn2_d[t * P:(t + 1) * P, :], xg[:, t % 2, :]).then_inc(xn2_stored[t % 2], 16)
            pool.wait_ge(x2_ready, TT)
            pool.dma_start(fng[:, :], fng_d.partition_broadcast(P)).then_inc(fng_in, 16)
            for b in range(2):
                pool.wait_ge(xn2_stored[b], 32)

            token_bound, row_bound = pool.alloc_register("token_bound"), pool.alloc_register("row_bound")
            token_last, row_last = pool.alloc_register("token_last"), pool.alloc_register("row_last")
            pool.reg_mov(token_last, S - 2)
            pool.reg_mov(row_last, S * TOP_K - 2)

            def gather(e, j):
                pool.wait_ge(idx_ready, e + 1)
                if not isinstance(e, int) or e >= DEPTH:
                    pool.wait_ge(xgT_done, e - DEPTH + 1)
                pool.reg_add(token_bound, token_last, 1)
                pool.indirect_dma_start(
                    out=x_exp[:, j % DEPTH, :], out_offset=None, in_=xn2_d[:, :],
                    in_offset=bass.IndirectOffsetOnAxis(ap=idx_i[:, 2 * j:2 * j + 1], axis=0),
                    bounds_check=token_bound, oob_is_err=False).then_inc(gathered[j % DEPTH], 16)

            def scatter(e, j):
                pool.wait_ge(y_ready, e + 1)
                pool.reg_add(row_bound, row_last, 1)
                pool.indirect_dma_start(
                    out=y_d[:, :], out_offset=bass.IndirectOffsetOnAxis(ap=idx_i[:, 2 * j + 1:2 * j + 2], axis=0),
                    in_=y_bufs[j % DEPTH], in_offset=None,
                    bounds_check=row_bound, oob_is_err=False).then_inc(scattered[j % DEPTH], 16)

            pool.wait_ge(tile_done, tile_no["out", 2 * TT - 1] + 1)
            for e in range(AHEAD):
                gather(e, e)

            def pool_pass(i):
                for j in range(UNROLL):
                    e = UNROLL * i + j
                    gather(e + AHEAD, (j + AHEAD) % UNROLL)
                    scatter(e, j)

            with pool.Fori(0, N_EXP // UNROLL - 1) as i:
                pool_pass(i)
            pool.wait_ge(over_list, 1)
            n_over = pool.value_load(over_i[0:1, 32:33], min_val=0, max_val=MAX_OVER)
            for j in range(UNROLL):
                e = N_EXP - UNROLL + j
                if j + AHEAD < UNROLL:
                    gather(e + AHEAD, j + AHEAD)
                if j >= UNROLL - 2:
                    i = j - UNROLL + 2
                    with pool.If(i < n_over):
                        gather(N_EXP + i, i)
                scatter(e, j)

            pool.sem_inc(over_done, 1)
            with pool.Fori(0, OVER_PASSES) as ii:
                with pool.If(DEPTH * ii < n_over):
                    for u in range(DEPTH):
                        i = DEPTH * ii + u
                        with pool.If(i < n_over):
                            with pool.If(i + 2 < n_over):
                                gather(N_EXP + 2 + i, (u + 2) % DEPTH)
                            scatter(N_EXP + i, u)
                            pool.wait_ge(scattered[u], 16 * (ii + RINGS + 1))
                            pool.sem_inc(over_done, 1)

        @block.scalar
        def _(act):
            act.wait_ge(cols_ready, 1)
            act.activation(cact, cols[:, ROW_C:ROW_C + 8], ACT.Silu).then_inc(cact_ready, 1)
            for t in range(TT):
                act.wait_ge(x_in[t], 16)
                if t:
                    act.wait_ge(ss_ready, t)
                act.activation(square, x_sb[:, t, :], ACT.Square, accum_out=ss1[:, t:t + 1]).then_inc(ss_ready, 1)
            act.wait_ge(ss_ready, TT)
            act.wait_ge(consts, 1)
            act.activation(rs1, ss1, ACT.Sqrt, bias=eps, scale=1.0 / D).then_inc(std_ready, 1)

            def turned(t, g0):
                for g in (g0 + 2 * t, g0 + 2 * t + 1):
                    half = g % 2
                    act.wait_ge(xT_done, g + 1)
                    act.activation(hT[:, 4 * half:4 * half + 4, t * P:(t + 1) * P],
                                   bank(2 + g % 2).rearrange("p (k s) -> p k s", k=4), ACT.Copy).then_inc(xT_free, 1)

            def hi_weights(kind, u):
                n = unit_no[kind, u]
                _, _, q, hi = units[n]
                act.wait_ge(landed[q], 16 * fills(n, q))
                slot_left(act, n, hi)
                act.activation(split[hi][:, :], slot(q), ACT.Copy).then_inc(w_hi_ready, 1)

            for t in range(TT):
                turned(t, 0)
            hi_weights("in", 0)
            for k in range(KD):
                if k == KD // 2:
                    hi_weights("in", 1)
                act.wait_ge(h_ready, k + 1)
                act.activation(h_hi[:, k, :], hT[:, k, :], ACT.Copy).then_inc(h_hi_ready, 1)
            hi_weights("in", 2)
            act.wait_ge(ang_ready, 1)
            act.activation(sin_t, ang, ACT.Sin, scale=sign).then_inc(rope_ready, 1)
            act.activation(cos_t, ang_abs, ACT.Sin, bias=half_pi, scale=-1.0).then_inc(rope_ready, 1)
            act.wait_ge(lam_ready, 1)
            act.activation(lam_e, lam_s, ACT.Exp).then_inc(lam_exp, 1)

            def empty_qk(j):
                n = tile_no["qk", j]
                b = bank(n % 2)
                c0 = ROW_BIN + (j if j < 8 else j + 4)
                act.wait_ge(tile_done, n + 1)
                act.activation(qk[:, j, :], b, ACT.Identity, bias=cols[:, c0:c0 + 1])
                if j >= 2:
                    act.wait_ge(roped, j - 1)
                for q in range(4):
                    r = q ^ 1
                    ins = act.activation(swapped[32 * r:32 * r + 32, j % 2, :], b[32 * q:32 * q + 32],
                                         ACT.Identity, bias=cols[32 * q:32 * q + 32, c0:c0 + 1])
                ins.then_inc(free_a, 1)

            for u in range(9):
                for j in ((12,) if u == 8 else () if u in (4, 5) else (2 * u, 2 * u + 1) if u < 4 else (2 * u - 4, 2 * u - 3)):
                    empty_qk(j)
                if u + 3 < 9:
                    hi_weights("in", u + 3)
                elif u == 6:
                    hi_weights("gate", 0)

            def exps(u):
                kind, h, i = att[u]
                sc = bank(2 + 2 * (u % 2), 2)
                s = att_s[:, 24 * (u % 2):24 * (u % 2) + 24]
                act.wait_ge(max_ready, u + 1)
                if u >= 2:
                    act.wait_ge(pT_done, t_steps[u - 1])
                if kind == "da":
                    w = (i + 1) * P
                    for m in range(2):
                        ins = act.activation(probs[:, u % 2, m * S:m * S + w], sc[:, m * S:m * S + w], ACT.Exp,
                                             bias=s[:, 2 + m:3 + m], scale=SCALE, accum_out=s[:, 4 + m:5 + m])
                else:
                    w = min(i + 1, 2) * P
                    for r in range(4):
                        act.activation(probs[:, u % 2, r * 256:r * 256 + w], sc[:, r * 256:r * 256 + w], ACT.Exp,
                                       bias=s[:, 4 + r:5 + r], scale=SCALE, accum_out=s[:, 8 + r:9 + r])
                    ins = act.activation(s[:, 16:20], s[:, 12:16], ACT.Exp)
                ins.then_inc(exp_done, 1)

            def probs_turned(u, n):
                kind, h, i = att[u]
                nb = (i + 1) if kind == "da" else min(i + 1, 2) * 2
                act.wait_ge(pT_done, n + 1)
                if n >= 2:
                    act.wait_ge(pv_done, n - 1)
                act.activation(pT[:, n % 2, 0:nb * P], bank(T_BANK)[:, 0:nb * P], ACT.Copy).then_inc(pT_ready, 1)

            def gate_tile(j):
                n = tile_no["gate", j]
                act.wait_ge(tile_done, n + 1)
                act.activation(gates[:, j, :], bank(n % 2), ACT.Tanh, scale=0.5,
                               bias=cols[:, ROW_BG + j:ROW_BG + j + 1]).then_inc(free_a, 1)

            def squares(u):
                _, h, i = att[u]
                act.wait_ge(o_ready, u + 1)
                if u:
                    act.wait_ge(sq_done, u)
                act.activation(rows[:, :], o_da[:, i, h, :], ACT.Square,
                               accum_out=ssq[:, i * 4 + h:i * 4 + h + 1]).then_inc(sq_done, 1)

            exps(0)
            exps(1)
            act.wait_ge(roped, 13)
            for u in range(NU):
                for n in steps_of(u):
                    probs_turned(u, n)
                    if n % 2:
                        j = n // 2
                        gate_tile(j)
                        if j % 2 == 0:
                            hi_weights(*(("gate", j // 2 + 1) if j < 14 else ("branch_a", 0)))
                if u + 2 < NU:
                    exps(u + 2)
                if u and att[u - 1][0] == "da":
                    squares(u - 1)
                if u == NU - 2:
                    act.wait_ge(sq_done, 16)
                    act.activation(rsq, ssq, ACT.Sqrt, bias=eps, scale=1.0 / P).then_inc(da_std, 1)
            hi_weights("branch_b", 0)
            for n in range(8):
                act.wait_ge(yT_done, n + 1)
                if n < 4:
                    ins = act.activation(y_hi[:, 4 + n, :], bank(2 + n), ACT.Copy)
                else:
                    ins = act.activation(y_hi[:, n - 4, :], bank(n - 2), ACT.Copy, scale=dag)
                ins.then_inc(y_hi_ready, 1)
            for u in (("branch_a", 1), ("branch_b", 1), ("out", 0), ("out", 1)):
                hi_weights(*u)
            for m in range(KD):
                if m in (4, 5):
                    hi_weights("out", m - 2)
                act.wait_ge(merged, m + 1)
                act.activation(m_hi[:, m, :], gates[:, m, :], ACT.Copy).then_inc(m_hi_ready, 1)

            for t in range(TT):
                act.wait_ge(x2_ready, t + 1)
                if t:
                    act.wait_ge(ss_ready, TT + t)
                act.activation(junk2, x_sb[:, t, :], ACT.Square, accum_out=ss2[:, t:t + 1]).then_inc(ss_ready, 1)
                act.wait_ge(ss_ready, TT + t + 1)
                act.activation(rs2[:, t:t + 1], ss2[:, t:t + 1], ACT.Sqrt, bias=eps, scale=1.0 / D).then_inc(std_ready, 1)
                act.wait_ge(xT_done, 2 * TT + 2 * t + 2)
                for k in range(KD // 2, KD):
                    ins = act.activation(hT[:, k, t * P:(t + 1) * P], bank(3)[:, (k - 4) * P:(k - 3) * P], ACT.Identity,
                                         bias=mod[:, 3 * KD + k:3 * KD + k + 1], scale=a2[:, k:k + 1])
                ins.then_inc(h2_act, 1)
                if t == TT - 1:
                    act.activation(warm, eps, ACT.Sigmoid)
                act.wait_ge(logits_done, t + 1)
                act.activation(logits_T[0:N_EXP, t * P:(t + 1) * P], bank(4)[0:N_EXP, t * P:(t + 1) * P],
                               ACT.Copy).then_inc(logits_ready, 1)
            act.wait_ge(logits_turned, 1)
            act.activation(scores, bank(5)[:, 0:TE], ACT.Sigmoid).then_inc(scores_ready, 1)

            def shared_gate(k):
                n = tile_no["sh_gate", k]
                act.wait_ge(tile_done, n + 1)
                act.activation(sg, bank(n % 2), ACT.Silu).then_inc(free_a, 1)

            shared_gate(0)

            def turn_x(e, b):
                act.wait_ge(xgT_done, e + 1)
                for k in range(KD // 2, KD):
                    ins = act.activation(xgT[:, b, k, :], bank(4, 2)[:, k * P:(k + 1) * P], ACT.Identity,
                                         bias=mod[:, 3 * KD + k:3 * KD + k + 1], scale=a2[:, k:k + 1])
                ins.then_inc(xgT_act, 1)

            def silu(e, b):
                act.wait_ge(gu_done, e + 1)
                act.activation(hact[:, b, :, :].rearrange("p k s -> p (k s)"), bank(2 + b)[:, 0:KF * SLOTS],
                               ACT.Silu).then_inc(silu_ready, 1)

            def weigh(e, y, w):
                act.wait_ge(dn_done, e + 1)
                act.activation(y[:, 0:S], bank(0), ACT.Copy, scale=w)
                act.activation(y[:, S:D], bank(1), ACT.Copy, scale=w).then_inc(y_ready, 1)

            def act_pass(i, last=False):
                for j in range(UNROLL):
                    e = UNROLL * i + j
                    if not last or j + 1 < UNROLL:
                        past(act, dn_done, e)
                        silu(e + 1, (j + 1) % 2)
                    if not last or j + 2 < UNROLL:
                        act.wait_ge(gu_done, e + 1)
                        turn_x(e + 2, j % 2)
                    past(act, scattered[j % DEPTH], 16 * (UNROLL // DEPTH * i + j // DEPTH))
                    weigh(e, y_bufs[j % DEPTH], idx_w[:, j:j + 1])

            turn_x(0, 0)
            turn_x(1, 1)
            silu(0, 0)
            act_pass(0)
            with act.Fori(1, N_EXP // UNROLL - 1) as i:
                act_pass(i)
            act_pass(N_EXP // UNROLL - 1, True)

            act.wait_ge(over_list, 1)
            n_over = act.value_load(over_i[0:1, 32:33], min_val=0, max_val=MAX_OVER)
            with act.If(0 < n_over):
                turn_x(N_EXP, 0)
            with act.Fori(0, OVER_PASSES) as ii:
                with act.If(DEPTH * ii < n_over):
                    for u in range(DEPTH):
                        i = DEPTH * ii + u
                        with act.If(i < n_over):
                            act.wait_ge(dn_done, N_EXP - 1 + i)
                            silu(N_EXP + i, u % 2)
                            with act.If(i + 1 < n_over):
                                act.wait_ge(gu_done, N_EXP + i)
                                turn_x(N_EXP + i + 1, (u + 1) % 2)
                            act.wait_ge(scattered[u], 16 * (ii + RINGS))
                            weigh(N_EXP + i, y_bufs[u], idx_w[:, u:u + 1])
            shared_gate(1)

            for t in range(TT):
                act.wait_ge(x3_ready, t + 1)
                if t:
                    act.wait_ge(ss3_ready, t)
                act.activation(junk2, x_sb[:, t, :], ACT.Square, accum_out=ss3[:, t:t + 1]).then_inc(ss3_ready, 1)
                act.wait_ge(ss3_ready, t + 1)
                act.activation(rs3[:, t:t + 1], ss3[:, t:t + 1], ACT.Sqrt, bias=eps, scale=1.0 / D).then_inc(std3_ready, 1)

        @block.vector
        def _(dve):
            steps = [0]

            def step(ins):
                ins.then_inc(dve_step, 1)
                steps[0] = steps[0] + 1

            def settle():
                dve.wait_ge(dve_step, steps[0])

            dve.wait_ge(rows_T, 1)
            step(dve.tensor_copy(cols[:, :], bank(O_BANK)[:, 0:ROWS]))
            settle()
            dve.tensor_scalar(dag, cols[:, ROW_DAG:ROWS], 1.0 - LAMBDA_INIT, None, ALU.mult)
            dve.tensor_scalar(cols[:, ROW_BG:ROW_BG + 16], cols[:, ROW_BG:ROW_BG + 16], 0.5, None,
                              ALU.mult).then_inc(cols_ready, 1)

            def rotary_angles():
                dve.wait_ge(pos_in, 32)
                step(dve.tensor_copy(ang_abs, pos_i))
                settle()
                step(dve.tensor_scalar(ang, ang_abs, invf, None, ALU.mult))
                settle()
                step(dve.tensor_scalar(rnd, ang, 1.0 / (2 * math.pi), ROUND, ALU.mult, ALU.add))
                settle()
                step(dve.tensor_scalar(rnd, rnd, ROUND, None, ALU.subtract))
                settle()
                for part in (TWO_PI_A, TWO_PI_B, TWO_PI_C):
                    step(dve.scalar_tensor_tensor(out=ang, in0=rnd, scalar=-part, in1=ang, op0=ALU.mult, op1=ALU.add))
                    settle()
                step(dve.tensor_scalar(ang, ang, PI_IN, -PI_IN, ALU.min, ALU.max))
                settle()
                dve.scalar_tensor_tensor(out=ang_abs, in0=ang, scalar=-1.0, in1=ang, op0=ALU.mult,
                                         op1=ALU.max).then_inc(ang_ready, 1)

            def normed(t, r):
                dve.tensor_scalar(xg[:, t % 2, :], x_sb[:, t, :], r[:, t:t + 1], None, ALU.mult).then_inc(xn_ready, 1)

            def part(n):
                return mod[:, n * KD:(n + 1) * KD]

            def ada_sum(u):
                n = unit_no["ada", u]
                q = units[n][2]
                w = as_k(q, KD)
                dve.wait_ge(landed[q], 16 * fills(n, q))
                b = by_vector.index(u)
                if b >= 2:
                    dve.wait_ge(tile_done, tile_no["ada", by_vector[b - 2]] + 1)
                for k in range(KD):
                    acc = accs[:, b % 2, k % 2, :]
                    if k < 2:
                        step(dve.tensor_scalar(acc, w[:, k, :], cact[:, k:k + 1], None, ALU.mult))
                    else:
                        dve.wait_ge(dve_step, steps[0] - 1)
                        step(dve.scalar_tensor_tensor(out=acc, in0=w[:, k, :], scalar=cact[:, k:k + 1], in1=acc,
                                                      op0=ALU.mult, op1=ALU.add))
                settle()
                dve.tensor_tensor(accs[:, b % 2, 0, :], accs[:, b % 2, 0, :], accs[:, b % 2, 1, :],
                                  ALU.add).then_inc(acc_ready, 1)

            def ada_tile(u):
                n = tile_no["ada", u]
                dve.wait_ge(tile_done, n + 1)
                if u // 4 in (2, 5):
                    g = (gate_b if u // 4 == 2 else gate2_b)[:, u % 4 * 256:(u % 4 + 1) * 256]
                    dve.tensor_tensor(g, g, bank(n % 2)[:, 0:256], ALU.add).then_inc(free_d, 1)
                else:
                    dve.tensor_tensor(mod[:, 2 * u:2 * u + 2], bank(n % 2)[:, 0:2],
                                      cols[:, ROW_ADA + 2 * u:ROW_ADA + 2 * u + 2], ALU.add).then_inc(free_d, 1)

            dve.wait_ge(cact_ready, 1)
            ada_sum(0)
            rotary_angles()
            ada_sum(1)
            ada_tile(0)
            dve.wait_ge(std_ready, 1)
            step(dve.reciprocal(rs1, rs1))
            settle()
            for t in range(TT):
                if t == 2:
                    ada_sum(3)
                    ada_tile(1)
                if t >= 2:
                    dve.wait_ge(xT_done, 2 * t - 2)
                normed(t, rs1)
            ada_sum(4)
            ada_tile(2)
            ada_tile(3)
            ada_sum(6)
            ada_tile(4)
            ada_sum(7)
            for u in (5, 6, 7):
                ada_tile(u)
            dve.wait_ge(free_d, 8)
            step(dve.scalar_tensor_tensor(out=a1, in0=part(1), scalar=1.0, in1=cols[:, ROW_N1:ROW_N1 + 8],
                                          op0=ALU.add, op1=ALU.mult))
            dve.wait_ge(xT_free, 2 * TT)
            settle()
            for k in range(KD + 1):
                if k < KD:
                    dve.tensor_scalar(hT[:, k, :], hT[:, k, :], a1[:, k:k + 1], part(0)[:, k:k + 1],
                                      ALU.mult, ALU.add).then_inc(h_ready, 1)
                if k:
                    dve.wait_ge(h_hi_ready, k)
                    dve.tensor_tensor(h_lo[:, k - 1, :], hT[:, k - 1, :], h_hi[:, k - 1, :].bitcast(F32),
                                      ALU.subtract).then_inc(h_lo_ready, 1)
            dve.wait_ge(misc_in, 16 * 2)
            lv = lam[:, :].rearrange("p (a b d) -> p a b d", a=2, b=2)
            lp = lam[:, 0:2 * HD].rearrange("p (a d) -> p a d", a=2)
            step(dve.tensor_tensor(lp[:, 0, :], lv[:, 0, 0, :], lv[:, 0, 1, :], ALU.mult))
            settle()
            step(dve.tensor_tensor(lp[:, 1, :], lv[:, 1, 0, :], lv[:, 1, 1, :], ALU.mult))
            settle()
            dve.tensor_reduce(lam_s, lp, AX_X, ALU.add).then_inc(lam_ready, 1)
            dve.wait_ge(lam_exp, 1)
            dve.scalar_tensor_tensor(out=neglam, in0=lam_e[:, 1:2], scalar=-LAMBDA_INIT, in1=lam_e[:, 0:1],
                                     op0=ALU.add, op1=ALU.subtract)

            def by_bank(a):
                return a.rearrange("p (a b) -> p b a", b=2)

            def pairs(a):
                return a.rearrange("p (b a) -> p b a", b=2)

            def row_max(u):
                kind, h, i = att[u]
                s = att_s[:, 24 * (u % 2):24 * (u % 2) + 24]
                dve.wait_ge(s_done, u + 1)
                if kind == "da":
                    w = (i + 1) * P
                    sc = bank(2 + 2 * (u % 2), 2).rearrange("p (m c) -> p m c", m=2)
                    step(dve.memset(sc[0:CHUNK, :, w - CHUNK:w], MASKED))
                    settle()
                    step(dve.tensor_reduce(s[:, 0:2], sc[:, :, 0:w], AX_X, ALU.max))
                    settle()
                    dve.tensor_scalar(s[:, 2:4], s[:, 0:2], -SCALE, None, ALU.mult).then_inc(max_ready, 1)
                    return
                w = min(i + 1, 2) * P
                sc = bank(2 + 2 * (u % 2), 2).rearrange("p (m c) -> p m c", m=4)
                step(dve.memset(sc[0:CHUNK, :, w - CHUNK:w], MASKED))
                if i:
                    dve.memset(sc[0:CHUNK, :, 0:CHUNK], MASKED)
                    step(dve.memset(sc[CHUNK:P, :, 0:2 * CHUNK], MASKED))
                settle()
                step(dve.tensor_reduce(s[:, 0:4], sc[:, :, 0:w], AX_X, ALU.max))
                settle()
                sink = by_bank(sinks[:, 4 * h:4 * h + 4])
                step(dve.scalar_tensor_tensor(out=pairs(s[:, 0:4]), in0=pairs(s[:, 0:4]), scalar=SCALE, in1=sink,
                                              op0=ALU.mult, op1=ALU.max))
                settle()
                dve.tensor_scalar(s[:, 4:8], s[:, 0:4], -1.0, None, ALU.mult)
                dve.tensor_tensor(pairs(s[:, 12:16]), sink, pairs(s[:, 0:4]), ALU.subtract).then_inc(max_ready, 1)

            def combine(u):
                kind, h, i = att[u]
                s = att_s[:, 24 * (u % 2):24 * (u % 2) + 24]
                dve.wait_ge(exp_done, u + 1)
                if kind == "da":
                    w = (i + 1) * P
                    p0, p1 = probs[:, u % 2, 0:w], probs[:, u % 2, S:S + w]
                    step(dve.reciprocal(s[:, 6:8], s[:, 4:6]))
                    settle()
                    step(dve.tensor_scalar(p1, p1, s[:, 7:8], neglam, ALU.mult, ALU.mult))
                    settle()
                    dve.scalar_tensor_tensor(out=p0, in0=p0, scalar=s[:, 6:7], in1=p1, op0=ALU.mult,
                                             op1=ALU.add).then_inc(p_ready, 1)
                    return
                dve.wait_ge(o_ready, u - 1)
                step(dve.tensor_tensor(s[:, 20:24], s[:, 8:12], s[:, 16:20], ALU.add))
                settle()
                step(dve.reciprocal(s[:, 20:24], s[:, 20:24]))

            def out_rows(u):
                kind, h, i = att[u]
                s = att_s[:, 24 * (u % 2):24 * (u % 2) + 24]
                dve.wait_ge(pv_done, t_steps[u] + (1 if kind == "da" else 2))
                if kind == "da":
                    dve.tensor_copy(o_da[:, i, h, :], bank(O_BANK)[:, 0:P]).then_inc(o_ready, 1)
                else:
                    settle()
                    dve.tensor_tensor(o_sw[:, i, 4 * h:4 * h + 4, :].rearrange("p (a b) v -> p b a v", b=2),
                                      bank(O_BANK)[:, 0:256].rearrange("p (b a v) -> p b a v", b=2, a=2),
                                      pairs(s[:, 20:24]).unsqueeze(3).broadcast_to([P, 2, 2, HD]),
                                      ALU.mult).then_inc(o_ready, 1)

            dve.wait_ge(rope_ready, 2)
            for kind, j, _ in [t for t in tiles if t[0] in ("qk", "v")]:
                n = tile_no[kind, j]
                if kind == "qk":
                    count = sum(1 for t in tiles[:n + 1] if t[2] == "A")
                    dve.wait_ge(free_a, count)
                    dve.tensor_tensor(qk[:, j, :], qk[:, j, :], cos_t, ALU.mult)
                    step(dve.tensor_tensor(swapped[:, j % 2, :], swapped[:, j % 2, :], sin_t, ALU.mult))
                    settle()
                    dve.tensor_tensor(qk[:, j, :], qk[:, j, :], swapped[:, j % 2, :], ALU.add).then_inc(roped, 1)
                    if j == 12:
                        row_max(0)
                        row_max(1)
                    continue
                dve.wait_ge(tile_done, n + 1)
                if j == 0:
                    dve.wait_ge(late_in, 16 * 6)
                if j < 4:
                    c, t0 = 256 * (j // 2), 2 * (j % 2)
                    dve.tensor_tensor(v_sb[:, t0:t0 + 2, c:c + 256], bank(n % 2).rearrange("p (t c) -> p t c", t=2),
                                      bias_v[:, c:c + 256].unsqueeze(1).broadcast_to([P, 2, 256]),
                                      ALU.add).then_inc(free_d, 1)
                else:
                    t0 = 2 * (j - 4)
                    dve.tensor_tensor(v_sb[:, t0:t0 + 2, 512:640],
                                      bank(n % 2).rearrange("p (t c) -> p t c", t=2)[:, :, 128:256],
                                      bias_v[:, 512:640].unsqueeze(1).broadcast_to([P, 2, P]),
                                      ALU.add).then_inc(free_d, 1)
            dve.wait_ge(roped, 13)
            dve.tensor_copy(kdup[0:64], qk[64:128, 12, :])
            dve.tensor_copy(kdup[64:128], qk[0:64, 12, :]).then_inc(kdup_ready, 1)

            def ada_at(n):
                return [j for kind, j, _ in filler(n) if kind == "ada"]

            def ada_of(u):
                return [j for n in steps_of(u) for j in ada_at(n)]

            def ahead_of(u):
                return min(steps_of(u)[-1] + 3, n_steps)

            combine(0)
            for u in range(NU):
                if u + 1 < NU:
                    combine(u + 1)
                if u + 2 < NU:
                    row_max(u + 2)
                for n in range(ahead_of(u - 1) if u else 0, ahead_of(u)):
                    for j in ada_at(n):
                        ada_sum(j)
                for j in ada_of(u):
                    ada_tile(j)
                if u == NU - 1:
                    dve.wait_ge(da_std, 1)
                    step(dve.reciprocal(rsq, rsq))
                    settle()
                    oda = O[:, 0:4 * S].rearrange("p (n v) -> p n v", v=P)
                    dve.tensor_tensor(oda, oda, rsq.unsqueeze(2).broadcast_to([P, 16, P]), ALU.mult).then_inc(da_scaled, 1)
                out_rows(u)
            dve.wait_ge(free_d, sum(1 for t in tiles[:tile_no["ada", 23] + 1] if t[2] == "D"))
            dve.tensor_scalar(gate_b[:, :], gate_b[:, :], 0.5, None, ALU.mult)
            dve.scalar_tensor_tensor(out=a2, in0=part(4), scalar=1.0, in1=cols[:, ROW_N2:ROW_N2 + 8],
                                     op0=ALU.add, op1=ALU.mult)

            for n in range(8):
                dve.wait_ge(y_hi_ready, n + 1)
                if n < 4:
                    ins = dve.tensor_tensor(y_lo[:, 4 + n, :], bank(2 + n), y_hi[:, 4 + n, :].bitcast(F32), ALU.subtract)
                else:
                    ins = dve.scalar_tensor_tensor(out=y_lo[:, n - 4, :], in0=bank(n - 2), scalar=dag,
                                                   in1=y_hi[:, n - 4, :].bitcast(F32), op0=ALU.mult, op1=ALU.subtract)
                ins.then_inc(y_lo_ready, 1)

            for j in range(16):
                n = tile_no["branch", j]
                m, b = j // 2, j % 2
                dve.wait_ge(tile_done, n + 1)
                dve.scalar_tensor_tensor(out=gates[:, 8 * b + m, :], in0=gates[:, 8 * b + m, :], scalar=1.0,
                                         in1=bank(n % 2), op0=ALU.add, op1=ALU.mult).then_inc(free_d, 1)
                if b:
                    count = sum(1 for t in tiles[:n + 1] if t[2] == "D")
                    dve.wait_ge(free_d, count)
                    dve.tensor_tensor(gates[:, m, :], gates[:, m, :], gates[:, 8 + m, :], ALU.add).then_inc(merged, 1)


            def norm2(t):
                dve.wait_ge(std_ready, 1 + t + 1)
                step(dve.reciprocal(rs2[:, t:t + 1], rs2[:, t:t + 1]))
                settle()
                if t >= 2:
                    dve.wait_ge(xn2_stored[t % 2], 16)
                    dve.wait_ge(xT_done, 2 * TT + 2 * t - 2)
                normed(t, rs2)

            def turned2(t):
                dve.wait_ge(xT_done, 2 * TT + 2 * t + 1)
                for k in range(KD // 2):
                    ins = dve.tensor_scalar(hT[:, k, t * P:(t + 1) * P], bank(2)[:, k * P:(k + 1) * P], a2[:, k:k + 1],
                                            part(3)[:, k:k + 1], ALU.mult, ALU.add)
                ins.then_inc(h2_dve, 1)

            for t in range(TT):
                for half in range(2):
                    n = tile_no["out", 2 * t + half]
                    dve.wait_ge(tile_done, n + 1)
                    step(dve.tensor_tensor(mixed[:, half, :], bank(n % 2), gate_b[:, half * S:(half + 1) * S], ALU.mult))
                    settle()
                    dve.sem_inc(free_d, 1)
                    dve.wait_ge(x_in[t], 32)
                    xs = x_sb[:, t, half * S:(half + 1) * S]
                    ins = dve.tensor_tensor(xs, xs, mixed[:, half, :], ALU.add)
                    step(ins) if half == 0 else ins.then_inc(x2_ready, 1)
                    if t and half == 0:
                        turned2(t - 1)
                norm2(t)
            turned2(TT - 1)

            tok_bc = tok1.unsqueeze(2).broadcast_to([P, TT, N_EXP])
            dve.tensor_copy(Z[:, :, :, 0], tok_bc).then_inc(z_ready, 1)
            dve.wait_ge(z_ready, 1)
            step(dve.tensor_tensor(Z[:, :, :, 2], tok_bc, Z[:, :, :, 0], ALU.subtract))

            dve.wait_ge(scores_ready, 1)
            step(dve.tensor_tensor(te(choice), te(scores), rbias[:, :].unsqueeze(1).broadcast_to([P, TT, N_EXP]), ALU.add))
            settle()
            for g in range(TT * N_GRP):
                ins = dve.max(top8[:, 8 * g:8 * g + 8], choice[:, 8 * g:8 * g + 8])
            step(ins)
            settle()
            best = top8.rearrange("p (g k) -> p g k", k=8)
            gsc, grank = over_f[:, 0:32], over_f[:, 32:64]
            step(dve.tensor_tensor(gsc.unsqueeze(2), best[:, :, 0:1], best[:, :, 1:2], ALU.add))
            settle()
            def tgg(a):
                return a.rearrange("p (t g h) -> p t g h", t=TT, g=8)

            rival = gsc.rearrange("p (t h) -> p t h", t=TT).unsqueeze(2).broadcast_to([P, TT, 8, 8])
            own = gsc.rearrange("p (t g) -> p t g", t=TT).unsqueeze(3).broadcast_to([P, TT, 8, 8])
            dve.tensor_tensor(tgg(masked), rival, own, ALU.is_gt)
            step(dve.tensor_tensor(tgg(replaced), rival, own, ALU.is_equal))
            settle()
            step(dve.tensor_tensor(replaced.rearrange("p (t g) -> p t g", t=TT), replaced.rearrange("p (t g) -> p t g", t=TT),
                                   tri8[:, :].unsqueeze(1).broadcast_to([P, TT, 64]), ALU.mult))
            settle()
            step(dve.tensor_tensor(masked, masked, replaced, ALU.add))
            settle()
            step(dve.tensor_reduce(grank, masked.rearrange("p (g h) -> p g h", h=8), AX_X, ALU.add))
            settle()
            step(dve.tensor_scalar(grank, grank, float(TOP_G), None, ALU.is_lt))
            settle()
            kept = grank.unsqueeze(2).broadcast_to([P, TT * N_GRP, 8])
            g8 = lambda a: a.rearrange("p (g k) -> p g k", k=8)
            step(dve.tensor_tensor(g8(masked), g8(choice), kept, ALU.mult))
            step(dve.tensor_scalar(gsc, grank, 1.0, -MASKED, ALU.subtract, ALU.mult))
            settle()
            step(dve.tensor_tensor(g8(masked), g8(masked), gsc.unsqueeze(2).broadcast_to([P, TT * N_GRP, 8]), ALU.add))
            settle()
            for t in range(TT):
                ins = dve.max(top8[:, 8 * t:8 * t + 8], te(masked)[:, t, :])
            step(ins)
            settle()
            for t in range(TT):
                ins = dve.match_replace(te(replaced)[:, t, :], top8[:, 8 * t:8 * t + 8], te(masked)[:, t, :], 2 * MASKED)
            step(ins)
            settle()
            dve.tensor_tensor(chosen, replaced, masked, ALU.not_equal).then_inc(chosen_ready, 1)
            dve.wait_ge(chosen_ready, 1)
            step(dve.tensor_tensor(masked, scores, chosen, ALU.mult))
            for t in range(TT):
                ins = dve.tensor_tensor_scan(te(cum)[:, t, :], ones[:, 0:N_EXP], te(chosen)[:, t, :], 0.0, ALU.mult, ALU.add)
            step(ins)
            settle()
            step(dve.tensor_reduce(denom, te(masked), AX_X, ALU.add))
            step(dve.tensor_tensor(cum, cum, chosen, ALU.subtract))
            settle()
            step(dve.reciprocal(rden, denom))
            step(dve.tensor_tensor(te(cum), te(cum), dest1.unsqueeze(2).broadcast_to([P, TT, N_EXP]), ALU.add))
            settle()
            step(dve.scalar_tensor_tensor(out=te(masked), in0=te(masked), scalar=ROUTED_SCALE,
                                          in1=rden.unsqueeze(2).broadcast_to([P, TT, N_EXP]), op0=ALU.mult, op1=ALU.mult))
            step(dve.tensor_copy(Z[:, :, :, 1], te(cum)))
            settle()
            step(dve.tensor_copy(Z[:, :, :, 4], te(masked)))
            step(dve.tensor_tensor(Z[:, :, :, 3], te(cum), Z[:, :, :, 1], ALU.subtract))
            settle()
            step(dve.tensor_tensor(te(masked), te(masked), Z[:, :, :, 4], ALU.subtract))
            settle()
            step(dve.tensor_copy(Z[:, :, :, 5], te(masked)))
            settle()
            step(dve.tensor_tensor(Z[:, :, :, 6], te(masked), Z[:, :, :, 5], ALU.subtract))

            def shared_act(k):
                n = tile_no["sh_up", k]
                dve.wait_ge(tile_done, n + 1)
                m = tile_no["sh_gate", k]
                dve.wait_ge(free_a, sum(1 for t in tiles[:m + 1] if t[2] == "A"))
                dve.tensor_tensor(hsT[k], sg, bank(n % 2), ALU.mult).then_inc(hs_ready, 1)
                dve.wait_ge(hs_ready, k + 1)
                dve.sem_inc(free_d, 1)

            dve.wait_ge(rank_done, 1)
            counts, over, cum_o = cum[:, 0:64], cum[:, 64:128], cum[:, 128:192]
            step(dve.scalar_tensor_tensor(out=rank_m, in0=bank(RANK_BANK)[:, 0:TE], scalar=1.0, in1=chosen,
                                          op0=ALU.add, op1=ALU.mult))
            settle()
            step(dve.tensor_scalar(rank_m, rank_m, 1.0, None, ALU.subtract))
            step(dve.tensor_copy(counts, bank(RANK_BANK)[:, TE:TE + N_EXP]))
            settle()

            def column(e):
                return te(rank_m)[:, :, bass.ds(e, 1)].broadcast_to([P, TT, SLOTS])

            slots4 = iota_s[:, :].unsqueeze(1).broadcast_to([P, TT, SLOTS])

            def one_hot(e, b):
                if not isinstance(e, int) or e >= 2:
                    dve.wait_ge(idx_done, e - 1)
                dve.tensor_tensor(onehot[:, b, :, :], slots4, column(e), ALU.is_equal).then_inc(oh_ready, 1)

            def indices(e, j):
                v = bank(IDX_BANK)[:, 0:PARTS]
                dve.wait_ge(idx_done, e + 1)
                dve.tensor_scalar(idx_f[:, 0:2], v[:, 0:2], 0.0, SKIP, ALU.is_equal, ALU.mult).then_inc(idx_step, 1)
                dve.wait_ge(idx_step, 2 * e + 1)
                dve.tensor_tensor(idx_f[:, 0:2], idx_f[:, 0:2], v[:, 0:2], ALU.add).then_inc(idx_step, 1)
                dve.tensor_reduce(idx_w[:, j:j + 1], v[:, 4:7], AX_X, ALU.add)
                dve.wait_ge(idx_step, 2 * e + 2)
                dve.scalar_tensor_tensor(out=idx_i[:, 2 * j:2 * j + 2], in0=v[:, 2:4], scalar=-1.0, in1=idx_f[:, 0:2],
                                         op0=ALU.add, op1=ALU.add).then_inc(idx_ready, 1)

            one_hot(0, 0)
            for e in range(AHEAD):
                one_hot(e + 1, (e + 1) % 2)
                indices(e, e)
            shared_act(0)

            def turn_x(e, b):
                dve.wait_ge(xgT_done, e + 1)
                for k in range(KD // 2):
                    ins = dve.tensor_scalar(xgT[:, b, k, :], bank(4, 2)[:, k * P:(k + 1) * P], a2[:, k:k + 1],
                                            mod[:, 3 * KD + k:3 * KD + k + 1], ALU.mult, ALU.add)
                ins.then_inc(xgT_dve, 1)

            def gate_up(e, b):
                dve.wait_ge(silu_ready, e + 1)
                h = hact[:, b, :, :].rearrange("p k s -> p (k s)")
                dve.tensor_tensor(h, h, bank(2 + b)[:, KF * SLOTS:2 * KF * SLOTS], ALU.mult).then_inc(hact_ready, 1)

            def overflow_list(part):
                if part == 0:
                    step(dve.tensor_scalar(over, counts, float(SLOTS), None, ALU.is_gt))
                    settle()
                    for m in (2, 3):
                        step(dve.scalar_tensor_tensor(out=over, in0=counts, scalar=float(m * SLOTS), in1=over,
                                                      op0=ALU.is_gt, op1=ALU.add))
                        settle()
                    step(dve.tensor_tensor_scan(cum_o, ones[:, 0:N_EXP], over, 0.0, ALU.mult, ALU.add))
                    settle()
                    step(dve.tensor_copy(over_i[:, 32:33], cum_o[:, N_EXP - 1:N_EXP]))
                elif part == 1:
                    step(dve.tensor_tensor(which, cum_o.unsqueeze(1).broadcast_to([P, 32, N_EXP]),
                                           iota_s[:, 0:32].unsqueeze(2).broadcast_to([P, 32, N_EXP]), ALU.is_le))
                elif part == 2:
                    step(dve.tensor_reduce(over_f[:, 64:96], which, AX_X, ALU.add))
                    settle()
                    step(dve.tensor_copy(over_i[:, 0:32], over_f[:, 64:96]))
                elif part == 3:
                    step(dve.tensor_tensor(which, which, over.unsqueeze(1).broadcast_to([P, 32, N_EXP]), ALU.mult))
                elif part == 4:
                    step(dve.tensor_reduce(over_f[:, 0:32], which, AX_X, ALU.add))
                    settle()
                    step(dve.tensor_tensor(over_f[:, 0:32], iota_s[:, 0:32], over_f[:, 0:32], ALU.subtract))
                    settle()
                    dve.tensor_scalar(over_f[:, 0:32], over_f[:, 0:32], float(SLOTS), float(SLOTS), ALU.mult,
                                      ALU.add).then_inc(over_list, 1)

            def over_one_hot(i, b):
                e = dve.value_load(over_i[0:1, bass.ds(i, 1)], min_val=0, max_val=N_EXP - 1)
                dve.wait_ge(idx_done, N_EXP - 1 + i)
                dve.scalar_tensor_tensor(out=onehot[:, b, :, :], in0=slots4, scalar=over_f[:, bass.ds(i, 1)],
                                         in1=column(e), op0=ALU.add, op1=ALU.is_equal).then_inc(oh_ready, 1)

            def dve_pass(i, last=False, n_over=None):
                for j in range(UNROLL):
                    e = UNROLL * i + j
                    if last and j >= UNROLL - 3:
                        for m in (0, 1):
                            at_j = j - (UNROLL - 3) - m
                            if at_j in (0, 1):
                                with dve.If(m < n_over):
                                    if at_j == 0:
                                        over_one_hot(m, m)
                                    else:
                                        dve.wait_ge(scattered[m], 16 * (RINGS - 1))
                                        indices(N_EXP + m, m)
                    if not last or j + AHEAD < UNROLL:
                        q = j + AHEAD - UNROLL
                        past(dve, scattered[q % DEPTH], 16 * (UNROLL // DEPTH * i + q // DEPTH + 1))
                        indices(e + AHEAD, (j + AHEAD) % UNROLL)
                    if not last or j + 1 < UNROLL:
                        gate_up(e + 1, (j + 1) % 2)
                    if not last or j + 2 < UNROLL:
                        dve.wait_ge(gu_done, e + 1)
                        turn_x(e + 2, j % 2)
                    if not last or j + AHEAD + 1 < UNROLL:
                        one_hot(e + AHEAD + 1, (j + AHEAD + 1) % 2)
                    if isinstance(i, int) and i == 0:
                        overflow_list(j)

            turn_x(0, 0)
            turn_x(1, 1)
            gate_up(0, 0)

            passes = N_EXP // UNROLL - 1
            dve_pass(0)
            with dve.Fori(1, passes) as i:
                dve_pass(i)
            n_over = dve.value_load(over_i[0:1, 32:33], min_val=0, max_val=MAX_OVER)
            dve_pass(passes, True, n_over)
            with dve.If(0 < n_over):
                turn_x(N_EXP, 0)
            with dve.Fori(0, OVER_PASSES) as ii:
                with dve.If(DEPTH * ii < n_over):
                    for u in range(DEPTH):
                        i = DEPTH * ii + u
                        with dve.If(i < n_over):
                            with dve.If(i + 2 < n_over):
                                over_one_hot(i + 2, u % 2)
                                dve.wait_ge(scattered[(u + 2) % DEPTH], 16 * (ii + RINGS + (u + 2) // DEPTH))
                                indices(N_EXP + i + 2, (u + 2) % DEPTH)
                            gate_up(N_EXP + i, u % 2)
                            with dve.If(i + 1 < n_over):
                                dve.wait_ge(gu_done, N_EXP + i)
                                turn_x(N_EXP + i + 1, (u + 1) % 2)
            shared_act(1)

            total = O[:, 0:D]

            def final(t):
                dve.wait_ge(std3_ready, t + 1)
                dve.reciprocal(rs3[:, t:t + 1], rs3[:, t:t + 1]).then_inc(rs3_ready, 1)
                dve.wait_ge(rs3_ready, t + 1)
                dve.scalar_tensor_tensor(out=x_sb[:, t, :], in0=x_sb[:, t, :], scalar=rs3[:, t:t + 1], in1=fng[:, :],
                                         op0=ALU.mult, op1=ALU.mult).then_inc(fin_ready, 1)

            dve.wait_ge(fng_in, 16)
            for t in range(TT):
                by_row = y_back(t).rearrange("p (k d) -> p k d", k=TOP_K)
                whole = DVE_ROWS if t < TT - 1 else DVE_ROWS - 2
                rows_k = y_back(t).rearrange("p (k d) -> p d k", k=TOP_K)[:, :, 0:whole]
                dve.wait_ge(y_in[t] if t < TT - 1 else last_in[1], 16)
                if t:
                    dve.wait_ge(x3_ready, t)
                dve.tensor_reduce(total, rows_k, AX_X, ALU.add).then_inc(summed, 1)
                dve.wait_ge(summed, t + 1)
                if t == TT - 1:
                    dve.wait_ge(last_in[2], 16)
                    for q, k in enumerate(range(whole, DVE_ROWS)):
                        dve.tensor_tensor(total, total, by_row[:, k, :], ALU.add).then_inc(summed, 1)
                        dve.wait_ge(summed, t + 2 + q)
                for half in range(2):
                    n = 2 * t + half
                    dve.wait_ge(sd_done, n + 1)
                    th = total[:, half * S:(half + 1) * S]
                    dve.tensor_tensor(th, th, bank(4 + n % 4), ALU.add).then_inc(sd_free, 1)
                dve.wait_ge(sd_free, 2 * t + 2)
                dve.tensor_tensor(total, total, gate2_b[:, :], ALU.mult).then_inc(sum_step, 1)
                dve.wait_ge(sum_step, t + 1)
                dve.tensor_tensor(x_sb[:, t, :], x_sb[:, t, :], total, ALU.add).then_inc(x3_ready, 1)
                if t:
                    final(t - 1)
            final(TT - 1)

        @block.tensor
        def _(pe):
            def weights(kind, u):
                n = unit_no[kind, u]
                _, _, q, hi = units[n]
                pe.wait_ge(w_lo_ready, products.index(n) + 1)
                return split[hi], split[q]

            def three(out, lhs, rhs, first, last):
                pe.matmul(out, lhs[0], rhs[0], start=first, stop=False)
                pe.matmul(out, lhs[0], rhs[1], start=False, stop=False)
                return pe.matmul(out, lhs[1], rhs[0], start=False, stop=last)

            pe.wait_ge(rows_in, 16 * 7)
            pe.wait_ge(ident_ready, 1)
            pe.transpose(bank(O_BANK)[:, 0:ROWS], rows[0:ROWS, :], ident[0:ROWS, 0:ROWS]).then_inc(rows_T, 1)

            def turn(t, g0):
                for half in range(2):
                    g = g0 + 2 * t + half
                    pe.wait_ge(xn_ready, g0 // 2 + t + 1)
                    if g >= 2:
                        pe.wait_ge(xT_free, g - 1)
                    for k in range(4):
                        mm = pe.transpose(bank(2 + g % 2)[:, k * P:(k + 1) * P],
                                          xg[:, t % 2, (4 * half + k) * P:(4 * half + k + 1) * P], ident[:, :])
                    mm.then_inc(xT_done, 1)

            def ada(u):
                n = tile_no["ada", u]
                freed(pe, n)
                if u in DIRECT:
                    q = units[unit_no["ada", u]][2]
                    pe.wait_ge(landed[q], 16 * fills(unit_no["ada", u], q))
                    for c in range(2):
                        for k in range(KD):
                            mm = pe.matmul(bank(n % 2)[:, c:c + 1], as_k(q, KD)[:, k, c * P:(c + 1) * P],
                                           cact[:, k:k + 1], start=(k == 0), stop=(k == KD - 1))
                    mm.then_inc(tile_done, 1)
                    return
                b = by_vector.index(u)
                pe.wait_ge(acc_ready, b + 1)
                acc = accs[:, b % 2, 0, :]
                if u // 4 in (2, 5):
                    mm = pe.matmul(bank(n % 2)[:, 0:256], ones[:, :], acc, start=True, stop=True)
                else:
                    for c in range(2):
                        mm = pe.matmul(bank(n % 2)[:, c:c + 1], acc[:, c * P:(c + 1) * P], ones[:, 0:1],
                                       start=True, stop=True)
                mm.then_inc(tile_done, 1)

            pe.wait_ge(consts, 1)
            ada(0)
            ada(1)
            turn(0, 0)
            turn(1, 0)
            pe.wait_ge(cact_ready, 1)
            ada(2)
            ada(3)
            ada(4)
            turn(2, 0)
            turn(3, 0)
            for u in range(5, 8):
                ada(u)

            def dense(n, w, c, rhs, ks, between=None):
                freed(pe, n)
                for k in range(ks):
                    if between and k == ks // 2:
                        between()
                    mm = pe.matmul(bank(n % 2), w[:, k, c * P:(c + 1) * P], rhs(k), start=(k == 0), stop=(k == ks - 1))
                mm.then_inc(tile_done, 1)

            def product_tile(n, w, c, x, k0, ks, half=None):
                if half != 1:
                    freed(pe, n)
                w = [part[:, :].rearrange("p (k f) -> p k f", k=ks) for part in w]
                for k in range(ks) if half is None else range(half * ks // 2, (half + 1) * ks // 2):
                    if n == tile_no["qk", 0]:
                        pe.wait_ge(h_lo_ready, k + 1)
                    mm = three(bank(n % 2), [part[:, k, c * P:(c + 1) * P] for part in w],
                               [part[:, k0 + k, :] for part in x], k == 0, k == ks - 1)
                if half == 0:
                    return
                mm.then_inc(tile_done, 1)

            def h_tile(kind, j, unit, c):
                product_tile(tile_no[kind, j], weights(*unit), c, (h_hi, h_lo), 0, KD)

            def scores_of(u):
                kind, h, i = att[u]
                sc = bank(2 + 2 * (u % 2), 2)
                if u >= 2:
                    pe.wait_ge(exp_done, u - 1)
                elif u == 0:
                    pe.wait_ge(roped, 5)
                if kind == "da":
                    for m in range(2):
                        a = slice(64 * m, 64 * m + 64)
                        mm = pe.matmul(sc[:, m * S:m * S + (i + 1) * P], qk[a, h, i * P:(i + 1) * P],
                                       qk[a, 4 + h, 0:(i + 1) * P], start=True, stop=True)
                else:
                    k0, w = max(i - 1, 0) * P, min(i + 1, 2) * P
                    for r in range(4):
                        n = 4 * h + r
                        a = slice(64 * (n % 2), 64 * (n % 2) + 64)
                        keys = qk[a, 12, :] if n % 2 == h else kdup[a]
                        c0 = r % 2 * S + r // 2 * 256
                        mm = pe.matmul(sc[:, c0:c0 + w], qk[a, 8 + n // 2, i * P:(i + 1) * P],
                                       keys[:, k0:k0 + w], start=True, stop=True)
                mm.then_inc(s_done, 1)

            for u in range(9):
                if u in (4, 5, 8):
                    w = [part[:, :].rearrange("p (k f) -> p k f", k=KD) for part in weights("in", u)]
                    if u == 8:
                        h_tile("qk", 12, ("in", 8), 0)
                        for u0 in (0, 1):
                            scores_of(u0)
                    for half in range(2):
                        n = tile_no["v", 2 * (u - 4) + half if u < 8 else 4 + half]
                        freed(pe, n)
                        for m in range(2):
                            t = 2 * half + m
                            for k in range(KD):
                                mm = three(bank(n % 2)[:, m * 256:(m + 1) * 256],
                                           [part[:, k, t * P:(t + 1) * P] for part in (h_hi, h_lo)],
                                           [part[:, k, :] for part in w], k == 0, k == KD - 1)
                        mm.then_inc(tile_done, 1)
                else:
                    j0 = 2 * u if u < 4 else 2 * u - 4
                    h_tile("qk", j0, ("in", u), 0)
                    h_tile("qk", j0 + 1, ("in", u), 1)

            def turn_probs(u, n):
                kind, h, i = att[u]
                half = n - t_steps[u]
                nb = i + 1 if kind == "da" else min(i + 1, 2)
                if n:
                    pe.wait_ge(pT_ready, n)
                blocks = ([(0, b) for b in range(nb)] if kind == "da"
                          else [(256 * (2 * half + r), b) for r in range(2) for b in range(nb)])
                for m, (c0, b) in enumerate(blocks):
                    mm = pe.transpose(bank(T_BANK)[:, m * P:(m + 1) * P],
                                      probs[:, u % 2, c0 + b * P:c0 + (b + 1) * P], ident[:, :])
                mm.then_inc(pT_done, 1)

            def values(u, n):
                kind, h, i = att[u]
                half = n - t_steps[u]
                nb = i + 1 if kind == "da" else min(i + 1, 2)
                pe.wait_ge(pT_ready, n + 1)
                if half == 0 and u:
                    pe.wait_ge(o_ready, u)
                if kind == "da":
                    for b in range(nb):
                        mm = pe.matmul(bank(O_BANK)[:, 0:P], pT[:, n % 2, b * P:(b + 1) * P],
                                       v_sb[:, b, h * P:(h + 1) * P], start=(b == 0), stop=(b == nb - 1))
                else:
                    k0 = max(i - 1, 0)
                    for r in range(2):
                        o0 = (2 * half + r) * HD
                        for b in range(nb):
                            m = r * nb + b
                            mm = pe.matmul(bank(O_BANK)[:, o0:o0 + HD], pT[:, n % 2, m * P:(m + 1) * P],
                                           v_sb[:, k0 + b, 512 + HD * h:512 + HD * h + HD],
                                           start=(b == 0), stop=(b == nb - 1))
                mm.then_inc(pv_done, 1)

            pe.wait_ge(roped, 13)
            pe.wait_ge(kdup_ready, 1)
            v_count = sum(1 for t in tiles[:tile_no["v", 4] + 1] if t[2] == "D")
            pe.wait_ge(free_d, v_count)
            for u in range(NU):
                if att[u][0] == "da":
                    pe.wait_ge(p_ready, u + 1)
                else:
                    pe.wait_ge(exp_done, u + 1)
                if u + 2 < NU:
                    scores_of(u + 2)
                for n in steps_of(u):
                    turn_probs(u, n)
                    for kind, j, half in filler(n):
                        if kind == "ada":
                            ada(j)
                        else:
                            product_tile(tile_no["gate", j], weights("gate", j // 2), j % 2, (h_hi, h_lo), 0, KD,
                                         half)
                    values(u, n)

            pe.wait_ge(o_ready, NU)
            for n in range(8):
                if n == 4:
                    pe.wait_ge(da_scaled, 1)
                if n >= 4:
                    pe.wait_ge(y_lo_ready, n - 3)
                src = O[:, 4 * S:8 * S] if n < 4 else O[:, 0:4 * S]
                for t in range(TT):
                    c = t * S + (n % 4) * P
                    mm = pe.transpose(bank(2 + n % 4)[:, t * P:(t + 1) * P], src[:, c:c + P], ident[:, :])
                mm.then_inc(yT_done, 1)
            pe.wait_ge(y_lo_ready, 8)
            for m in range(8):
                for b, kind in enumerate(("branch_a", "branch_b")):
                    product_tile(tile_no["branch", 2 * m + b], weights(kind, m // 4), m % 4, (y_hi, y_lo), 4 * b, 4)

            def turn2(t):
                pe.wait_ge(xn_ready, TT + t + 1)
                for half, left in enumerate((h2_dve, h2_act)):
                    if t:
                        pe.wait_ge(left, t)
                    for k in range(4):
                        mm = pe.transpose(bank(2 + half)[:, k * P:(k + 1) * P],
                                          xg[:, t % 2, (4 * half + k) * P:(4 * half + k + 1) * P], ident[:, :])
                    mm.then_inc(xT_done, 1)

            def router(t):
                pe.wait_ge(h2_dve, t + 1)
                pe.wait_ge(h2_act, t + 1)
                if t == 0:
                    pe.wait_ge(late_in, 16 * 6)
                for k in range(KD):
                    mm = pe.matmul(bank(4)[0:N_EXP, t * P:(t + 1) * P], wr[:, k, :], hT[:, k, t * P:(t + 1) * P],
                                   start=(k == 0), stop=(k == KD - 1))
                mm.then_inc(logits_done, 1)

            w_out = {}
            for t in range(TT):
                for half in range(2):
                    n = tile_no["out", 2 * t + half]
                    freed(pe, n)
                    for k in range(KD):
                        if t == 0 and half == 0:
                            if k % 2 == 0:
                                w_out[k // 2] = [part[:, :].rearrange("p (k f) -> p k f", k=2)
                                                 for part in weights("out", k // 2)]
                            pe.wait_ge(m_lo_ready, k + 1)
                        mm = three(bank(n % 2), [part[:, k, t * P:(t + 1) * P] for part in (m_hi, m_lo)],
                                   [part[:, k % 2, half * S:(half + 1) * S] for part in w_out[k // 2]], k == 0, k == KD - 1)
                    mm.then_inc(tile_done, 1)
                    if t and half == 0:
                        turn2(t - 1)
                if t:
                    router(t - 1)
            turn2(TT - 1)
            router(TT - 1)
            pe.wait_ge(logits_ready, TT)
            for t in range(TT):
                mm = pe.transpose(bank(5)[:, t * N_EXP:(t + 1) * N_EXP], logits_T[0:N_EXP, t * P:(t + 1) * P],
                                  ident[0:N_EXP, 0:N_EXP])
            mm.then_inc(logits_turned, 1)

            def shared_tiles(k, q, between=None):
                for c, kind in enumerate(("sh_gate", "sh_up")):
                    dense(tile_no[kind, k], as_k(q + c, KD), k, lambda k: hT[:, k, :], KD, between if c else None)

            def ranks():
                def add(lhs, to, src, width, first, last):
                    return pe.matmul(bank(RANK_BANK)[:, to * N_EXP:(to + width) * N_EXP], lhs[:, :],
                                     chosen[:, src * N_EXP:(src + width) * N_EXP], start=first, stop=last)

                pe.wait_ge(chosen_ready, 1)
                add(upper, 0, 0, TT, True, False)
                for d in range(1, TT):
                    add(ones, d, 0, TT - d, False, d == TT - 1)
                for t in range(TT):
                    mm = add(ones, TT, t, 1, t == 0, t == TT - 1)
                mm.then_inc(rank_done, 1)

            for q in (9, 10):
                pe.wait_ge(landed[q], 16 * (fills(len(units), q) + 1))
            shared_tiles(0, 9, ranks)

            def tokens(e, b, payload=None):
                pe.wait_ge(oh_ready, e + 1)
                past(pe, idx_ready, e)
                z = Z[:, :, bass.ds(e if payload is None else payload, 1), :]
                for t in range(TT):
                    mm = pe.matmul(bank(IDX_BANK)[:, 0:PARTS], onehot[:, b, t, :],
                                   z[:, t, :, :].rearrange("p a c -> p (a c)"), start=(t == 0), stop=(t == TT - 1))
                mm.then_inc(idx_done, 1)

            for e in range(AHEAD):
                tokens(e, e % 2)

            def turn_tokens(e, x):
                past(pe, xgT_dve, e)
                past(pe, xgT_act, e)
                for k in range(KD):
                    mm = pe.transpose(bank(4, 2)[:, k * P:(k + 1) * P], x[:, k * P:(k + 1) * P], ident[:, :])
                mm.then_inc(xgT_done, 1)

            def gate_up(e, b, q):
                pe.wait_ge(xgT_dve, e + 1)
                pe.wait_ge(xgT_act, e + 1)
                for c in range(2):
                    w = as_k(q + c, KD)
                    for m in range(KF):
                        o = (KF * c + m) * SLOTS
                        for k in range(KD):
                            mm = pe.matmul(bank(2 + b)[:, o:o + SLOTS], w[:, k, m * P:(m + 1) * P], xgT[:, b, k, :],
                                           start=(k == 0), stop=(k == KD - 1))
                mm.then_inc(gu_done, 1)

            def down(e, b, q):
                pe.wait_ge(hact_ready, e + 1)
                past(pe, y_ready, e)
                w = as_k(q, KF)
                for half in range(2):
                    for k in range(KF):
                        mm = pe.matmul(bank(half), hact[:, b, k, :], w[:, k, half * S:(half + 1) * S],
                                       start=(k == 0), stop=(k == KF - 1))
                mm.then_inc(dn_done, 1)

            dense_uses = [fills(len(units), s) + int(s in (9, 10)) for s in range(12)]

            def round_of(i, j):
                return UNROLL // DEPTH * i + j // DEPTH + 1

            def arrived(i, j, part):
                q = 3 * (j % DEPTH) + part
                pe.wait_ge(landed[q], 16 * (round_of(i, j) + dense_uses[q]))

            def turn_expert(e, i, j):
                pe.wait_ge(gathered[j % DEPTH], 16 * round_of(i, j))
                turn_tokens(e, x_exp[:, j % DEPTH, :])

            def gate_up_expert(e, i, j):
                arrived(i, j, 0)
                arrived(i, j, 1)
                gate_up(e, j % 2, 3 * (j % DEPTH))

            def over_tokens(i, b):
                e = pe.value_load(over_i[0:1, bass.ds(i, 1)], min_val=0, max_val=N_EXP - 1)
                tokens(N_EXP + i, b, e)

            def pe_pass(i, last=False, n_over=None):
                for j in range(UNROLL):
                    e = UNROLL * i + j
                    if last and j >= UNROLL - 2:
                        m = j - UNROLL + 2
                        with pe.If(m < n_over):
                            over_tokens(m, m)
                    if not last or j + AHEAD < UNROLL:
                        tokens(e + AHEAD, (j + AHEAD) % 2)
                    if not last or j + 1 < UNROLL:
                        past(pe, hact_ready, e)
                        gate_up_expert(e + 1, i, j + 1)
                    if not last or j + 2 < UNROLL:
                        turn_expert(e + 2, i, j + 2)
                    arrived(i, j, 2)
                    down(e, j % 2, 3 * (j % DEPTH) + 2)

            turn_expert(0, 0, 0)
            gate_up_expert(0, 0, 0)
            turn_expert(1, 0, 1)
            pe.wait_ge(hs_ready, 1)
            pe_pass(0)
            with pe.Fori(1, N_EXP // UNROLL - 1) as i:
                pe_pass(i)
            n_over = pe.value_load(over_i[0:1, 32:33], min_val=0, max_val=MAX_OVER)
            pe_pass(N_EXP // UNROLL - 1, True, n_over)

            def over_turn(i, u, round4):
                pe.wait_ge(gathered[u], 16 * round4)
                turn_tokens(N_EXP + i, x_exp[:, u, :])

            with pe.If(0 < n_over):
                over_turn(0, 0, RINGS + 1)
            with pe.Fori(0, OVER_PASSES) as ii:
                with pe.If(DEPTH * ii < n_over):
                    for u in range(DEPTH):
                        i = DEPTH * ii + u
                        q, round2 = 3 * (u % 2), 2 * ii + u // 2 + 1
                        with pe.If(i < n_over):
                            with pe.If(i + 2 < n_over):
                                over_tokens(i + 2, u % 2)
                            pe.wait_ge(ov_landed[q], 16 * round2)
                            pe.wait_ge(ov_landed[q + 1], 16 * round2)
                            pe.wait_ge(hact_ready, N_EXP - 1 + i)
                            gate_up(N_EXP + i, u % 2, 3 + q)
                            with pe.If(i + 1 < n_over):
                                over_turn(i + 1, (u + 1) % DEPTH, ii + RINGS + 1 + (u + 1) // DEPTH)
                            pe.wait_ge(ov_landed[q + 2], 16 * round2)
                            down(N_EXP + i, u % 2, 3 + q + 2)

            pe.wait_ge(y_ready, n_over + N_EXP)
            for q in (0, 1):
                pe.wait_ge(landed[q], 16 * (dense_uses[q] + RINGS + 1))
            shared_tiles(1, 0)
            pe.wait_ge(hs_ready, KF)
            pe.wait_ge(landed[2], 16 * (dense_uses[2] + RINGS + 1))
            pe.wait_ge(xgT_dve, n_over + N_EXP)
            pe.wait_ge(xgT_act, n_over + N_EXP)
            w = as_k(2, KF)

            def shared_down(t):
                for half in range(2):
                    n = 2 * t + half
                    if n >= 4:
                        pe.wait_ge(sd_free, n - 3)
                    for k in range(KF):
                        pe.matmul(bank(4 + n % 4), hsT[k][:, t * P:(t + 1) * P], w[:, k, half * S:(half + 1) * S],
                                  start=(k == 0), stop=False)

            for t in range(TT):
                shared_down(t)
                pe.wait_ge(y_in[t] if t < TT - 1 else last_in[0], 16)
                rows_k = y_back(t).rearrange("p (k d) -> p k d", k=TOP_K)
                for half in range(2):
                    for k in range(TOP_K - PE_ROWS, TOP_K):
                        mm = pe.matmul(bank(4 + (2 * t + half) % 4), ident[:, :], rows_k[:, k, half * S:(half + 1) * S],
                                       start=False, stop=(k == TOP_K - 1))
                    mm.then_inc(sd_done, 1)


_INS = ["x", "c", "positions", "norm1_g", "norm2_g", "w_ada", "b_ada", "w_in", "b_in", "da_lambda", "da_norm_g",
        "sw_sinks", "w_branch_a", "w_branch_b", "w_gate", "b_gate", "w_out", "w_router", "router_bias",
        "w_exp_gate", "w_exp_up", "w_exp_down", "w_sh_gate", "w_sh_up", "w_sh_down", "final_norm_g"]
_WHOLE = ("c", "positions", "final_norm_g")


def kernel(**inputs):
    import numpy as _np
    import concourse.bacc as _bacc
    from concourse import mybir as _mybir
    from concourse.bass_utils import run_bass_kernel_spmd as _run

    nc = _bacc.Bacc("TRN2", target_bir_lowering=False, num_devices=1)
    arrays, args = {}, []

    def give(name, a):
        arrays[f"in_{name}_dram"] = a
        args.append(nc.dram_tensor(f"in_{name}_dram", a.shape, _mybir.dt.from_np(a.dtype), kind="ExternalInput").ap())

    for name in _INS:
        a = _np.ascontiguousarray(inputs[name])
        give(name, a if name in _WHOLE else a[0])
    freq = 1.0 / (10000.0 ** (_np.arange(0, HD, 2) / HD))
    give("inv_freq", _np.tile(freq, 4).astype(_np.float32).reshape(P, 1))
    args.append(nc.dram_tensor("out_0_dram", (S, D), _mybir.dt.float32, kind="ExternalOutput").ap())
    build(nc, *args)
    r = _run(nc, [arrays], core_ids=[0])
    return r.results[0]["out_0_dram"].reshape(1, S, D)
```
